# Optimizing a Trainium2 kernel written in Bass

```python
import math
import jax, jax.numpy as jnp
from jax import lax
import numpy as np

D_MODEL = 1024
BATCH = 1
SEQ = 1024
DEPTH = 1

HG_HEADS = 4
HG_DK = 128
HG_DV = 128
HG_WIDTH = HG_HEADS * HG_DK
HG_CHUNK = 64
DA_HEADS = 4
DA_HEAD = 64
DA_VDIM = 2 * DA_HEAD
DA_QK_WIDTH = DA_HEADS * 2 * DA_HEAD
DA_WIDTH = DA_HEADS * DA_VDIM
Q_BLOCK = 128
ROPE_THETA = 10000.0
N_GROUPS = 4
EXPERTS_PER_GROUP = 8
N_EXPERTS = N_GROUPS * EXPERTS_PER_GROUP
TOP_K = 2
D_FF_EXPERT = 512
MOE_BLOCK = 128
EPS = 1e-6
IN_COLS = 4 * HG_WIDTH + 2 * DA_QK_WIDTH + DA_WIDTH + 2 * D_MODEL


def rms_norm(x, gain):
    xf = x.astype(jnp.float32)
    y = xf * lax.rsqrt(jnp.mean(xf * xf, axis=-1, keepdims=True) + EPS)
    return (y * gain.astype(jnp.float32)).astype(x.dtype)

def rope(x, pos):
    half = x.shape[-1] // 2
    inv = ROPE_THETA ** (-jnp.arange(half, dtype=jnp.float32) / half)
    ang = pos.astype(jnp.float32)[:, None] * inv[None, :]
    cos = jnp.cos(ang)[None, :, None, :]
    sin = jnp.sin(ang)[None, :, None, :]
    x1, x2 = x[..., :half].astype(jnp.float32), x[..., half:].astype(jnp.float32)
    return jnp.concatenate([x1 * cos - x2 * sin, x1 * sin + x2 * cos], axis=-1).astype(x.dtype)

def hgrn2_chunked(q, k, v, log_f):
    B, S, H, DK = q.shape
    DV = v.shape[-1]
    C = HG_CHUNK
    NC = S // C

    def to_chunks(t):
        return t.astype(jnp.float32).reshape(B, NC, C, H, t.shape[-1]).transpose(1, 0, 3, 2, 4)

    qc, kc, vc, gc = to_chunks(q), to_chunks(k), to_chunks(v), to_chunks(log_f)
    causal = jnp.tril(jnp.ones((C, C), dtype=bool))

    def step(state, inp):
        qi, ki, vi, gi = inp
        b = jnp.cumsum(gi, axis=-2)
        b_ref = b[..., C // 2 - 1:C // 2, :]
        q_rel = qi * jnp.exp(b - b_ref)
        k_rel = ki * jnp.exp(b_ref - b)
        scores = jnp.einsum('bhtk,bhsk->bhts', q_rel, k_rel)
        scores = jnp.where(causal, scores, 0.0)
        o = (jnp.einsum('bhts,bhsv->bhtv', scores, vi)
             + jnp.einsum('bhtk,bhkv->bhtv', qi * jnp.exp(b), state))
        b_end = b[..., -1:, :]
        k_end = ki * jnp.exp(b_end - b)
        new_state = (jnp.exp(b_end[..., 0, :])[..., None] * state
                     + jnp.einsum('bhsk,bhsv->bhkv', k_end, vi))
        return new_state, o

    state0 = jnp.zeros((B, H, DK, DV), jnp.float32)
    _, o = lax.scan(step, state0, (qc, kc, vc, gc))
    return o.transpose(1, 0, 3, 2, 4).reshape(B, S, H, DV)

def diff_attention(q1, q2, k1, k2, v, lam):
    B, S, H, D = q1.shape
    NQ = S // Q_BLOCK
    scale = D ** -0.5
    key_pos = jnp.arange(S)

    def block(i):
        start = i * Q_BLOCK
        qb1 = lax.dynamic_slice_in_dim(q1, start, Q_BLOCK, axis=1)
        qb2 = lax.dynamic_slice_in_dim(q2, start, Q_BLOCK, axis=1)
        qpos = start + jnp.arange(Q_BLOCK)
        mask = key_pos[None, :] <= qpos[:, None]

        def probs(qb, kk):
            s = jnp.einsum('bqhd,bshd->bhqs', qb, kk).astype(jnp.float32) * scale
            return jax.nn.softmax(jnp.where(mask, s, -jnp.inf), axis=-1)

        a = probs(qb1, k1) - lam * probs(qb2, k2)
        return jnp.einsum('bhqs,bshv->bqhv', a.astype(v.dtype), v)

    o = lax.map(block, jnp.arange(NQ))
    return o.transpose(1, 0, 2, 3, 4).reshape(B, S, H, v.shape[-1])

def hier_moe(xn, w_rg, b_rg, w_re, b_re, w1, w3, w2):
    B, S, D = xn.shape
    T = B * S
    xt = xn.reshape(T, D)
    g_logits = (xt @ w_rg).astype(jnp.float32) + b_rg.astype(jnp.float32)
    g_sel = jnp.argmax(g_logits, axis=-1)
    g_w = jnp.max(jax.nn.softmax(g_logits, axis=-1), axis=-1, keepdims=True)
    e_logits = ((xt @ w_re).astype(jnp.float32) + b_re.astype(jnp.float32)).reshape(
        T, N_GROUPS, EXPERTS_PER_GROUP)
    e_in_group = jnp.sum(e_logits * jax.nn.one_hot(g_sel, N_GROUPS, dtype=jnp.float32)[:, :, None], axis=1)
    top_v, top_i = lax.top_k(e_in_group, TOP_K)
    e_w = jax.nn.softmax(top_v, axis=-1) * g_w

    A = T * TOP_K
    expert_id = (g_sel[:, None] * EXPERTS_PER_GROUP + top_i).reshape(A).astype(jnp.int32)
    token_id = jnp.repeat(jnp.arange(T, dtype=jnp.int32), TOP_K)
    weight = e_w.reshape(A)

    order = jnp.argsort(expert_id)
    se = expert_id[order]
    counts = jnp.zeros((N_EXPERTS,), jnp.int32).at[expert_id].add(1)
    padded = (counts + MOE_BLOCK - 1) // MOE_BLOCK * MOE_BLOCK
    pad_end = jnp.cumsum(padded)
    pad_start = pad_end - padded
    start = jnp.cumsum(counts) - counts
    dest = pad_start[se] + jnp.arange(A, dtype=jnp.int32) - start[se]
    P = A + N_EXPERTS * MOE_BLOCK
    NB = P // MOE_BLOCK
    buf_tok = jnp.full((P,), T, jnp.int32).at[dest].set(token_id[order])
    buf_w = jnp.zeros((P,), jnp.float32).at[dest].set(weight[order])
    block_start = jnp.arange(NB, dtype=jnp.int32) * MOE_BLOCK
    block_expert = jnp.minimum(
        jnp.sum(pad_end[None, :] <= block_start[:, None], axis=1), N_EXPERTS - 1).astype(jnp.int32)
    x_pad = jnp.concatenate([xt, jnp.zeros((1, D), xt.dtype)], axis=0)

    def run_block(args):
        tok, w, e = args
        xb = x_pad[tok]
        hid = jax.nn.silu(xb @ w1[e]) * (xb @ w3[e])
        return (hid @ w2[e]) * w[:, None].astype(xb.dtype)

    y = lax.map(run_block, (buf_tok.reshape(NB, MOE_BLOCK), buf_w.reshape(NB, MOE_BLOCK), block_expert))
    out = jnp.zeros((T + 1, D), xt.dtype).at[buf_tok].add(y.reshape(P, D))
    return out[:T].reshape(B, S, D)

def first_inputs(seed: int = 0) -> dict:
    key = jax.random.key(seed)
    ks = jax.random.split(key, 20)

    def nrm(k, shape, scale):
        return jax.random.normal(k, shape, jnp.float32) * scale

    def gain(k, shape):
        return 1.0 + nrm(k, shape, 0.02)

    return {
        "x": nrm(ks[0], (BATCH, SEQ, D_MODEL), 1.0),
        "norm_mix": gain(ks[1], (DEPTH, D_MODEL)),
        "w_in": nrm(ks[2], (DEPTH, D_MODEL, IN_COLS), D_MODEL ** -0.5),
        "hg_lb": nrm(ks[3], (DEPTH + 1, HG_WIDTH), 0.1),
        "hg_out_norm": gain(ks[4], (DEPTH, HG_DV)),
        "da_q_norm": gain(ks[5], (DEPTH, DA_HEAD)),
        "da_k_norm": gain(ks[6], (DEPTH, DA_HEAD)),
        "da_lambda": nrm(ks[7], (DEPTH, 4, DA_HEAD), 0.1),
        "da_out_norm": gain(ks[8], (DEPTH, DA_VDIM)),
        "w_branch_hg": nrm(ks[9], (DEPTH, HG_WIDTH, D_MODEL), HG_WIDTH ** -0.5),
        "w_branch_da": nrm(ks[10], (DEPTH, DA_WIDTH, D_MODEL), DA_WIDTH ** -0.5),
        "w_out": nrm(ks[11], (DEPTH, D_MODEL, D_MODEL), D_MODEL ** -0.5),
        "norm_moe": gain(ks[12], (DEPTH, D_MODEL)),
        "w_router_group": nrm(ks[13], (DEPTH, D_MODEL, N_GROUPS), D_MODEL ** -0.5),
        "b_router_group": nrm(ks[14], (DEPTH, N_GROUPS), 0.01),
        "w_router_expert": nrm(ks[15], (DEPTH, D_MODEL, N_EXPERTS), D_MODEL ** -0.5),
        "b_router_expert": nrm(ks[16], (DEPTH, N_EXPERTS), 0.01),
        "w1": nrm(ks[17], (DEPTH, N_EXPERTS, D_MODEL, D_FF_EXPERT), D_MODEL ** -0.5),
        "w3": nrm(ks[18], (DEPTH, N_EXPERTS, D_MODEL, D_FF_EXPERT), D_MODEL ** -0.5),
        "w2": nrm(ks[19], (DEPTH, N_EXPERTS, D_FF_EXPERT, D_MODEL), D_FF_EXPERT ** -0.5),
    }

def first_block(x, norm_mix, w_in, hg_lb, hg_out_norm, da_q_norm, da_k_norm, da_lambda,
              da_out_norm, w_branch_hg, w_branch_da, w_out, norm_moe, w_router_group,
              b_router_group, w_router_expert, b_router_expert, w1, w3, w2):
    B, S, _ = x.shape
    pos = jnp.arange(S)
    widths = [HG_WIDTH] * 4 + [DA_QK_WIDTH, DA_QK_WIDTH, DA_WIDTH, D_MODEL, D_MODEL]
    splits = [int(v) for v in np.cumsum(widths)[:-1]]
    lb_all = jnp.cumsum(jax.nn.softmax(hg_lb.astype(jnp.float32), axis=0), axis=0)

    for l in range(DEPTH):
        h = rms_norm(x, norm_mix[l])
        proj = h @ w_in[l]
        hq, hf, hi, hog, dq, dk, dv, gate_hg, gate_da = jnp.split(proj, splits, axis=-1)

        lb = lb_all[l]
        f = lb + (1.0 - lb) * jax.nn.sigmoid(hf.astype(jnp.float32))
        heads_hg = lambda t: t.reshape(B, S, HG_HEADS, t.shape[-1] // HG_HEADS)
        o_hg = hgrn2_chunked(heads_hg(hq), heads_hg(1.0 - f), heads_hg(hi), heads_hg(jnp.log(f)))
        o_hg = rms_norm(o_hg, hg_out_norm[l]) * jax.nn.silu(heads_hg(hog).astype(jnp.float32))
        y_hg = o_hg.reshape(B, S, HG_WIDTH).astype(x.dtype) @ w_branch_hg[l]

        qn = rope(rms_norm(dq.reshape(B, S, 2 * DA_HEADS, DA_HEAD), da_q_norm[l]), pos)
        kn = rope(rms_norm(dk.reshape(B, S, 2 * DA_HEADS, DA_HEAD), da_k_norm[l]), pos)
        qn = qn.reshape(B, S, DA_HEADS, 2, DA_HEAD)
        kn = kn.reshape(B, S, DA_HEADS, 2, DA_HEAD)
        v = dv.reshape(B, S, DA_HEADS, DA_VDIM)
        lam_p = da_lambda[l].astype(jnp.float32)
        lam_init = 0.8 - 0.6 * math.exp(-0.3 * l)
        lam = jnp.exp(jnp.sum(lam_p[0] * lam_p[1])) - jnp.exp(jnp.sum(lam_p[2] * lam_p[3])) + lam_init
        o_da = diff_attention(qn[..., 0, :], qn[..., 1, :], kn[..., 0, :], kn[..., 1, :], v, lam)
        o_da = rms_norm(o_da, da_out_norm[l]) * (1.0 - lam_init)
        y_da = o_da.reshape(B, S, DA_WIDTH).astype(x.dtype) @ w_branch_da[l]

        mixed = jax.nn.sigmoid(gate_hg) * y_hg + jax.nn.sigmoid(gate_da) * y_da
        x = x + (mixed @ w_out[l]).astype(x.dtype)

        x = x + hier_moe(rms_norm(x, norm_moe[l]), w_router_group[l], b_router_group[l],
                         w_router_expert[l], b_router_expert[l], w1[l], w3[l], w2[l]).astype(x.dtype)
    return x


HEAD_DIM = 64
MIX_WIDTH = D_MODEL
A_HEADS = (MIX_WIDTH // 2) // HEAD_DIM
A_KV_HEADS = 2
A_GROUP = A_HEADS // A_KV_HEADS
B_HEADS = (MIX_WIDTH // 2) // HEAD_DIM
WINDOW = 128
BLOCK = 128
D_FF = 4 * D_MODEL

A_Q_W = A_HEADS * HEAD_DIM
A_KV_W = A_KV_HEADS * HEAD_DIM
B_W = B_HEADS * HEAD_DIM
IN_SPLITS = tuple(np.cumsum([A_Q_W, A_KV_W, A_KV_W, B_W, B_W, B_W]).tolist())
IN_WIDTH = A_Q_W + 2 * A_KV_W + 3 * B_W + B_HEADS


def rmsnorm(x, g):
    x32 = x.astype(jnp.float32)
    y = x32 * lax.rsqrt(jnp.mean(x32 * x32, axis=-1, keepdims=True) + EPS)
    return (y * g.astype(jnp.float32)).astype(x.dtype)

def alibi_slopes(n):
    return jnp.exp2(-(8.0 / n) * (jnp.arange(n, dtype=jnp.float32) + 1.0))

def swa_sinks_attention(q, k, v, sinks):
    b, s, _, d = q.shape
    nb = s // BLOCK
    scale = 1.0 / math.sqrt(d)
    qb = q.reshape(b, nb, BLOCK, A_KV_HEADS, A_GROUP, d)
    pad = ((0, 0), (BLOCK, 0), (0, 0), (0, 0))
    kp = jnp.pad(k, pad).reshape(b, nb + 1, BLOCK, A_KV_HEADS, d)
    vp = jnp.pad(v, pad).reshape(b, nb + 1, BLOCK, A_KV_HEADS, d)
    kb = jnp.concatenate([kp[:, :-1], kp[:, 1:]], axis=2)
    vb = jnp.concatenate([vp[:, :-1], vp[:, 1:]], axis=2)
    scores = jnp.einsum('bnqkgd,bnskd->bnkgqs', qb, kb).astype(jnp.float32) * scale
    qpos = BLOCK + jnp.arange(BLOCK)
    kpos = jnp.arange(2 * BLOCK)
    dist = qpos[:, None] - kpos[None, :]
    band = (dist >= 0) & (dist < WINDOW)
    first_pad = (jnp.arange(nb) == 0)[:, None, None] & (kpos < BLOCK)[None, None, :]
    valid = band[None] & ~first_pad
    slopes = alibi_slopes(A_HEADS).reshape(A_KV_HEADS, A_GROUP)
    alibi = -slopes[:, :, None, None] * dist.astype(jnp.float32)[None, None]
    scores = scores + alibi[None, None]
    scores = jnp.where(valid[None, :, None, None], scores, -jnp.inf)
    sink = sinks.astype(jnp.float32).reshape(1, 1, A_KV_HEADS, A_GROUP, 1, 1)
    m = jnp.maximum(jnp.max(scores, axis=-1, keepdims=True), sink)
    p = jnp.exp(scores - m)
    denom = jnp.sum(p, axis=-1, keepdims=True) + jnp.exp(sink - m)
    p = (p / denom).astype(v.dtype)
    out = jnp.einsum('bnkgqs,bnskd->bnqkgd', p, vb)
    return out.reshape(b, s, A_HEADS, d)

def forgetting_attention(q, k, v, log_f):
    b, s, h, d = q.shape
    nb = s // BLOCK
    scale = 1.0 / math.sqrt(d)
    c = jnp.cumsum(log_f, axis=1)
    c_keys = jnp.transpose(c, (0, 2, 1))
    qb = jnp.moveaxis(q.reshape(b, nb, BLOCK, h, d), 1, 0)
    cb = jnp.moveaxis(c.reshape(b, nb, BLOCK, h), 1, 0)
    kpos = jnp.arange(s)

    def block_step(args):
        qi, ci, i = args
        sc = jnp.einsum('bqhd,bshd->bhqs', qi, k).astype(jnp.float32) * scale
        bias = jnp.transpose(ci, (0, 2, 1))[..., None] - c_keys[:, :, None, :]
        qpos = i * BLOCK + jnp.arange(BLOCK)
        causal = kpos[None, :] <= qpos[:, None]
        sc = jnp.where(causal[None, None], sc + bias, -jnp.inf)
        p = jax.nn.softmax(sc, axis=-1).astype(v.dtype)
        return jnp.einsum('bhqs,bshd->bqhd', p, v)

    out = lax.map(block_step, (qb, cb, jnp.arange(nb)))
    return jnp.moveaxis(out, 0, 1).reshape(b, s, h, d)

def second_inputs(seed: int = 0) -> dict:
    key = jax.random.key(seed)
    ks = jax.random.split(key, 14)
    f32 = jnp.float32
    x = jax.random.normal(ks[0], (BATCH, SEQ, D_MODEL), f32)
    attn_norm_g = 1.0 + 0.02 * jax.random.normal(ks[1], (D_MODEL,), f32)
    w_in = jax.random.normal(ks[2], (D_MODEL, IN_WIDTH), f32) * D_MODEL ** -0.5
    b_forget = 2.0 + 0.5 * jax.random.normal(ks[3], (B_HEADS,), f32)
    q_norm_a = 1.0 + 0.02 * jax.random.normal(ks[4], (HEAD_DIM,), f32)
    k_norm_a = 1.0 + 0.02 * jax.random.normal(ks[5], (HEAD_DIM,), f32)
    sink_logits = 0.5 * jax.random.normal(ks[6], (A_HEADS,), f32)
    q_norm_b = 1.0 + 0.02 * jax.random.normal(ks[7], (HEAD_DIM,), f32)
    k_norm_b = 1.0 + 0.02 * jax.random.normal(ks[8], (HEAD_DIM,), f32)
    w_out = jax.random.normal(ks[9], (MIX_WIDTH, D_MODEL), f32) * MIX_WIDTH ** -0.5
    mlp_norm_g = 1.0 + 0.02 * jax.random.normal(ks[10], (D_MODEL,), f32)
    w_up = jax.random.normal(ks[11], (D_MODEL, D_FF), f32) * D_MODEL ** -0.5
    w_down = jax.random.normal(ks[12], (D_FF, D_MODEL), f32) * D_FF ** -0.5
    return {"x": x, "attn_norm_g": attn_norm_g, "w_in": w_in, "b_forget": b_forget,
            "q_norm_a": q_norm_a, "k_norm_a": k_norm_a, "sink_logits": sink_logits,
            "q_norm_b": q_norm_b, "k_norm_b": k_norm_b, "w_out": w_out,
            "mlp_norm_g": mlp_norm_g, "w_up": w_up, "w_down": w_down}

def second_block(x, attn_norm_g, w_in, b_forget, q_norm_a, k_norm_a, sink_logits,
              q_norm_b, k_norm_b, w_out, mlp_norm_g, w_up, w_down):
    b, s, _ = x.shape
    for _layer in range(DEPTH):
        xn = rmsnorm(x, attn_norm_g)
        proj = jnp.einsum('bsd,de->bse', xn, w_in)
        qa, ka, va, qb, kb, vb, f_logit = jnp.split(proj, IN_SPLITS, axis=-1)
        qa = rmsnorm(qa.reshape(b, s, A_HEADS, HEAD_DIM), q_norm_a)
        ka = rmsnorm(ka.reshape(b, s, A_KV_HEADS, HEAD_DIM), k_norm_a)
        va = va.reshape(b, s, A_KV_HEADS, HEAD_DIM)
        out_a = swa_sinks_attention(qa, ka, va, sink_logits)
        qb = rmsnorm(qb.reshape(b, s, B_HEADS, HEAD_DIM), q_norm_b)
        kb = rmsnorm(kb.reshape(b, s, B_HEADS, HEAD_DIM), k_norm_b)
        vb = vb.reshape(b, s, B_HEADS, HEAD_DIM)
        log_f = jax.nn.log_sigmoid(f_logit.astype(jnp.float32) + b_forget.astype(jnp.float32))
        out_b = forgetting_attention(qb, kb, vb, log_f)
        mixed = jnp.concatenate([out_a.reshape(b, s, A_Q_W), out_b.reshape(b, s, B_W)], axis=-1)
        x = x + jnp.einsum('bse,ed->bsd', mixed, w_out)
        hn = rmsnorm(x, mlp_norm_g)
        hid = jnp.square(jax.nn.relu(jnp.einsum('bsd,df->bsf', hn, w_up)))
        x = x + jnp.einsum('bsf,fd->bsd', hid, w_down)
    return x


def setup_inputs(seed=0):
    out = dict(first_inputs(seed))
    for name, value in second_inputs(seed + 1).items():
        if name != "x":
            out[name + "_2"] = value
    return out


def reference(
    x, norm_mix, w_in, hg_lb, hg_out_norm, da_q_norm, da_k_norm, da_lambda, da_out_norm,
    w_branch_hg, w_branch_da, w_out, norm_moe, w_router_group, b_router_group, w_router_expert,
    b_router_expert, w1, w3, w2, attn_norm_g_2, w_in_2, b_forget_2, q_norm_a_2, k_norm_a_2,
    sink_logits_2, q_norm_b_2, k_norm_b_2, w_out_2, mlp_norm_g_2, w_up_2, w_down_2,
):
    x = first_block(
        x, norm_mix, w_in, hg_lb, hg_out_norm, da_q_norm, da_k_norm, da_lambda, da_out_norm,
        w_branch_hg, w_branch_da, w_out, norm_moe, w_router_group, b_router_group,
        w_router_expert, b_router_expert, w1, w3, w2,
    )
    return second_block(
        x, attn_norm_g_2, w_in_2, b_forget_2, q_norm_a_2, k_norm_a_2, sink_logits_2, q_norm_b_2,
        k_norm_b_2, w_out_2, mlp_norm_g_2, w_up_2, w_down_2,
    )


_drawn_inputs = setup_inputs


def setup_inputs(seed=0):
    import zlib

    import numpy as np

    out = dict(_drawn_inputs(seed))
    spreads = {}
    factors = {'hg_out_norm': 3.116,
     'b_router_group': 3.491,
     'attn_norm_g_2': 5.658,
     'q_norm_a_2': 8.0,
     'k_norm_a_2': 8.0,
     'sink_logits_2': 193.978,
     'q_norm_b_2': 8.0,
     'k_norm_b_2': 8.0,
     'mlp_norm_g_2': 3.506}
    for name, (base, spread) in spreads.items():
        noise = np.random.default_rng([zlib.crc32(name.encode()), seed]).standard_normal(out[name].shape)
        drawn = base * np.exp(spread * noise) if base else spread * noise
        out[name] = __import__('jax').numpy.asarray(drawn.astype(out[name].dtype))
    for name, factor in factors.items():
        out[name] = (out[name] * factor).astype(out[name].dtype)
    return out
```

```python
from contextlib import ExitStack
import math

import numpy as np
import concourse.bass as bass
import concourse.mybir as mybir
from concourse.alu_op_type import AluOpType as ALU

ACT = mybir.ActivationFunctionType
AX = mybir.AxisListType
F32, F32R, BF16, I32 = mybir.dt.float32, mybir.dt.float32r, mybir.dt.bfloat16, mybir.dt.int32

P = 128
S, D = 1024, 1024
NT, ND = S // P, D // P
N = 512
EPS = 1e-6
KB = 1024

HG_H, HG_D, CHUNK = 4, 128, 64
NCH = S // CHUNK
DA_H, DA_D = 4, 64
LAM_INIT = 0.8 - 0.6 * math.exp(-0.3 * 0)
NG, NE8, NE = 4, 8, 32
FF = 512
TOPK = 2
NBLK = (S * TOPK + NE * (P - 1)) // P
NBLK += NBLK % 2
NSLOT_BLK = NBLK + 1
HD, AH, AKV, BH = 64, 8, 2, 8
BAUG = HD + 2 + NT
DFF = 4 * D
NEG = -1e30

RING = 4


def chain(eng, sem):
    n = [0]

    def done(ins):
        n[0] += 1
        ins.then_inc(sem, 1)
        return n[0]

    def then(ins):
        eng.wait_ge(sem, done(ins))

    return done, then


def inverse_root(dve, then, r, ms, root, tmp):
    then(dve.reciprocal(r, root))
    then(dve.tensor_tensor(tmp, r, r, ALU.mult))
    then(dve.tensor_tensor(tmp, tmp, ms, ALU.mult))
    then(dve.tensor_scalar(tmp, tmp, -0.5, 1.5, ALU.mult, ALU.add))
    then(dve.tensor_tensor(r, r, tmp, ALU.mult))


class Mem:

    def __init__(self, nc, base):
        self.nc, self.base, self.n = nc, base, 0

    def at(self, name, kb, shape, dt=F32):
        self.n += 1
        return self.nc.alloc_sbuf_tensor_at(f"{name}_{self.n}", list(shape), dt, offset=self.base + (int(kb * KB) + 31) // 32 * 32)


RINGS, CONST, ACTS, FREE, XRES = 0, 24, 32, 96, 175


class Env:

    def __init__(self, nc, ctx, dram):
        self.nc, self.ctx, self.d, self.nsem = nc, ctx, dram, 0
        base = (nc.sbuf_base + 31) // 32 * 32
        ctx.enter_context(nc.sbuf_tensor("arena", [P, 207 * KB // 4], F32))
        self.mem = Mem(nc, base)
        self.pair = [ctx.enter_context(nc.psum_tensor(f"banks{i}", [P, 2 * N], F32)) for i in range(4)]
        self.bank = [self.pair[i // 2][:, i % 2 * N:i % 2 * N + N] for i in range(8)]
        at = self.mem.at
        self.w_raw = at("w_raw", RINGS, [P, RING, N])
        self.w_hi = at("w_hi", RINGS + 8, [P, RING, N], F32R)
        self.w_lo = at("w_lo", RINGS + 16, [P, RING, N], F32R)
        self.act_hi = at("act_hi", ACTS, [P, ND, S], F32R)
        self.act_lo = at("act_lo", ACTS + 32, [P, ND, S], F32R)
        self.xres = at("xres", XRES, [P, NT, D])
        self.ident = at("ident", CONST, [P, P])
        self.ident_bf = at("ident_bf", CONST + 0.5, [P, P], BF16)
        self.mask_bf = at("mask_bf", CONST + 0.75, [P, P], BF16)
        self.mask_f = at("mask_f", CONST + 1, [P, P])

        self.sems = []

    def sem(self, name):
        self.nsem += 1
        self.sems.append(self.nc.alloc_semaphore(name=f"{name}_{self.nsem}"))
        return self.sems[-1]

    def recycle_sems(self):
        self.nc.clear_and_free_semaphores(self.sems)
        self.nc.all_engine_barrier()
        self.sems = []


def norm_stage(v, gain, load_from=None):
    nc, at, sem = v.nc, v.mem.at, v.sem
    gain_b = at("gain_b", FREE, [P, D])
    junk = at("junk", FREE + 4, [P, D])
    xs = at("xs", FREE + 8, [P, 2, D])
    ss = at("ss", FREE + 16, [P, NT])
    ms = at("ms", FREE + 16.1, [P, NT])
    rt = at("rt", FREE + 16.2, [P, NT])
    rstd, tmp = at("rstd", FREE + 16.3, [P, NT]), at("rstd_tmp", FREE + 16.4, [P, NT])
    gain_in, x_in = sem("gain_in"), [sem(f"x_in{t}") for t in range(NT)] if load_from is not None else None
    sq_done, ms_done, rt_done, link = sem("sq_done"), sem("ms_done"), sem("rt_done"), sem("dve_link")
    xs_done, tr_done, hi_done, lo_done = sem("xs_done"), sem("tr_done"), sem("hi_done"), sem("lo_done")

    def hi_of(h, t):
        return v.act_hi[:, 4 * h:4 * h + 4, t * P:(t + 1) * P]

    def lo_of(h, t):
        return v.act_lo[:, 4 * h:4 * h + 4, t * P:(t + 1) * P]

    def tr_bank(n):
        return v.bank[n % 4][:, :].rearrange("p (c t) -> p c t", c=4)

    with nc.Block() as block:
        @block.sync
        def _(sp):
            if load_from is not None:
                for t in range(NT):
                    sp.dma_start(v.xres[:, t, :], load_from[t * P:(t + 1) * P, :]).then_inc(x_in[t], 16)
            sp.dma_start(gain_b[:, :], gain.broadcast_to([P, D])).then_inc(gain_in, 16)

        @block.scalar
        def _(act):
            def evacuate_hi(t):
                for h in range(2):
                    n = 2 * t + h
                    act.wait_ge(tr_done, n + 1)
                    act.activation(hi_of(h, t), tr_bank(n), ACT.Copy).then_inc(hi_done, 1)

            for t in range(NT):
                if load_from is not None:
                    act.wait_ge(x_in[t], 16)
                if t:
                    act.wait_ge(sq_done, t)
                act.activation(junk[:, :], v.xres[:, t, :], ACT.Square, accum_out=ss[:, t:t + 1]).then_inc(sq_done, 1)
                act.wait_ge(ms_done, t + 1)
                act.activation(rt[:, t:t + 1], ms[:, t:t + 1], ACT.Sqrt).then_inc(rt_done, 1)
                if t:
                    evacuate_hi(t - 1)
            evacuate_hi(NT - 1)

        @block.vector
        def _(dve):
            def evacuate_lo(t):
                for h in range(2):
                    n = 2 * t + h
                    dve.wait_ge(hi_done, n + 1)
                    dve.tensor_tensor(lo_of(h, t), tr_bank(n), hi_of(h, t).bitcast(F32), ALU.subtract).then_inc(lo_done, 1)

            _, then = chain(dve, link)
            dve.wait_ge(gain_in, 16)
            for t in range(NT):
                dve.wait_ge(sq_done, t + 1)
                dve.tensor_scalar(ms[:, t:t + 1], ss[:, t:t + 1], 1.0 / D, EPS, ALU.mult, ALU.add).then_inc(ms_done, 1)
                dve.wait_ge(rt_done, t + 1)
                col = slice(t, t + 1)
                inverse_root(dve, then, rstd[:, col], ms[:, col], rt[:, col], tmp[:, col])
                if t >= 2:
                    dve.wait_ge(tr_done, 2 * (t - 1))
                dve.scalar_tensor_tensor(out=xs[:, t % 2, :], in0=v.xres[:, t, :], scalar=rstd[:, t:t + 1],
                                         in1=gain_b[:, :], op0=ALU.mult, op1=ALU.mult).then_inc(xs_done, 1)
                if t:
                    evacuate_lo(t - 1)
            evacuate_lo(NT - 1)

        @block.tensor
        def _(pe):
            for t in range(NT):
                pe.wait_ge(xs_done, t + 1)
                for h in range(2):
                    n = 2 * t + h
                    if n >= 4:
                        pe.wait_ge(lo_done, n - 3)
                    for c in range(4):
                        k = 4 * h + c
                        last = pe.transpose(v.bank[n % 4][:, c * P:(c + 1) * P], xs[:, t % 2, k * P:(k + 1) * P], v.ident[:, :])
                    last.then_inc(tr_done, 1)


class Tile:

    def __init__(self, kind, parts, cols, act, k, first, last, b0=0):
        self.kind, self.parts, self.cols, self.act, self.k = kind, parts, cols, act, k
        self.first, self.last, self.b0 = first, last, b0
        self.after = None
        self.units = NT if kind == "nat" else 2 * (cols // P)


def dense_stage(v, tiles, dve_program, act_steps=None, act_after=None, sp_before=None, sp_steps=None, sems=None):
    nc, sem = v.nc, v.sem
    landed = [sem(f"w_landed{i}") for i in range(RING)]
    hi_done, lo_done, used = sem("w_hi_done"), sem("w_lo_done"), sem("w_used")
    ready, free = sems
    act_steps, sp_steps = act_steps or {}, sp_steps or {}

    with nc.Block() as block:
        @block.sync
        def _(sp):
            if sp_before:
                sp_before(sp)
            for n, tile in enumerate(tiles):
                if n >= RING:
                    sp.wait_ge(lo_done, n - RING + 1)
                for ap, c0, c1 in tile.parts:
                    sp.dma_start(v.w_raw[:, n % RING, c0:c1], ap).then_inc(landed[n % RING], 16)
                for f in sp_steps.get(n, ()):
                    f(sp)

        count, arrived, spent, n_used, n_banks = [0] * RING, [], [], 0, 0
        for n, tile in enumerate(tiles):
            count[n % RING] += 16 * len(tile.parts)
            arrived.append(count[n % RING])
            if tile.last:
                n_banks += tile.units
            else:
                n_used += 1
            spent.append((ready, n_banks) if tile.last else (used, n_used))

        @block.scalar
        def _(act):
            for n, tile in enumerate(tiles):
                act.wait_ge(landed[n % RING], arrived[n])
                if n >= RING:
                    act.wait_ge(*spent[n - RING])
                act.activation(v.w_hi[:, n % RING, :tile.cols], v.w_raw[:, n % RING, :tile.cols], ACT.Copy).then_inc(hi_done, 1)
                for f in act_steps.get(n, ()):
                    f(act)
            if act_after:
                act_after(act)

        @block.gpsimd
        def _(pool):
            for n, tile in enumerate(tiles):
                pool.wait_ge(hi_done, n + 1)
                pool.tensor_tensor(v.w_lo[:, n % RING, :tile.cols], v.w_raw[:, n % RING, :tile.cols],
                                   v.w_hi[:, n % RING, :tile.cols].bitcast(F32), ALU.subtract).then_inc(lo_done, 1)

        @block.vector
        def _(dve):
            dve_program(dve)

        @block.tensor
        def _(pe):
            freed = [0] * 8
            banks = 0
            for n, tile in enumerate(tiles):
                pe.wait_ge(lo_done, n + 1)
                if tile.after:
                    pe.wait_ge(*tile.after)
                hi, lo = tile.act
                w_hi, w_lo = v.w_hi[:, n % RING, :tile.cols], v.w_lo[:, n % RING, :tile.cols]
                for u in range(tile.units):
                    b = tile.b0 + u
                    if tile.first and freed[b]:
                        pe.wait_ge(free, freed[b])
                    if tile.kind == "nat":
                        t = slice(u * P, (u + 1) * P)
                        out = v.bank[b][:, :tile.cols]
                        prods = [(hi[:, tile.k, t], w_hi), (hi[:, tile.k, t], w_lo), (lo[:, tile.k, t], w_hi)]
                    else:
                        c, t = slice(u // 2 * P, u // 2 * P + P), slice(u % 2 * N, u % 2 * N + N)
                        out = v.bank[b][:, :]
                        prods = [(w_hi[:, c], hi[:, tile.k, t]), (w_hi[:, c], lo[:, tile.k, t]), (w_lo[:, c], hi[:, tile.k, t])]
                    for i, (left, right) in enumerate(prods):
                        mm = pe.matmul(out, left, right, start=(tile.first and i == 0), stop=(tile.last and i == 2))
                    if tile.last:
                        banks += 1
                        freed[b] = banks
                        mm.then_inc(ready, 1)
                    elif u == tile.units - 1:
                        mm.then_inc(used, 1)


def rows(w, k, c0, c1):
    return w[k * P:(k + 1) * P, c0:c1]


def group(kind, w, k_tiles, c0, c1, act, k0=0, b0=0):
    return [Tile(kind, [(rows(w, k, c0, c1), 0, c1 - c0)], c1 - c0, act, k0 + k, k == 0, k == k_tiles - 1, b0)
            for k in range(k_tiles)]


class Heads:

    def __init__(self, v, name, dst, heads, at_kb):
        at, sem = v.mem.at, v.sem
        self.dst, self.h = dst, heads
        self.sq = at(name + "_sq", at_kb, [P, heads * HD])
        self.ss = at(name + "_ss", at_kb + 2, [P, NT, heads])
        self.rt = at(name + "_rt", at_kb + 2.25, [P, NT, heads])
        self.r = at(name + "_r", at_kb + 2.5, [P, NT, heads])
        self.tmp = at(name + "_tmp", at_kb + 2.75, [P, NT, heads])
        self.ms_done, self.rt_done = sem(name + "_ms"), sem(name + "_rt")

    def take(self, dve, then, bank, t, free):
        x = self.dst(t)
        src = bank.rearrange("p (h d) -> p h d", h=self.h)
        dve.tensor_copy(x, src).then_inc(free, 1)

    def stat(self, dve, then, t):
        x = self.dst(t)
        sq = self.sq[:, :].rearrange("p (h d) -> p h d", h=self.h)
        then(dve.tensor_tensor(sq, x, x, ALU.mult))
        then(dve.tensor_reduce(self.ss[:, t, :], sq, AX.X, ALU.add))

    def mean(self, dve):
        dve.tensor_scalar(self.ss[:, :, :], self.ss[:, :, :], 1.0 / HD, EPS, ALU.mult, ALU.add).then_inc(self.ms_done, 1)

    def root(self, act):
        act.wait_ge(self.ms_done, 1)
        act.activation(self.rt[:, :, :], self.ss[:, :, :], ACT.Sqrt).then_inc(self.rt_done, 1)

    def inverse(self, dve, then):
        dve.wait_ge(self.rt_done, 1)
        inverse_root(dve, then, self.r[:, :, :], self.ss[:, :, :], self.rt[:, :, :], self.tmp[:, :, :])

    def scale(self, dve, then, t, gain):
        x = self.dst(t)
        then(dve.tensor_tensor(x, x, self.r[:, t, :].unsqueeze(2).broadcast_to([P, self.h, HD]), ALU.mult))
        then(dve.tensor_tensor(x, x, gain.unsqueeze(1).broadcast_to([P, self.h, HD]), ALU.mult))


def rotate(dve, done, then, x, cos, sin, tmp):
    half = HD // 2
    h = x.shape[1]
    x1, x2 = x[:, :, :half], x[:, :, half:]
    c = cos.unsqueeze(1).broadcast_to([P, h, half])
    s = sin.unsqueeze(1).broadcast_to([P, h, half])
    t = [tmp[:, i, :].rearrange("p (h d) -> p h d", h=h) for i in range(4)]
    done(dve.tensor_tensor(t[0], x1, c, ALU.mult))
    done(dve.tensor_tensor(t[1], x2, s, ALU.mult))
    done(dve.tensor_tensor(t[2], x1, s, ALU.mult))
    then(dve.tensor_tensor(t[3], x2, c, ALU.mult))
    done(dve.tensor_tensor(x1, t[0], t[1], ALU.subtract))
    then(dve.tensor_tensor(x2, t[2], t[3], ALU.add))


HG_W, DA_W = HG_H * HG_D, DA_H * 2 * DA_D
COL = dict(zip(("hq", "hf", "hi", "hog", "dq", "dk", "dv", "gate_hg", "gate_da"),
               np.cumsum([0] + [HG_W] * 4 + [DA_W] * 3 + [D]).tolist()))


def block1_tensors(v):
    at = v.mem.at
    v.hqT = at("hqT", FREE, [P, HG_H, S])
    v.hfT = at("hfT", FREE + 16, [P, HG_H, S])
    v.hv = at("hv", FREE + 32, [P, NT, HG_W])
    v.dq = at("dq", FREE + 48, [P, NT, DA_W])
    v.dk = at("dk", FREE + 64, [P, NT, DA_W])
    v.dv = at("dv", FREE + 80, [P, NT, DA_W])


def project1_stage(v):
    nc, at, sem, d = v.nc, v.mem.at, v.sem, v.d
    act_ops = (v.act_hi, v.act_lo)
    w_in = d["w_in"]
    order = ["dq", "dk", "dv", "hq", "hf", "hi", "hog", "gate_hg", "gate_hg+", "gate_da", "gate_da+"]
    tiles = []
    for name in order:
        c0 = COL[name.rstrip("+")] + (N if name.endswith("+") else 0)
        tiles += group("tr" if name[:2] in ("hq", "hf", "ga") else "nat", w_in, ND, c0, c0 + N, act_ops)
    index = {name: g for g, name in enumerate(order)}

    temps = FREE + 96
    q_heads = Heads(v, "dq", lambda t: v.dq[:, t, :].rearrange("p (h d) -> p h d", d=DA_D), 8, temps)
    k_heads = Heads(v, "dk", lambda t: v.dk[:, t, :].rearrange("p (h d) -> p h d", d=DA_D), 8, temps + 3)
    rot = at("rot", temps + 6, [P, 4, 256])
    stage = at("stage", temps + 10, [P, 2, N])
    cos, sin = at("cos", 29, [P, NT, DA_D // 2]), at("sin", 30, [P, NT, DA_D // 2])
    gains = at("gains", 28, [P, 2, DA_D])
    ready, free = sem("bank_ready"), sem("bank_free")
    tables, link = sem("tables"), sem("dve_link")
    staged, stored = sem("gate_staged"), [sem(f"gate_stored{i}") for i in range(2)]

    def load_tables(sp):
        sp.dma_start(cos[:, :, :], d["rope_cos"].rearrange("(t p) c -> p t c", p=P)).then_inc(tables, 16)
        sp.dma_start(sin[:, :, :], d["rope_sin"].rearrange("(t p) c -> p t c", p=P)).then_inc(tables, 16)
        sp.dma_start(gains[:, 0, :], d["da_q_norm"].broadcast_to([P, DA_D])).then_inc(tables, 16)
        sp.dma_start(gains[:, 1, :], d["da_k_norm"].broadcast_to([P, DA_D])).then_inc(tables, 16)

    n_staged = [0]

    def banks_to_dram(g, func, dst):
        def run(act):
            for b in range(8):
                i = n_staged[0]
                n_staged[0] += 1
                act.wait_ge(ready, 8 * g + b + 1)
                if i >= 2:
                    act.wait_ge(stored[i % 2], 16 * (i // 2))
                act.activation(stage[:, i % 2, :], v.bank[b][:, :], func).then_inc(free, 1)
                act.wait_ge(free, 8 * g + b + 1)
                act.dma_start(dst(b), stage[:, i % 2, :]).then_inc(stored[i % 2], 16)
        return run

    def gate_rows(gate, more):
        return lambda b: v.d["gateT"][gate, more * 4 + b // 2, :, (b % 2) * N:(b % 2) * N + N]

    steps = {}

    def after(g, offset, f):
        steps.setdefault(8 * (g + 1) + offset, []).append(f)

    after(index["dq"], 6, q_heads.root)
    after(index["dk"], 6, k_heads.root)
    last = []
    for name, func, dst in (("hog", ACT.Silu, lambda b: v.d["hog"][b * P:(b + 1) * P, :]),
                            ("gate_hg", ACT.Sigmoid, gate_rows(0, 0)), ("gate_hg+", ACT.Sigmoid, gate_rows(0, 1)),
                            ("gate_da", ACT.Sigmoid, gate_rows(1, 0)), ("gate_da+", ACT.Sigmoid, gate_rows(1, 1))):
        g = index[name]
        if 8 * (g + 1) < len(tiles):
            after(g, 2, banks_to_dram(g, func, dst))
        else:
            last.append(banks_to_dram(g, func, dst))

    def act_after(act):
        for f in last:
            f(act)
        for i in range(2):
            act.wait_ge(stored[i], 16 * ((n_staged[0] + 1 - i) // 2))

    def dve_program(dve):
        done, then = chain(dve, link)
        dve.wait_ge(tables, 64)
        then(dve.tensor_scalar(gains[:, 0, :], gains[:, 0, :], DA_D ** -0.5, None, ALU.mult))
        for g, (heads, gain) in enumerate(((q_heads, 0), (k_heads, 1))):
            for t in range(NT):
                dve.wait_ge(ready, 8 * g + t + 1)
                heads.take(dve, then, v.bank[t][:, :], t, free)
                dve.wait_ge(free, 8 * g + t + 1)
                heads.stat(dve, then, t)
            heads.mean(dve)
            heads.inverse(dve, then)
            for t in range(NT):
                heads.scale(dve, then, t, gains[:, gain, :])
                rotate(dve, done, then, heads.dst(t), cos[:, t, :], sin[:, t, :], rot)
        for name, dst in (("dv", v.dv), ("hq", v.hqT), ("hf", v.hfT), ("hi", v.hv)):
            g = index[name]
            for b in range(8):
                dve.wait_ge(ready, 8 * g + b + 1)
                out = dst[:, b, :] if name in ("dv", "hi") else dst[:, b // 2, (b % 2) * N:(b % 2) * N + N]
                dve.tensor_copy(out, v.bank[b][:, :]).then_inc(free, 1)

    dense_stage(v, tiles, dve_program, steps, act_after, sp_before=load_tables, sems=(ready, free))


def hgrn_stage(v):
    nc, at, sem, d = v.nc, v.mem.at, v.sem, v.d
    o = at("o_raw", ACTS, [P, NT, HG_W])
    sets = [dict((name, at(f"{name}{i}", ACTS + 16 + 16 * i + 4 * j, [P, S]))
                 for j, name in enumerate(("q_rel", "k_rel", "q_dec", "k_end"))) for i in range(2)]
    b_ = at("b", ACTS + 48, [P, S])
    e_ = at("e", ACTS + 52, [P, S])
    keep = at("keep", ACTS + 56, [P, S])
    k_rows = at("k_rows", ACTS + 60, [P, NT, P])
    scT = at("scT", FREE + 96, [P, 2, NT, CHUNK])
    st = at("state", FREE + 100, [P, NCH, P])
    causal = at("causal", FREE + 108, [P, CHUNK], I32)
    lb = at("lb", FREE + 108.5, [P, 2, HG_H])
    lbt = at("lbt", FREE + 108.75, [P, 4, HG_H])
    dec = at("dec", FREE + 109, [P, 2, NCH])
    consts, link, alink = sem("consts"), sem("dve_link"), sem("act_link")
    lb_exp, sig, f_done, ln_done = sem("lb_exp"), sem("sig"), sem("f_done"), sem("ln_done")
    to_exp, exps = sem("to_exp"), sem("exps")
    qk_done, kend_done, scores, scT_done = sem("qk_done"), sem("kend_done"), sem("scores"), sem("scT_done")
    tr_done, rows_done, u_done, state_done, u_read = sem("tr_done"), sem("rows_done"), sem("u_done"), sem("state_done"), sem("u_read")
    o_done, o_read, zero, decs = sem("o_done"), sem("o_read"), sem("zero"), sem("decs")
    sum_done, root_done, hog_in, gain_in = sem("sum_done"), sem("root_done"), sem("hog_in"), sem("gain_in")

    def by_chunk(x):
        return x.rearrange("p (c t) -> p c t", t=CHUNK)

    sq = at("sq", ACTS + 16, [P, NT, HG_W])
    hog = at("hog", ACTS + 32, [P, NT, HG_W])
    gain = at("hg_gain", ACTS + 48, [P, HG_D])
    ssum = at("ssum", ACTS + 49, [P, NT * HG_H])
    root, inv, itmp = (at(f"o_{i}", ACTS + 49.25 + 0.25 * i, [P, NT * HG_H]) for i in range(3))
    v.o_hg = at("o_hg", FREE, [P, NT, HG_W])

    with nc.Block() as block:
        @block.sync
        def _(sp):
            sp.dma_start(keep[:, :], d["chunk_keep"].broadcast_to([P, S])).then_inc(consts, 16)
            sp.dma_start(causal[:, :], d["causal_st"]).then_inc(consts, 16)
            with nc.allow_non_contiguous_dma("lower bounds by partition"):
                sp.dma_start(lbt[:, 0:2, :], d["hg_lb"].rearrange("r (h p) -> p r h", p=P)).then_inc(consts, 16)
            sp.wait_ge(o_read, 2 * HG_H)
            sp.dma_start(hog[:, :, :], d["hog"].rearrange("(t p) c -> p t c", p=P)).then_inc(hog_in, 16)
            sp.dma_start(gain[:, :], d["hg_out_norm"].broadcast_to([P, HG_D])).then_inc(hog_in, 16)

        @block.scalar
        def _(act):
            act.activation(v.hfT[:, :, :], v.hfT[:, :, :], ACT.Sigmoid).then_inc(sig, 1)
            act.wait_ge(lb_exp, 1)
            act.activation(lbt[:, 2:4, :], lbt[:, 2:4, :], ACT.Exp).then_inc(sig, 1)

            def out(h):
                for half in range(2):
                    n = 2 * h + half
                    act.wait_ge(o_done, n + 1)
                    act.activation(o[:, 4 * half:4 * half + 4, h * P:(h + 1) * P],
                                   v.bank[6 + half][:, :].rearrange("p (t c) -> p t c", t=4), ACT.Copy).then_inc(o_read, 1)

            for h in range(HG_H):
                act.wait_ge(f_done, h + 1)
                act.activation(v.hfT[:, h, :], v.hfT[:, h, :], ACT.Ln).then_inc(ln_done, 1)
                for i, sign in enumerate((1.0, -1.0, 1.0, 1.0)):
                    if i == 2:
                        act.wait_ge(qk_done, 4 * h + 2)
                    else:
                        act.wait_ge(to_exp, 3 * h + (0, 1, 2, 2)[i] + 1)
                    act.activation(e_[:, :], (b_ if i == 2 else e_)[:, :], ACT.Exp, scale=sign).then_inc(exps, 1)
                if h:
                    out(h - 1)
                for half in range(2):
                    n = 2 * h + half
                    act.wait_ge(tr_done, n + 1)
                    if h:
                        act.wait_ge(u_done, 2 * h)
                    act.activation(k_rows[:, 4 * half:4 * half + 4, :],
                                   v.bank[half][:, :].rearrange("p (t c) -> p t c", t=4), ACT.Copy).then_inc(rows_done, 1)
            out(HG_H - 1)
            act.wait_ge(sum_done, 1)
            act.activation(root[:, :], ssum[:, :], ACT.Sqrt).then_inc(root_done, 1)

        @block.vector
        def _(dve):
            done, then = chain(dve, link)
            dve.memset(scT[:, :, :, :], 0.0).then_inc(zero, 1)
            dve.wait_ge(consts, 48)
            then(dve.tensor_tensor(lb[:, 0, :], lbt[:, 0, :], lbt[:, 1, :], ALU.max))
            dve.tensor_tensor(lbt[:, 2:4, :], lbt[:, 0:2, :], lb[:, 0:1, :].broadcast_to([P, 2, HG_H]), ALU.subtract).then_inc(lb_exp, 1)
            dve.wait_ge(sig, 2)
            then(dve.tensor_tensor(lb[:, 1, :], lbt[:, 2, :], lbt[:, 3, :], ALU.add))
            then(dve.reciprocal(lb[:, 1, :], lb[:, 1, :]))
            then(dve.tensor_tensor(lb[:, 0, :], lbt[:, 2, :], lb[:, 1, :], ALU.mult))
            then(dve.tensor_scalar(lb[:, 1, :], lb[:, 0, :], -1.0, 1.0, ALU.mult, ALU.add))

            def states(h):
                for c in range(NCH):
                    if c % 8 == 0:
                        dve.wait_ge(u_done, 2 * h + c // 8 + 1)
                    u = v.bank[2 + c % 2][:, (c // 2 % 4) * P:(c // 2 % 4 + 1) * P]
                    if c == 0:
                        if h:
                            dve.wait_ge(o_done, 2 * h)
                        ins = dve.tensor_copy(st[:, 0, :], u)
                    else:
                        dve.wait_ge(state_done, NCH * h + c)
                        ins = dve.scalar_tensor_tensor(out=st[:, c, :], in0=st[:, c - 1, :], scalar=dec[:, h % 2, c:c + 1], in1=u,
                                                       op0=ALU.mult, op1=ALU.add)
                    ins.then_inc(state_done, 1)

            def causal_scores(h):
                dve.wait_ge(scores, h + 1)
                if h >= 2:
                    dve.wait_ge(o_done, 2 * (h - 1))
                dve.copy_predicated(scT[:, h % 2, :, :], causal[:, :].unsqueeze(1).broadcast_to([P, NT, CHUNK]),
                                    v.bank[4 + h % 2][:, :].rearrange("p (t c) -> p t c", t=NT)).then_inc(scT_done, 1)

            for h in range(HG_H):
                s = sets[h % 2]
                if h >= 2:
                    dve.wait_ge(o_done, 2 * (h - 1))
                f = v.hfT[:, h, :]
                then(dve.tensor_scalar(f, f, lb[:, 1, h:h + 1], lb[:, 0, h:h + 1], ALU.mult, ALU.add))
                dve.tensor_scalar(s["k_end"][:, :], f, -1.0, 1.0, ALU.mult, ALU.add).then_inc(f_done, 1)
                dve.wait_ge(ln_done, h + 1)
                if h:
                    dve.wait_ge(exps, 4 * h)
                then(dve.tensor_tensor_scan(b_[:, :], keep[:, :], f, 0.0, ALU.mult, ALU.add))
                mid, end = by_chunk(b_[:, :])[:, :, CHUNK // 2 - 1:CHUNK // 2], by_chunk(b_[:, :])[:, :, CHUNK - 1:CHUNK]
                for i in range(4):
                    if i != 2:
                        ref = (mid if i < 2 else end).broadcast_to([P, NCH, CHUNK])
                        pair = (by_chunk(b_[:, :]), ref) if i < 2 else (ref, by_chunk(b_[:, :]))
                        dve.tensor_tensor(by_chunk(e_[:, :]), pair[0], pair[1], ALU.subtract).then_inc(to_exp, 1)
                    dve.wait_ge(exps, 4 * h + i + 1)
                    if i == 2:
                        then(dve.tensor_copy(dec[:, h % 2, :], by_chunk(e_[:, :])[:, :, CHUNK - 1:CHUNK].rearrange("p c o -> p (c o)")))
                    name, src = (("q_rel", v.hqT[:, h, :]), ("k_rel", s["k_end"][:, :]), ("q_dec", v.hqT[:, h, :]), ("k_end", s["k_end"][:, :]))[i]
                    ins = dve.tensor_tensor(s[name][:, :], src, e_[:, :], ALU.mult)
                    ins.then_inc(qk_done, 1)
                    dve.wait_ge(qk_done, 4 * h + i + 1)
                if h:
                    causal_scores(h - 1)
                    states(h - 1)
            causal_scores(HG_H - 1)
            states(HG_H - 1)
            dve.wait_ge(o_read, 2 * HG_H)
            heads = "p t (h c) -> p (t h) c"
            o3, sq3, og3 = (x[:, :, :].rearrange(heads, c=HG_D) for x in (o, sq, v.o_hg))
            then(dve.tensor_tensor(sq3, o3, o3, ALU.mult))
            then(dve.tensor_reduce(ssum[:, :], sq3, AX.X, ALU.add))
            dve.tensor_scalar(ssum[:, :], ssum[:, :], 1.0 / HG_D, EPS, ALU.mult, ALU.add).then_inc(sum_done, 1)
            dve.wait_ge(root_done, 1)
            inverse_root(dve, then, inv[:, :], ssum[:, :], root[:, :], itmp[:, :])
            then(dve.tensor_tensor(o3, o3, inv[:, :].unsqueeze(2).broadcast_to([P, NT * HG_H, HG_D]), ALU.mult))
            dve.wait_ge(hog_in, 32)
            then(dve.tensor_tensor(o3, o3, gain[:, :].unsqueeze(1).broadcast_to([P, NT * HG_H, HG_D]), ALU.mult))
            then(dve.tensor_tensor(v.o_hg[:, :, :], o[:, :, :], hog[:, :, :], ALU.mult))

        @block.tensor
        def _(pe):
            def chunk_rows(c):
                return slice(c % 2 * CHUNK, c % 2 * CHUNK + CHUNK)

            for h in range(HG_H):
                s = sets[h % 2]
                hc = slice(h * P, (h + 1) * P)
                pe.wait_ge(qk_done, 4 * h + 2)
                if h >= 2:
                    pe.wait_ge(scT_done, h - 1)
                for c in range(NCH):
                    t = slice(c * CHUNK, (c + 1) * CHUNK)
                    mm = pe.matmul(v.bank[4 + h % 2][chunk_rows(c), c // 2 * CHUNK:(c // 2 + 1) * CHUNK],
                                   s["k_rel"][:, t], s["q_rel"][:, t], start=True, stop=True)
                mm.then_inc(scores, 1)
                pe.wait_ge(qk_done, 4 * h + 4)
                for half in range(2):
                    if h:
                        pe.wait_ge(rows_done, 2 * (h - 1) + half + 1)
                    for t in range(4):
                        tt = 4 * half + t
                        mm = pe.transpose(v.bank[half][:, t * P:(t + 1) * P], s["k_end"][:, tt * P:(tt + 1) * P], v.ident[:, :])
                    mm.then_inc(tr_done, 1)
                for c in range(NCH):
                    n = 2 * h + c // 8
                    if c % 8 == 0:
                        pe.wait_ge(rows_done, n + 1)
                        if n:
                            pe.wait_ge(state_done, 8 * n)
                    r = chunk_rows(c)
                    mm = pe.matmul(v.bank[2 + c % 2][:, (c // 2 % 4) * P:(c // 2 % 4 + 1) * P], k_rows[r, c // 2, :], v.hv[r, c // 2, hc],
                                   start=True, stop=True)
                    if c % 8 == 7:
                        mm.then_inc(u_done, 1)
                pe.wait_ge(scT_done, h + 1)
                for half in range(2):
                    n = 2 * h + half
                    if h:
                        pe.wait_ge(o_read, n - 1)
                    for c in range(8 * half, 8 * half + 8):
                        r, tt = chunk_rows(c), c // 2
                        out = v.bank[6 + half][r, (tt % 4) * P:(tt % 4 + 1) * P]
                        mm = pe.matmul(out, scT[r, h % 2, tt, :], v.hv[r, tt, hc], start=True, stop=(c == 0))
                        if c:
                            pe.wait_ge(state_done, NCH * h + c)
                            mm = pe.matmul(out, s["q_dec"][:, c * CHUNK:(c + 1) * CHUNK], st[:, c - 1, :], start=False, stop=True)
                    mm.then_inc(o_done, 1)


def score_products(pe, v, pair, lhsT, keys, nk, diagonal):
    for c0 in range(0, nk, N):
        c1 = min(c0 + N, nk)
        masked = diagonal and c1 == nk
        mm = pe.matmul(pair[:, c0:c1], lhsT, keys[:, c0:c1], start=True, stop=not masked)
        if masked:
            mm = pe.matmul(pair[:, nk - P:nk], v.ident_bf[:, :], v.mask_bf[:, :], start=False, stop=True)
    return mm


def diff_attention_stage(v):
    nc, at, sem, d = v.nc, v.mem.at, v.sem, v.d
    qT, kT = at("qT", FREE + 16, [P, DA_H, S]), at("kT", FREE + 32, [P, DA_H, S])
    probs = at("probs", ACTS, [P, 2, 2, S])
    a_ = at("a", ACTS + 16, [P, 2, S])
    aT = at("aT", ACTS + 24, [P, 2, S])
    o = at("o_raw", ACTS + 32, [P, NT, DA_W])
    sq = at("sq", ACTS + 48, [P, NT, DA_W])
    small = FREE + 96
    lam_in = at("lam_in", small, [P, 4, DA_D])
    lam_pr = at("lam_pr", small + 1, [P, 2, DA_D])
    lam = at("lam", small + 1.5, [P, 4])
    gain = at("da_gain", small + 2, [P, 2 * DA_D])
    nmax, sums, inv, coef = (at(n, small + 3 + 0.25 * i, [P, 4, 2]) for i, n in enumerate(("nmax", "sums", "inv", "coef")))
    ssum, root, rinv, itmp = (at(f"oda_{i}", small + 4 + 0.25 * i, [P, NT * DA_H]) for i in range(4))
    v.o_da = at("o_da", FREE + 48, [P, NT, DA_W])

    link, lam_loaded, lam_dot, lam_exp = sem("dve_link"), sem("lam_loaded"), sem("lam_dot"), sem("lam_exp")
    tr_ready, q_read, k_read = sem("tr_ready"), sem("q_read"), sem("k_read")
    scored, maxed, exped, mixed = sem("scored"), sem("maxed"), sem("exped"), sem("mixed")
    turned, turn_read, weighed, weigh_read = sem("turned"), sem("turn_read"), sem("weighed"), sem("weigh_read")
    sum_done, root_done = sem("sum_done"), sem("root_done")
    units = [(h, i) for h in range(DA_H) for i in range(NT)]
    groups = [-(-(i + 1) // 4) for _, i in units]
    behind = np.cumsum([0] + groups).tolist()

    with nc.Block() as block:
        @block.sync
        def _(sp):
            sp.dma_start(lam_in[:, :, :], d["da_lambda"].rearrange("(o a) c -> o a c", o=1).broadcast_to([P, 4, DA_D])).then_inc(lam_loaded, 16)
            sp.dma_start(gain[:, :], d["da_out_norm"].broadcast_to([P, 2 * DA_D])).then_inc(lam_loaded, 16)

        @block.scalar
        def _(act):
            for n in range(2 * NT):
                if n % 2:
                    act.wait_ge(tr_ready, n + 1)
                    dst = kT[:, :, n // 2 * P:(n // 2 + 1) * P]
                    act.activation(dst, v.bank[n % 4].rearrange("p (h t) -> p h t", h=DA_H), ACT.Copy).then_inc(k_read, 1)
                if n == 8:
                    act.wait_ge(lam_dot, 1)
                    act.activation(lam[:, 0:2], lam[:, 0:2], ACT.Exp).then_inc(lam_exp, 1)

            def turn_out(p):
                for g in range(groups[p]):
                    n = behind[p] + g
                    c1 = min((g + 1) * N, (units[p][1] + 1) * P)
                    act.wait_ge(turned, n + 1)
                    if g == 0 and p >= 2:
                        act.wait_ge(weighed, p - 1)
                    act.activation(aT[:, p % 2, g * N:c1], v.bank[4 + n % 2][:, :c1 - g * N], ACT.Copy).then_inc(turn_read, 1)

            for p, (h, i) in enumerate(units):
                nk = (i + 1) * P
                for half in range(2):
                    act.wait_ge(maxed, 2 * p + half + 1)
                    if p >= 2:
                        act.wait_ge(mixed, p - 1)
                    act.activation(probs[:, p % 2, half, :nk], v.pair[half][:, :nk], ACT.Exp, bias=nmax[:, p % 4, half:half + 1],
                                   accum_out=sums[:, p % 4, half:half + 1]).then_inc(exped, 1)
                if p:
                    turn_out(p - 1)
            turn_out(len(units) - 1)
            act.wait_ge(sum_done, 1)
            act.activation(root[:, :], ssum[:, :], ACT.Sqrt).then_inc(root_done, 1)

        @block.vector
        def _(dve):
            done, then = chain(dve, link)
            dve.wait_ge(lam_loaded, 32)
            pairs = lam_in[:, :, :].rearrange("p (a b) c -> p a b c", b=2)
            then(dve.tensor_tensor(lam_pr[:, :, :], pairs[:, :, 0, :], pairs[:, :, 1, :], ALU.mult))
            dve.tensor_reduce(lam[:, 0:2], lam_pr[:, :, :], AX.X, ALU.add).then_inc(lam_dot, 1)
            done(dve.tensor_scalar(gain[:, :], gain[:, :], 1.0 - LAM_INIT, None, ALU.mult))
            for n in range(0, 2 * NT, 2):
                dve.wait_ge(tr_ready, n + 1)
                dst = qT[:, :, n // 2 * P:(n // 2 + 1) * P]
                dve.tensor_copy(dst, v.bank[n % 4].rearrange("p (h t) -> p h t", h=DA_H)).then_inc(q_read, 1)
            dve.wait_ge(lam_exp, 1)
            then(dve.tensor_tensor(lam[:, 2:3], lam[:, 1:2], lam[:, 0:1], ALU.subtract))
            then(dve.tensor_scalar(lam[:, 3:4], lam[:, 2:3], -LAM_INIT, None, ALU.add))

            def mix(p):
                s, nk = p % 4, (units[p][1] + 1) * P
                dve.wait_ge(exped, 2 * p + 2)
                then(dve.reciprocal(inv[:, s, :], sums[:, s, :]))
                then(dve.scalar_tensor_tensor(out=coef[:, s, 0:1], in0=sums[:, s, 0:1], scalar=inv[:, s, 1:2], in1=lam[:, 3:4],
                                              op0=ALU.mult, op1=ALU.mult))
                if p >= 2:
                    dve.wait_ge(turned, behind[p - 1])
                dve.scalar_tensor_tensor(out=a_[:, p % 2, :nk], in0=probs[:, p % 2, 1, :nk], scalar=coef[:, s, 0:1],
                                         in1=probs[:, p % 2, 0, :nk], op0=ALU.mult, op1=ALU.add).then_inc(mixed, 1)

            def out(p):
                h, i = units[p]
                dve.wait_ge(weighed, p + 1)
                dve.tensor_scalar(o[:, i, h * P:(h + 1) * P], v.bank[6 + p % 2][:, 0:P], inv[:, p % 4, 0:1], None,
                                  ALU.mult).then_inc(weigh_read, 1)

            for p, (h, i) in enumerate(units):
                nk = (i + 1) * P
                for half in range(2):
                    dve.wait_ge(scored, 2 * p + half + 1)
                    dve.tensor_reduce(nmax[:, p % 4, half:half + 1], v.pair[half][:, :nk], AX.X, ALU.max, negate=True).then_inc(maxed, 1)
                if p >= 1:
                    mix(p - 1)
                if p >= 2:
                    out(p - 2)
            mix(len(units) - 1)
            out(len(units) - 2)
            out(len(units) - 1)
            dve.wait_ge(weigh_read, len(units))
            heads = "p t (h c) -> p (t h) c"
            o3, sq3, od3 = (x[:, :, :].rearrange(heads, c=2 * DA_D) for x in (o, sq, v.o_da))
            then(dve.tensor_tensor(sq3, o3, o3, ALU.mult))
            then(dve.tensor_reduce(ssum[:, :], sq3, AX.X, ALU.add))
            dve.tensor_scalar(ssum[:, :], ssum[:, :], 1.0 / (2 * DA_D), EPS, ALU.mult, ALU.add).then_inc(sum_done, 1)
            dve.wait_ge(root_done, 1)
            inverse_root(dve, then, rinv[:, :], ssum[:, :], root[:, :], itmp[:, :])
            then(dve.tensor_tensor(o3, o3, rinv[:, :].unsqueeze(2).broadcast_to([P, NT * DA_H, 2 * DA_D]), ALU.mult))
            then(dve.tensor_tensor(od3, o3, gain[:, :].unsqueeze(1).broadcast_to([P, NT * DA_H, 2 * DA_D]), ALU.mult))

        @block.tensor
        def _(pe):
            for n in range(2 * NT):
                if n >= 4:
                    pe.wait_ge(k_read if n % 2 else q_read, n // 2 - 1)
                src, t = (v.dk if n % 2 else v.dq), n // 2
                for h in range(DA_H):
                    mm = pe.transpose(v.bank[n % 4][:, h * P:(h + 1) * P], src[:, t, h * P:(h + 1) * P], v.ident[:, :])
                mm.then_inc(tr_ready, 1)
            pe.wait_ge(q_read, NT)
            pe.wait_ge(k_read, NT)

            def scores(p):
                h, i = units[p]
                for half in range(2):
                    if p:
                        pe.wait_ge(exped, 2 * (p - 1) + half + 1)
                    r = slice(half * DA_D, (half + 1) * DA_D)
                    mm = score_products(pe, v, v.pair[half], qT[r, h, i * P:(i + 1) * P], kT[r, h, :], (i + 1) * P, True)
                    mm.then_inc(scored, 1)

            def turn(p):
                pe.wait_ge(mixed, p + 1)
                for g in range(groups[p]):
                    n = behind[p] + g
                    if n >= 2:
                        pe.wait_ge(turn_read, n - 1)
                    for j in range(4 * g, min(4 * g + 4, units[p][1] + 1)):
                        mm = pe.transpose(v.bank[4 + n % 2][:, (j - 4 * g) * P:(j - 4 * g + 1) * P], a_[:, p % 2, j * P:(j + 1) * P], v.ident[:, :])
                    mm.then_inc(turned, 1)

            def weigh(p):
                h, i = units[p]
                pe.wait_ge(turn_read, behind[p + 1])
                if p >= 2:
                    pe.wait_ge(weigh_read, p - 1)
                for j in range(i + 1):
                    mm = pe.matmul(v.bank[6 + p % 2][:, 0:P], aT[:, p % 2, j * P:(j + 1) * P], v.dv[:, j, h * P:(h + 1) * P],
                                   start=(j == 0), stop=(j == i))
                mm.then_inc(weighed, 1)

            for p in range(len(units)):
                scores(p)
                if p >= 2:
                    weigh(p - 2)
                if p >= 1:
                    turn(p - 1)
            weigh(len(units) - 2)
            turn(len(units) - 1)
            weigh(len(units) - 1)


def turn_rows_stage(v, chunk, arrive=None, sp_program=None):
    nc, sem = v.nc, v.sem
    turned, hi_done, lo_done = sem("turned"), sem("hi_done"), sem("lo_done")

    def part(x, h, t):
        return x[:, 4 * h:4 * h + 4, t * P:(t + 1) * P]

    def bank(n):
        return v.bank[n % 8].rearrange("p (c t) -> p c t", c=4)

    with nc.Block() as block:
        @block.sync
        def _(sp):
            if sp_program:
                sp_program(sp)

        @block.scalar
        def _(act):
            for n in range(2 * NT):
                act.wait_ge(turned, n + 1)
                act.activation(part(v.act_hi, n % 2, n // 2), bank(n), ACT.Copy).then_inc(hi_done, 1)

        @block.vector
        def _(dve):
            for n in range(2 * NT):
                dve.wait_ge(hi_done, n + 1)
                dve.tensor_tensor(part(v.act_lo, n % 2, n // 2), bank(n), part(v.act_hi, n % 2, n // 2).bitcast(F32),
                                  ALU.subtract).then_inc(lo_done, 1)

        @block.tensor
        def _(pe):
            for n in range(2 * NT):
                t, h = n // 2, n % 2
                if arrive and h == 0:
                    arrive(pe, t)
                if n >= 8:
                    pe.wait_ge(lo_done, n - 7)
                for c in range(4):
                    mm = pe.transpose(v.bank[n % 8][:, c * P:(c + 1) * P], chunk(t, 4 * h + c), v.ident[:, :])
                mm.then_inc(turned, 1)


def turn_mixers_stage(v):
    def chunk(t, k):
        return (v.o_hg if k < 4 else v.o_da)[:, t, k % 4 * P:(k % 4 + 1) * P]
    turn_rows_stage(v, chunk)


def branch_stage(v):
    nc, at, sem, d = v.nc, v.mem.at, v.sem, v.d
    v.mix_hi, v.mix_lo = at("mix_hi", FREE, [P, ND, S], F32R), at("mix_lo", FREE + 32, [P, ND, S], F32R)
    hg = at("hg_part", FREE + 64, [P, 8, N])
    gate = at("gate", FREE + 80, [P, 8, N])
    m = at("m", FREE + 96, [P, 2, N])
    W = 2 * P
    act = (v.act_hi, v.act_lo)
    tiles = []
    for g in range(D // W):
        c0, c1 = g * W, (g + 1) * W
        tiles += group("tr", d["w_branch_hg"], HG_W // P, c0, c1, act, 0, 0)
        tiles += group("tr", d["w_branch_da"], DA_W // P, c0, c1, act, HG_W // P, 4)
    ready, free, link = sem("bank_ready"), sem("bank_free"), sem("dve_link")
    gate_in = [sem(f"gate_in{i}") for i in range(8)]
    m_done, hi_done = sem("m_done"), sem("mix_hi_done")
    used = []
    for g in range(D // W):
        used += [(g, side, u) for side in range(2) for u in range(4)]

    def load_gate(n):
        g, side, u = used[n]

        def run(sp):
            if n >= 8:
                sp.wait_ge(free, n - 7)
            sp.dma_start(gate[:, n % 8, :], d["gateT"][side, 2 * g + u // 2, :, u % 2 * N:u % 2 * N + N]).then_inc(gate_in[n % 8], 16)
        return run

    sp_steps = {n: [load_gate(n)] for n in range(len(used))}
    act_steps = {}

    def hi_part(g):
        def run(act_):
            for u in range(4):
                i = 4 * g + u
                act_.wait_ge(m_done, i + 1)
                act_.activation(v.mix_hi[:, 2 * g + u // 2, u % 2 * N:u % 2 * N + N], m[:, i % 2, :], ACT.Copy).then_inc(hi_done, 1)
        return run

    for g in range(D // W - 1):
        act_steps[8 * (g + 1) + 2] = [hi_part(g)]

    def dve_program(dve):
        done, then = chain(dve, link)
        for g in range(D // W):
            for side in range(2):
                for u in range(4):
                    n = 8 * g + 4 * side + u
                    dve.wait_ge(gate_in[n % 8], 16 * (n // 8 + 1))
                    dve.wait_ge(ready, n + 1)
                    if side == 0:
                        dve.tensor_tensor(hg[:, 4 * (g % 2) + u, :], v.bank[u], gate[:, n % 8, :], ALU.mult).then_inc(free, 1)
                        continue
                    i = 4 * g + u
                    if i >= 2:
                        dve.wait_ge(lo_done, i - 1)
                    dve.tensor_tensor(m[:, i % 2, :], v.bank[4 + u], gate[:, n % 8, :], ALU.mult).then_inc(free, 1)
                    dve.wait_ge(free, n + 1)
                    dve.tensor_tensor(m[:, i % 2, :], m[:, i % 2, :], hg[:, 4 * (g % 2) + u, :], ALU.add).then_inc(m_done, 1)
                    if i:
                        low(dve, i - 1)
        low(dve, 4 * (D // W) - 1)

    lo_done = sem("mix_lo_done")

    def low(dve, i):
        g, u = i // 4, i % 4
        dve.wait_ge(hi_done, i + 1)
        c, t = 2 * g + u // 2, slice(u % 2 * N, u % 2 * N + N)
        dve.tensor_tensor(v.mix_lo[:, c, t], m[:, i % 2, :], v.mix_hi[:, c, t].bitcast(F32), ALU.subtract).then_inc(lo_done, 1)

    dense_stage(v, tiles, dve_program, act_steps, act_after=hi_part(D // W - 1), sp_steps=sp_steps, sems=(ready, free))


def add_rows_stage(v, tiles, groups_of, load_from=None, to_dram=None):
    nc, sem = v.nc, v.sem
    ready, free = sem("bank_ready"), sem("bank_free")
    x_in = sem("x_in")

    def load(sp):
        if load_from is not None:
            sp.dma_start(v.xres[:, :, :], load_from.rearrange("(t p) c -> p t c", p=P)).then_inc(x_in, 16)

    def dve_program(dve):
        if load_from is not None:
            dve.wait_ge(x_in, 16)
        for g, c0 in enumerate(groups_of):
            for t in range(NT):
                dve.wait_ge(ready, 8 * g + t + 1)
                x = v.xres[:, t, c0:c0 + N]
                dve.tensor_tensor(x, v.bank[t], x, ALU.add).then_inc(free, 1)

    dense_stage(v, tiles, dve_program, sp_before=load, sems=(ready, free))


def output1_stage(v):
    act = (v.mix_hi, v.mix_lo)
    tiles = sum((group("nat", v.d["w_out"], ND, c, c + N, act) for c in (0, N)), [])
    add_rows_stage(v, tiles, (0, N), load_from=v.d["x"])


def router_stage(v):
    nc, at, sem, d = v.nc, v.mem.at, v.sem, v.d
    f = FREE
    gain_b, junk = at("gain_b", f, [P, D]), at("junk", f + 4, [P, D])
    xs = at("xs", f + 8, [P, 2, D])
    xT = at("xT", f + 16, [P, 2, ND, P])
    wr = at("w_router", f + 24, [P, ND, NG + NE])
    bias = at("b_router", f + 25.5, [P, NG + NE])
    lg = at("logits", f + 26, [P, NT, NG + NE])
    upper, ones = at("upper", f + 28, [P, P]), at("ones", f + 28.5, [P, P])
    n_first = NG + NE8 + NSLOT_BLK + NT + NBLK // 2
    firsts = at("firsts", f + 29, [P, n_first])
    ss, ms, rt, rstd, tmp = (at(f"r{i}", f + 30 + 0.125 * i, [P, NT]) for i in range(5))
    A = [at(f"route{i}", f + 31 + i, [P, NT * NE]) for i in range(12)]
    B = [at(f"small{i}", f + 43 + 0.25 * i, [P, NT * NE8]) for i in range(12)]
    cmp_ = at("cmp", f + 48, [P, NSLOT_BLK * NE])
    token_rows = at("token_rows", f + 56, [P, TOPK, NT, 2], I32)
    v.e_w = at("e_w", CONST + 2, [P, TOPK, NT])
    v.dest = at("dest", CONST + 2.25, [P, TOPK, NT], I32)
    v.blk_e = at("blk_e", CONST + 2.5, [1, NSLOT_BLK], I32)
    v.turns = at("turns", CONST + 2.75, [1, 8], I32)
    v.slots = at("slots", CONST + 3, [P, NSLOT_BLK, 2], I32)

    const_in, slots_init = sem("const_in"), sem("slots_init")
    sq_done, ms_done, rt_done, link = sem("sq_done"), sem("ms_done"), sem("rt_done"), sem("dve_link")
    xs_done, stored, turned, xT_done, logit, logit_read = (sem(n) for n in ("xs_done", "stored", "turned", "xT_done", "logit", "logit_read"))
    x_exp, exped, chosen, ranked, ones_set = sem("x_exp"), sem("exped"), sem("chosen"), sem("ranked"), sem("ones_set")
    placed, scattered, listed = sem("placed"), sem("scattered"), sem("listed")
    store_n = [sem(f"store{i}") for i in range(2)]

    def first(a, n):
        return firsts[:, a:a + n]

    f_group, f_expert, f_block, f_tile, f_turn = (first(a, n) for a, n in zip(
        np.cumsum([0, NG, NE8, NSLOT_BLK, NT]).tolist(), (NG, NE8, NSLOT_BLK, NT, NBLK // 2)))

    with nc.Block() as block:
        @block.sync
        def _(sp):
            sp.dma_start(gain_b[:, :], d["norm_moe"].broadcast_to([P, D])).then_inc(const_in, 16)
            sp.dma_start(wr[:, :, 0:NG], d["w_router_group"].rearrange("(k p) n -> p k n", p=P)).then_inc(const_in, 16)
            sp.dma_start(wr[:, :, NG:], d["w_router_expert"].rearrange("(k p) n -> p k n", p=P)).then_inc(const_in, 16)
            sp.dma_start(bias[:, 0:NG], d["b_router_group"].broadcast_to([P, NG])).then_inc(const_in, 16)
            sp.dma_start(bias[:, NG:], d["b_router_expert"].broadcast_to([P, NE])).then_inc(const_in, 16)
            sp.dma_start(upper[:, :], d["upper"]).then_inc(const_in, 16)
            sp.dma_start(firsts[:, :], d["firsts"].broadcast_to([P, n_first])).then_inc(const_in, 16)
            sp.dma_start(token_rows[:, :, :, :], d["token_rows"]).then_inc(const_in, 16)
            sp.dma_start(d["slot_table"], d["slot_init"]).then_inc(slots_init, 16)
            for t in range(NT):
                sp.wait_ge(xs_done, t + 1)
                sp.dma_start(d["xn"][t * P:(t + 1) * P, :], xs[:, t % 2, :]).then_inc(store_n[t % 2], 16)
            for i in range(2):
                sp.wait_ge(store_n[i], 16 * NT // 2)
            sp.wait_ge(scattered, 16 * TOPK * NT)
            with nc.allow_non_contiguous_dma("slots of a block by partition"):
                sp.dma_start(v.slots[:, :, :], d["slot_table"].rearrange("(b p) o -> p b o", p=P)).then_inc(listed, 16)
            sp.wait_ge(listed, 16)

        @block.gpsimd
        def _(pool):
            pool.wait_ge(slots_init, 16)
            pool.wait_ge(const_in, 128)
            pool.wait_ge(placed, 1)
            for k in range(TOPK):
                for t in range(NT):
                    pool.indirect_dma_start(d["slot_table"], bass.IndirectOffsetOnAxis(ap=v.dest[:, k, t:t + 1], axis=0),
                                            token_rows[:, k, t, :], None).then_inc(scattered, 16)

        @block.scalar
        def _(act):
            for t in range(NT):
                if t:
                    act.wait_ge(sq_done, t)
                act.activation(junk[:, :], v.xres[:, t, :], ACT.Square, accum_out=ss[:, t:t + 1]).then_inc(sq_done, 1)
                act.wait_ge(ms_done, t + 1)
                act.activation(rt[:, t:t + 1], ms[:, t:t + 1], ACT.Sqrt).then_inc(rt_done, 1)
                for h in range(2):
                    act.wait_ge(turned, 2 * t + h + 1)
                    if t >= 2:
                        act.wait_ge(logit, t - 1)
                    act.activation(xT[:, t % 2, 4 * h:4 * h + 4, :], v.bank[(2 * t + h) % 4].rearrange("p (c t) -> p c t", c=4),
                                   ACT.Copy).then_inc(xT_done, 1)
            act.wait_ge(x_exp, 1)
            act.activation(B[1][:, 0:NT * NG], B[0][:, 0:NT * NG], ACT.Exp).then_inc(exped, 1)
            act.wait_ge(x_exp, 2)
            act.activation(B[11][:, 0:NT], B[10][:, 0:NT], ACT.Exp).then_inc(exped, 1)

        @block.vector
        def _(dve):
            done, then = chain(dve, link)
            dve.memset(ones[:, :], 1.0).then_inc(ones_set, 1)
            dve.wait_ge(const_in, 128)
            for t in range(NT):
                col = slice(t, t + 1)
                dve.wait_ge(sq_done, t + 1)
                dve.tensor_scalar(ms[:, col], ss[:, col], 1.0 / D, EPS, ALU.mult, ALU.add).then_inc(ms_done, 1)
                dve.wait_ge(rt_done, t + 1)
                inverse_root(dve, then, rstd[:, col], ms[:, col], rt[:, col], tmp[:, col])
                if t >= 2:
                    dve.wait_ge(turned, 2 * (t - 1))
                    dve.wait_ge(store_n[t % 2], 16 * (t // 2))
                dve.scalar_tensor_tensor(out=xs[:, t % 2, :], in0=v.xres[:, t, :], scalar=rstd[:, col], in1=gain_b[:, :],
                                         op0=ALU.mult, op1=ALU.mult).then_inc(xs_done, 1)
                if t:
                    dve.wait_ge(logit, t)
                    then(dve.tensor_tensor(lg[:, t - 1, :], v.bank[4 + (t - 1) % 2][:, 0:NG + NE], bias[:, :], ALU.add))
            dve.wait_ge(logit, NT)
            then(dve.tensor_tensor(lg[:, NT - 1, :], v.bank[4 + (NT - 1) % 2][:, 0:NG + NE], bias[:, :], ALU.add))

            def grid(x, n):
                return x[:, 0:NT * n].rearrange("p (t n) -> p t n", n=n)

            def over(x, n):
                return x[:, 0:NT].unsqueeze(2).broadcast_to([P, NT, n])

            def row(x, n):
                return x.unsqueeze(1).broadcast_to([P, NT, n])

            def first_max(values, n, order, hot, top, t1, t2):
                then(dve.tensor_reduce(top, values, AX.X, ALU.max))
                then(dve.tensor_tensor(t1, values, top.unsqueeze(2).broadcast_to([P, NT, n]), ALU.is_equal))
                then(dve.tensor_tensor(t1, t1, row(order, n), ALU.mult))
                then(dve.tensor_reduce(t2, t1, AX.X, ALU.max))
                then(dve.tensor_tensor(hot, t1, t2.unsqueeze(2).broadcast_to([P, NT, n]), ALU.is_equal))

            G, E = lg[:, :, 0:NG], lg[:, :, NG:].rearrange("p t (g e) -> p t g e", g=NG)
            g_hot, g_top, g_w = grid(B[2], NG), B[3][:, 0:NT], B[4][:, 0:NT]
            first_max(G, NG, f_group, g_hot, g_top, grid(B[5], NG), B[6][:, 0:NT])
            dve.tensor_tensor(grid(B[0], NG), G, g_top.unsqueeze(2).broadcast_to([P, NT, NG]), ALU.subtract).then_inc(x_exp, 1)
            dve.wait_ge(exped, 1)
            then(dve.tensor_reduce(g_w, grid(B[1], NG), AX.X, ALU.add))
            then(dve.reciprocal(g_w, g_w))
            four = "p (t g e) -> p t g e"
            masked = A[0][:, :].rearrange(four, t=NT, g=NG)
            eg = grid(B[7], NE8)
            for t in range(NT):
                done(dve.tensor_tensor(masked[:, t], E[:, t], g_hot[:, t].unsqueeze(2).broadcast_to([P, NG, NE8]), ALU.mult))
            dve.wait_ge(link, done(dve.memset(tmp[:, :], 0.0)))
            then(dve.tensor_reduce(eg, masked.rearrange("p t g e -> p t e g"), AX.X, ALU.add))
            hot = [grid(B[8], NE8), grid(B[9], NE8)]
            first_max(eg, NE8, f_expert, hot[0], ss[:, :], grid(B[5], NE8), B[6][:, 0:NT])
            then(dve.scalar_tensor_tensor(out=eg, in0=hot[0], scalar=-3e38, in1=eg, op0=ALU.mult, op1=ALU.add))
            first_max(eg, NE8, f_expert, hot[1], ms[:, :], grid(B[5], NE8), B[6][:, 0:NT])
            dve.tensor_tensor(B[10][:, 0:NT], ms[:, :], ss[:, :], ALU.subtract).then_inc(x_exp, 1)
            dve.wait_ge(exped, 2)
            then(dve.tensor_scalar(rt[:, :], B[11][:, 0:NT], 1.0, None, ALU.add))
            then(dve.reciprocal(rt[:, :], rt[:, :]))
            then(dve.tensor_tensor(v.e_w[:, 0, :], rt[:, :], g_w, ALU.mult))
            then(dve.tensor_tensor(v.e_w[:, 1, :], v.e_w[:, 0, :], B[11][:, 0:NT], ALU.mult))
            pick = [A[1], A[2]]
            for k in range(TOPK):
                for t in range(NT):
                    done(dve.tensor_tensor(pick[k][:, :].rearrange(four, t=NT, g=NG)[:, t], hot[k][:, t].unsqueeze(1).broadcast_to([P, NG, NE8]),
                                           g_hot[:, t].unsqueeze(2).broadcast_to([P, NG, NE8]), ALU.mult))
            dve.wait_ge(link, done(dve.memset(tmp[:, :], 0.0)))
            dve.tensor_tensor(A[3][:, :], A[1][:, :], A[2][:, :], ALU.add).then_inc(chosen, 1)
            dve.wait_ge(ranked, 1)
            count, blocks, upto = A[4][:, 0:NE], A[5][:, 0:NE], A[6][:, 0:NE]
            then(dve.tensor_copy(count, v.bank[1][:, 0:NE]))
            c3 = cmp_[:, 0:NE * NT].rearrange("p (e n) -> p e n", n=NT)
            then(dve.tensor_tensor(c3, count.unsqueeze(2).broadcast_to([P, NE, NT]), f_tile.unsqueeze(1).broadcast_to([P, NE, NT]), ALU.is_gt))
            then(dve.tensor_reduce(blocks, c3, AX.X, ALU.add))
            then(dve.tensor_tensor_scan(upto, ones[:, 0:NE], blocks, 0.0, ALU.mult, ALU.add))
            c3 = cmp_[0:1, :].rearrange("p (b e) -> p b e", e=NE)
            then(dve.tensor_tensor(c3, upto[0:1].unsqueeze(1).broadcast_to([1, NSLOT_BLK, NE]),
                                   f_block[0:1].unsqueeze(2).broadcast_to([1, NSLOT_BLK, NE]), ALU.is_le))
            then(dve.tensor_reduce(A[7][0:1, 0:NSLOT_BLK], c3, AX.X, ALU.add))
            then(dve.tensor_scalar(v.blk_e[:, :], A[7][0:1, 0:NSLOT_BLK], float(NE - 1), None, ALU.min))
            then(dve.tensor_scalar(A[8][0:1, 0:NBLK // 2], f_turn[0:1], upto[0:1, NE - 1:NE], None, ALU.is_lt))
            then(dve.tensor_reduce(A[9][0:1, 0:1], A[8][0:1, 0:NBLK // 2], AX.X, ALU.add))
            then(dve.tensor_copy(v.turns[:, 0:1], A[9][0:1, 0:1]))
            then(dve.tensor_tensor(blocks, upto, blocks, ALU.subtract))
            then(dve.tensor_scalar(blocks, blocks, float(P), None, ALU.mult))
            r3 = v.bank[0][:, 0:NT * NE].rearrange("p (t e) -> p t e", e=NE)
            s3 = A[10][:, :].rearrange("p (t e) -> p t e", e=NE)
            then(dve.tensor_tensor(s3, r3, blocks.unsqueeze(1).broadcast_to([P, NT, NE]), ALU.add))
            for k in range(TOPK):
                p3 = pick[k][:, :].rearrange("p (t e) -> p t e", e=NE)
                then(dve.tensor_tensor(p3, p3, s3, ALU.mult))
                then(dve.tensor_reduce(B[k][:, 0:NT], p3, AX.X, ALU.add))
                ins = dve.tensor_copy(v.dest[:, k, :], B[k][:, 0:NT])
                if k:
                    ins.then_inc(placed, 1)
                else:
                    then(ins)

        @block.tensor
        def _(pe):
            pe.wait_ge(const_in, 128)
            for t in range(NT):
                pe.wait_ge(xs_done, t + 1)
                for h in range(2):
                    n = 2 * t + h
                    if n >= 4:
                        pe.wait_ge(xT_done, n - 3)
                    for c in range(4):
                        k = 4 * h + c
                        mm = pe.transpose(v.bank[n % 4][:, c * P:(c + 1) * P], xs[:, t % 2, k * P:(k + 1) * P], v.ident[:, :])
                    mm.then_inc(turned, 1)
                pe.wait_ge(xT_done, 2 * t + 2)
                if t >= 2:
                    pe.wait_ge(link, logit_links(t - 2))
                for k in range(ND):
                    mm = pe.matmul(v.bank[4 + t % 2][:, 0:NG + NE], xT[:, t % 2, k, :], wr[:, k, :], start=(k == 0), stop=(k == ND - 1))
                mm.then_inc(logit, 1)
            pe.wait_ge(chosen, 1)
            pe.wait_ge(ones_set, 1)
            M = A[3][:, :].rearrange("p (t e) -> p t e", e=NE)
            for t in range(NT):
                out = v.bank[0][:, t * NE:(t + 1) * NE]
                for j in range(t):
                    pe.matmul(out, ones[:, :], M[:, j, :], start=(j == 0), stop=False)
                pe.matmul(out, upper[:, :], M[:, t, :], start=(t == 0), stop=True)
            for j in range(NT):
                mm = pe.matmul(v.bank[1][:, 0:NE], ones[:, :], M[:, j, :], start=(j == 0), stop=(j == NT - 1))
            mm.then_inc(ranked, 1)


def logit_links(t):
    return 5 * (t + 2) + t + 1


def experts_stage(v):
    nc, at, sem, d = v.nc, v.mem.at, v.sem, v.d
    w1 = [at(f"w1_{i}", ACTS + 48 * i, [P, ND, FF]) for i in range(2)]
    w3 = [at(f"w3_{i}", ACTS + 48 * i + 16, [P, ND, FF]) for i in range(2)]
    w2 = [at(f"w2_{i}", ACTS + 48 * i + 32, [P, FF // P, D]) for i in range(2)]
    o = ACTS + 96
    idx = [at(f"idx{i}", o + 46 + 0.25 * i, [P, 2], I32) for i in range(2)]
    xg = [at(f"xg{i}", o + 4 * i, [P, D]) for i in range(2)]
    xT = [at(f"xT{i}", o + 8 + 4 * i, [P, ND, P]) for i in range(2)]
    act_h = at("silu", o + 16, [P, FF])
    hid = at("hid", o + 18, [P, FF])
    hidT = at("hidT", o + 20, [P, FF // P, P])
    y = [at(f"y{i}", o + 24 + 4 * i, [P, D]) for i in range(2)]
    pair_xT, h1, h3, b_hT, pair_y = v.pair[0], v.bank[2], v.bank[3], v.bank[4], v.pair[3]

    w13_in, w2_in = [sem(f"w13_in{i}") for i in range(2)], [sem(f"w2_in{i}") for i in range(2)]
    x_in, y_out, y_stored = [sem(f"x_in{i}") for i in range(2)], sem("y_out"), sem("y_stored")
    idx_set, x_turned, xT_done = sem("idx_set"), sem("x_turned"), sem("xT_done")
    h_done, silu_done, hid_done, h_turned, hT_done = (sem(n) for n in ("h_done", "silu_done", "hid_done", "h_turned", "hT_done"))
    y_done, y_read = sem("y_done"), sem("y_read")
    idx_seen, y_seen = sem("idx_seen"), sem("y_seen")

    def turns(eng):
        return eng.value_load(v.turns[0:1, 0:1], min_val=1, max_val=NBLK // 2)

    with nc.Block() as block:
        @block.sync
        def _(sp):
            n_turns = turns(sp)
            with sp.Fori(0, n_turns) as i:
                for p in range(2):
                    e = sp.value_load(v.blk_e[0:1, bass.ds(2 * i + p, 1)], min_val=0, max_val=NE - 1)
                    sp.wait_ge(h_done, 2 * i + p + 1)
                    for w, src in ((w1[p], d["w1"]), (w3[p], d["w3"])):
                        sp.dma_start(w[:, :, :], src[bass.ds(e, 1), :, :].rearrange("o (k p) n -> p (o k) n", p=P)).then_inc(w13_in[p], 16)
                    sp.wait_ge(y_done, 2 * i + p + 1)
                    sp.dma_start(w2[p][:, :, :], d["w2"][bass.ds(e, 1), :, :].rearrange("o (k p) n -> p (o k) n", p=P)).then_inc(w2_in[p], 16)

        @block.gpsimd
        def _(pool):
            n_turns = turns(pool)

            def gather(p, slot, count):
                pool.tensor_copy(idx[p][:, :], slot).then_inc(idx_set, 1)
                pool.wait_ge(idx_set, count)
                pool.sem_inc(idx_seen, 1)
                pool.indirect_dma_start(xg[p][:, :], None, d["xn"], bass.IndirectOffsetOnAxis(ap=idx[p][:, 0:1], axis=0)).then_inc(x_in[p], 16)

            pool.sem_inc(y_stored, 2)
            gather(0, v.slots[:, 0, :], 1)
            with pool.Fori(0, n_turns) as i:
                for p in range(2):
                    pool.wait_ge(x_turned, 2 * i + p + 1)
                    gather(1 - p, v.slots[:, bass.ds(2 * i + p + 1, 1), :].rearrange("p o c -> p (o c)"), 2 * i + p + 2)
                    pool.wait_ge(y_read, 1 + 2 * i + p + 1)
                    pool.sem_inc(y_seen, 1)
                    pool.indirect_dma_start(d["y"], bass.IndirectOffsetOnAxis(ap=idx[p][:, 1:2], axis=0), y[p][:, :], None).then_inc(y_out, 16)
                    pool.wait_ge(y_out, 16 * (2 * i + p + 1))
                    pool.sem_inc(y_stored, 1)

        @block.scalar
        def _(act):
            n_turns = turns(act)
            with act.Fori(0, n_turns) as i:
                for p in range(2):
                    b = 2 * i + p
                    act.wait_ge(h_done, 2 + b + 1)
                    act.activation(act_h[:, :], h1, ACT.Silu).then_inc(silu_done, 1)
                    act.wait_ge(h_turned, b + 1)
                    act.activation(hidT[:, :, :], b_hT.rearrange("p (k t) -> p k t", t=P), ACT.Copy).then_inc(hT_done, 1)

        @block.vector
        def _(dve):
            n_turns = turns(dve)

            def copy_xT(p, count):
                dve.wait_ge(x_turned, count)
                dve.tensor_copy(xT[p][:, :, :], pair_xT[:, :].rearrange("p (k t) -> p k t", t=P)).then_inc(xT_done, 1)

            dve.sem_inc(hid_done, 1)
            dve.sem_inc(y_read, 1)
            copy_xT(0, 1)
            with dve.Fori(0, n_turns) as i:
                for p in range(2):
                    b = 2 * i + p
                    dve.wait_ge(silu_done, b + 1)
                    dve.tensor_tensor(hid[:, :], act_h[:, :], h3, ALU.mult).then_inc(hid_done, 1)
                    copy_xT(1 - p, b + 2)
                    dve.wait_ge(y_done, 2 + b + 1)
                    dve.wait_ge(y_stored, b + 1)
                    dve.tensor_copy(y[p][:, :], pair_y[:, :]).then_inc(y_read, 1)

        @block.tensor
        def _(pe):
            n_turns = turns(pe)
            pe.sem_inc(h_done, 2)
            pe.sem_inc(y_done, 2)

            def turn_x(p, arrived):
                pe.wait_ge(x_in[p], arrived)
                for k in range(ND):
                    mm = pe.transpose(pair_xT[:, k * P:(k + 1) * P], xg[p][:, k * P:(k + 1) * P], v.ident[:, :])
                mm.then_inc(x_turned, 1)

            turn_x(0, 16)
            with pe.Fori(0, n_turns) as i:
                for p in range(2):
                    b = 2 * i + p
                    pe.wait_ge(xT_done, b + 1)
                    pe.wait_ge(w13_in[p], 32 * (i + 1))
                    pe.wait_ge(hid_done, 1 + b)
                    for out, w in ((h1, w1[p]), (h3, w3[p])):
                        for k in range(ND):
                            mm = pe.matmul(out, xT[p][:, k, :], w[:, k, :], start=(k == 0), stop=(k == ND - 1))
                    mm.then_inc(h_done, 1)
                    turn_x(1 - p, 16 * (i + 1) + 16 * p)
                    pe.wait_ge(hid_done, 1 + b + 1)
                    for k in range(FF // P):
                        mm = pe.transpose(b_hT[:, k * P:(k + 1) * P], hid[:, k * P:(k + 1) * P], v.ident[:, :])
                    mm.then_inc(h_turned, 1)
                    pe.wait_ge(hT_done, b + 1)
                    pe.wait_ge(w2_in[p], 16 * (i + 1))
                    pe.wait_ge(y_read, 1 + b)
                    for c in range(D // N):
                        for k in range(FF // P):
                            mm = pe.matmul(pair_y[:, c * N:(c + 1) * N], hidT[:, k, :], w2[p][:, k, c * N:(c + 1) * N],
                                           start=(k == 0), stop=(k == FF // P - 1))
                    mm.then_inc(y_done, 1)


def combine_stage(v):
    nc, at, sem, d = v.nc, v.mem.at, v.sem, v.d
    SLOTS = 3
    y = at("y_rows", ACTS, [P, SLOTS, TOPK, D])
    t1 = at("t1", ACTS + 32, [P, 2, D])
    y_in, link, added = [sem(f"y_in{i}") for i in range(SLOTS)], sem("dve_link"), sem("added")
    with nc.Block() as block:
        @block.sync
        def _(sp):
            rows_of = d["y"].rearrange("(k t p) c -> t p k c", p=P, t=NT)
            for t in range(NT):
                if t >= SLOTS:
                    sp.wait_ge(added, t - SLOTS + 1)
                sp.dma_start(y[:, t % SLOTS, :, :], rows_of[t, :, 0:TOPK, :]).then_inc(y_in[t % SLOTS], 16)

        @block.vector
        def _(dve):
            done, then = chain(dve, link)
            for t in range(NT):
                s = t % SLOTS
                dve.wait_ge(y_in[s], 16 * (t // SLOTS + 1))
                then(dve.tensor_scalar(t1[:, t % 2, :], y[:, s, 0, :], v.e_w[:, 0, t:t + 1], None, ALU.mult))
                then(dve.scalar_tensor_tensor(out=t1[:, t % 2, :], in0=y[:, s, 1, :], scalar=v.e_w[:, 1, t:t + 1], in1=t1[:, t % 2, :],
                                              op0=ALU.mult, op1=ALU.add))
                dve.tensor_tensor(v.xres[:, t, :], v.xres[:, t, :], t1[:, t % 2, :], ALU.add).then_inc(added, 1)


QA_W, KVA_W, B_W = AH * HD, 2 * AKV * HD, BH * HD
COL2 = dict(zip(("qa", "kva", "qb", "kb", "vb", "f"), np.cumsum([0, QA_W, KVA_W, B_W, B_W, B_W]).tolist()))
KVF_W = KVA_W + BH


def block2_tensors(v):
    at = v.mem.at
    v.qa = at("qa", FREE, [P, NT, QA_W])
    v.kvf = at("kvf", FREE + 16, [P, NT, KVF_W])
    v.vb = at("vb", FREE + 24.5, [P, NT, B_W])
    v.qb = at("qb_aug", FREE + 40.5, [P, NT, BH, BAUG])
    v.kb = at("kb_aug", FREE + 59, [P, NT, BH, BAUG])
    v.log_f = at("log_f", FREE + 77.5, [P, NT, BH])


def project2_stage(v):
    nc, at, sem, d = v.nc, v.mem.at, v.sem, v.d
    block2_tensors(v)
    act_ops, w = (v.act_hi, v.act_lo), d["w_in_2"]
    order = ["kva", "qa", "qb", "kb", "vb"]
    index = {name: g for g, name in enumerate(order)}
    tiles = [Tile("nat", [(rows(w, k, COL2["kva"], COL2["kva"] + KVA_W), 0, KVA_W), (rows(w, k, COL2["f"], COL2["f"] + BH), KVA_W, KVF_W)],
                  KVF_W, act_ops, k, k == 0, k == ND - 1) for k in range(ND)]
    for name in order[1:]:
        tiles += group("nat", w, ND, COL2[name], COL2[name] + N, act_ops)

    gains = at("gains2", CONST + 3, [P, 4, HD])
    bias = at("b_forget", CONST + 2, [P, BH])
    z, e, u, dif, corr = (at(f"forget{i}", CONST + kb, [P, NT, BH]) for i, kb in enumerate((2.25, 2.5, 2.75, 7, 7.25)))

    def heads_of(name, dst, heads):
        return Heads(v, name, dst, heads, CONST + 4)

    plain = "p (h d) -> p h d"
    heads = {"kva": heads_of("ka", lambda t: v.kvf[:, t, 0:AKV * HD].rearrange(plain, d=HD), AKV),
             "qa": heads_of("qa", lambda t: v.qa[:, t, :].rearrange(plain, d=HD), AH),
             "qb": heads_of("qb", lambda t: v.qb[:, t, :, 0:HD], BH),
             "kb": heads_of("kb", lambda t: v.kb[:, t, :, 0:HD], BH)}
    ready, free, link, tables = sem("bank_ready"), sem("bank_free"), sem("dve_link"), sem("tables")
    e_arg, e_done, u_set, ln_done = sem("e_arg"), sem("e_done"), sem("u_set"), sem("ln_done")

    def load_tables(sp):
        for i, name in enumerate(("k_norm_a_2", "q_norm_a_2", "q_norm_b_2", "k_norm_b_2")):
            sp.dma_start(gains[:, i, :], d[name].broadcast_to([P, HD])).then_inc(tables, 16)
        sp.dma_start(bias[:, :], d["b_forget_2"].broadcast_to([P, BH])).then_inc(tables, 16)

    def forget_exp(act):
        act.wait_ge(e_arg, 1)
        act.activation(e[:, :, :], e[:, :, :], ACT.Exp).then_inc(e_done, 1)

    def forget_ln(act):
        act.wait_ge(u_set, 1)
        act.activation(z[:, :, :], u[:, :, :], ACT.Ln).then_inc(ln_done, 1)

    steps = {8 + 2: [forget_exp], 8 + 3: [forget_ln]}
    for name, h in heads.items():
        steps.setdefault(8 * (index[name] + 1) + (4 if name == "kva" else 6), []).append(h.root)

    def dve_program(dve):
        done, then = chain(dve, link)
        then(dve.memset(v.qb[:, :, :, HD:], 0.0))
        then(dve.memset(v.kb[:, :, :, HD:], 0.0))
        done(dve.memset(v.qb[:, :, :, HD:HD + 1], 1.0))
        done(dve.memset(v.kb[:, :, :, HD + 1:HD + 2], 1.0))
        for t in range(NT):
            then(dve.memset(v.kb[:, t, :, HD + 2 + t:HD + 3 + t], 1.0))
        dve.wait_ge(tables, 80)
        for i in (1, 2):
            then(dve.tensor_scalar(gains[:, i, :], gains[:, i, :], HD ** -0.5, None, ALU.mult))
        g = index["kva"]
        for t in range(NT):
            dve.wait_ge(ready, 8 * g + t + 1)
            dve.tensor_copy(v.kvf[:, t, :], v.bank[t][:, 0:KVF_W]).then_inc(free, 1)
        dve.wait_ge(free, 8 * g + NT)
        then(dve.tensor_tensor(z[:, :, :], v.kvf[:, :, KVA_W:], bias[:, :].unsqueeze(1).broadcast_to([P, NT, BH]), ALU.add))
        dve.scalar_tensor_tensor(out=e[:, :, :], in0=z[:, :, :], scalar=-1.0, in1=z[:, :, :], op0=ALU.mult, op1=ALU.min).then_inc(e_arg, 1)
        then(dve.tensor_scalar(v.log_f[:, :, :], z[:, :, :], 0.0, None, ALU.min))
        dve.wait_ge(e_done, 1)
        dve.tensor_scalar(u[:, :, :], e[:, :, :], 1.0, None, ALU.add).then_inc(u_set, 1)
        dve.wait_ge(u_set, 1)
        then(dve.scalar_tensor_tensor(out=dif[:, :, :], in0=u[:, :, :], scalar=-1.0, in1=e[:, :, :], op0=ALU.add, op1=ALU.subtract))
        then(dve.reciprocal(corr[:, :, :], u[:, :, :]))
        then(dve.tensor_tensor(corr[:, :, :], dif[:, :, :], corr[:, :, :], ALU.mult))
        dve.wait_ge(ln_done, 1)
        then(dve.tensor_tensor(corr[:, :, :], corr[:, :, :], z[:, :, :], ALU.subtract))
        then(dve.tensor_tensor(v.log_f[:, :, :], v.log_f[:, :, :], corr[:, :, :], ALU.add))
        for i, name in enumerate(("kva", "qa", "qb", "kb")):
            h, g = heads[name], index[name]
            for t in range(NT):
                if name != "kva":
                    dve.wait_ge(ready, 8 * g + t + 1)
                    if name == "qa":
                        dve.tensor_copy(v.qa[:, t, :].rearrange("p (a g d) -> p g a d", g=AKV, d=HD),
                                        v.bank[t].rearrange("p (g a d) -> p g a d", g=AKV, d=HD)).then_inc(free, 1)
                    else:
                        h.take(dve, then, v.bank[t][:, :], t, free)
                    dve.wait_ge(free, 8 * g + t + 1)
                h.stat(dve, then, t)
            h.mean(dve)
            h.inverse(dve, then)
            for t in range(NT):
                h.scale(dve, then, t, gains[:, i, :])
        g = index["vb"]
        for t in range(NT):
            dve.wait_ge(ready, 8 * g + t + 1)
            dve.tensor_copy(v.vb[:, t, :], v.bank[t][:, :]).then_inc(free, 1)

    dense_stage(v, tiles, dve_program, steps, sp_before=load_tables, sems=(ready, free))


class ForgetUnit:

    def __init__(self, h, i):
        self.h, self.i, self.window = h, i, False
        self.width, self.exps = (i + 1) * P, 1
        self.blocks = [(j * P, j, 0, j == 0, j == i) for j in range(i + 1)]


class WindowUnit:

    def __init__(self, g, i):
        self.g, self.i, self.window = g, i, True
        self.keys = min(2, i + 1) * P
        self.width, self.exps = self.keys * (AH // AKV), AH // AKV + 1
        first = max(0, i - 1)
        self.blocks = [(a * self.keys + (j - first) * P, j, a, j == first, j == i) for a in range(AH // AKV) for j in range(first, i + 1)]


def attention2_stage(v):
    nc, at, sem, d = v.nc, v.mem.at, v.sem, v.d
    qbT, kbT = at("qbT", ACTS, [P, BH, S]), at("kbT", ACTS + 32, [P, BH, S])
    qaT, kaT = at("qaT", FREE + 40.5, [P, AH // AKV, S]), at("kaT", FREE + 56.5, [P, S])
    probs, aT = at("probs", RINGS, [P, 3, S]), at("probsT", RINGS + 12, [P, 2, S])
    alibi = [at("alibi0", CONST + 4, [P, AH // AKV, 2 * P]), at("alibi1", RINGS + 20, [P, AH // AKV, 2 * P])]
    v.out_a, v.out_b = at("out_a", FREE, [P, NT, QA_W]), at("out_b", FREE + 60.5, [P, NT, B_W])
    small = CONST + 2
    upto, ones = at("upto", small, [P, P]), at("ones", small + 0.5, [P, P])
    sinks = at("sinks", small + 1, [P, AH])
    mraw, nmax, snk, sums, inv = (at(n, small + 1.25 + 0.125 * i, [P, 4, 4]) for i, n in enumerate(("mraw", "nmax", "snk", "sums", "inv")))

    HALF = AH // AKV
    units = []
    for i in range(NT):
        for g in range(AKV):
            units += [ForgetUnit(h, i) for h in range(4 * g, 4 * g + 4)] + [WindowUnit(g, i)]
    n_units = len(units)
    exped_upto = np.cumsum([0] + [u.exps for u in units]).tolist()
    halves = [-(-u.width // N) for u in units]
    high_upto = np.cumsum([0] + [n - 1 for n in halves]).tolist()

    consts, link, cum_ready, columns = sem("consts"), sem("dve_link"), sem("cum_ready"), sem("columns")
    alibi_in, tr_ready, tr_act, tr_dve = sem("alibi_in"), sem("tr_ready"), sem("tr_act"), sem("tr_dve")
    upto_set = sem("upto_set")
    scored, maxed, exped = sem("scored"), sem("maxed"), sem("exped")
    turned_low, turned_high, low_read, high_read = sem("turned_low"), sem("turned_high"), sem("low_read"), sem("high_read")
    weighed, weigh_read = sem("weighed"), sem("weigh_read")

    moves = []
    for t in range(NT):
        ts = slice(t * P, (t + 1) * P)
        for src, dst in ((v.qb, qbT), (v.kb, kbT)):
            for b in range(2):
                moves.append(([(src[:, t, 4 * b + a, :], slice(0, BAUG), a) for a in range(4)], dst[0:BAUG, 4 * b:4 * b + 4, ts], BAUG))
    for t in range(NT):
        moves.append(([(v.qa[:, t, a * P:(a + 1) * P], slice(0, P), a) for a in range(HALF)],
                      qaT[:, :, t * P:(t + 1) * P], P))
    for b in range(2):
        moves.append(([(v.kvf[:, 4 * b + a, 0:P], slice(0, P), a) for a in range(4)],
                      kaT[:, 4 * b * P:4 * (b + 1) * P].rearrange("p (a t) -> p a t", t=P), P))
    TRB = 6

    with nc.Block() as block:
        @block.sync
        def _(sp):
            sp.dma_start(upto[:, :], d["upper"]).then_inc(consts, 16)
            sp.dma_start(sinks[:, :], d["sink_logits_2"].broadcast_to([P, AH])).then_inc(consts, 16)
            for g in range(AKV):
                sp.dma_start(alibi[g][:, :, :], d["alibi"][:, g * HALF:(g + 1) * HALF, :]).then_inc(alibi_in, 16)

        @block.scalar
        def _(act):
            for n, (_, dst, parts) in enumerate(moves):
                if n % 2 == 0:
                    act.wait_ge(tr_ready, n + 1)
                    act.activation(dst, v.bank[n % TRB][0:parts, :].rearrange("p (a t) -> p a t", t=P), ACT.Copy).then_inc(tr_act, 1)

            def turn_out(p):
                act.wait_ge(turned_low, p + 1)
                if p >= 2:
                    act.wait_ge(weighed, p - 1)
                c = min(units[p].width, N)
                act.activation(aT[:, p % 2, :c], v.bank[4][:, :c], ACT.Copy).then_inc(low_read, 1)

            for p, u in enumerate(units):
                act.wait_ge(maxed, p + 1)
                s, q = p % 4, probs[:, p % 3, :]
                if u.window:
                    for a in range(HALF):
                        c = slice(a * u.keys, (a + 1) * u.keys)
                        act.activation(q[:, c], q[:, c], ACT.Exp, bias=nmax[:, s, a:a + 1], accum_out=sums[:, s, a:a + 1]).then_inc(exped, 1)
                    act.activation(snk[:, s, :], snk[:, s, :], ACT.Exp).then_inc(exped, 1)
                else:
                    if p >= 3:
                        act.wait_ge(turned_low, p - 2)
                        if high_upto[p - 2]:
                            act.wait_ge(turned_high, high_upto[p - 2])
                    act.activation(q[:, :u.width], v.pair[p % 2][:, :u.width], ACT.Exp, bias=nmax[:, s, 0:1],
                                   accum_out=sums[:, s, 0:1]).then_inc(exped, 1)
                if p >= 2:
                    turn_out(p - 2)
            for p in (n_units - 2, n_units - 1):
                turn_out(p)

        @block.vector
        def _(dve):
            done, then = chain(dve, link)
            dve.wait_ge(consts, 32)
            done(dve.memset(ones[:, :], 1.0))
            dve.tensor_tensor(upto[:, :], upto[:, :], v.ident[:, :], ALU.add).then_inc(upto_set, 1)
            dve.wait_ge(cum_ready, 1)
            own = v.bank[7][:, 0:NT * BH].rearrange("p (t h) -> p t h", h=BH)
            total = v.bank[7][:, NT * BH:2 * NT * BH].rearrange("p (t h) -> p t h", h=BH)
            done(dve.tensor_copy(v.qb[:, :, :, HD + 1:HD + 2].rearrange("p t h o -> p t (h o)"), own))
            then(dve.tensor_scalar(v.kb[:, :, :, HD:HD + 1].rearrange("p t h o -> p t (h o)"), own, -1.0, None, ALU.mult))
            for i in range(1, NT):
                ins = dve.tensor_tensor(v.qb[:, i, :, HD + 2:HD + 2 + i], v.qb[:, i - 1, :, HD + 2:HD + 2 + i],
                                        total[:, i - 1, :].unsqueeze(2).broadcast_to([P, BH, i]), ALU.add)
                if i < NT - 1:
                    then(ins)
                else:
                    ins.then_inc(columns, 1)
            for n, (_, dst, parts) in enumerate(moves):
                if n % 2:
                    dve.wait_ge(tr_ready, n + 1)
                    dve.tensor_copy(dst, v.bank[n % TRB][0:parts, :].rearrange("p (a t) -> p a t", t=P)).then_inc(tr_dve, 1)

            def turn_out(p):
                if halves[p] < 2:
                    return
                dve.wait_ge(turned_high, high_upto[p + 1])
                if p >= 2:
                    dve.wait_ge(weighed, p - 1)
                c = units[p].width
                dve.tensor_copy(aT[:, p % 2, N:c], v.bank[5][:, :c - N]).then_inc(high_read, 1)

            def out(p):
                u, s = units[p], p % 4
                dve.wait_ge(weighed, p + 1)
                if u.window:
                    then(dve.tensor_tensor(inv[:, s, :], sums[:, s, :], snk[:, s, :], ALU.add))
                    then(dve.reciprocal(inv[:, s, :], inv[:, s, :]))
                    c = u.g * HALF * HD
                    dve.tensor_tensor(v.out_a[:, u.i, c:c + HALF * HD].rearrange("p (a d) -> p a d", d=HD),
                                      v.bank[6 + p % 2][:, 0:HALF * HD].rearrange("p (a d) -> p a d", d=HD),
                                      inv[:, s, :].unsqueeze(2).broadcast_to([P, HALF, HD]), ALU.mult).then_inc(weigh_read, 1)
                else:
                    then(dve.reciprocal(inv[:, s, 0:1], sums[:, s, 0:1]))
                    dve.tensor_scalar(v.out_b[:, u.i, u.h * HD:(u.h + 1) * HD], v.bank[6 + p % 2][:, 0:HD], inv[:, s, 0:1], None,
                                      ALU.mult).then_inc(weigh_read, 1)

            dve.wait_ge(alibi_in, 32)
            for p, u in enumerate(units):
                dve.wait_ge(scored, p + 1)
                s, q = p % 4, probs[:, p % 3, :]
                if u.window:
                    if p >= 3:
                        dve.wait_ge(turned_low, p - 2)
                        if high_upto[p - 2]:
                            dve.wait_ge(turned_high, high_upto[p - 2])
                    sink = sinks[:, u.g * HALF:(u.g + 1) * HALF]
                    for a in range(HALF):
                        c = slice(a * u.keys, (a + 1) * u.keys)
                        ins = dve.tensor_tensor_reduce(q[:, c], v.pair[p % 2][:, c], alibi[u.g][:, a, 2 * P - u.keys:], 1.0, -3.0e38,
                                                       ALU.add, ALU.max, mraw[:, s, a:a + 1])
                        (done if a < HALF - 1 else then)(ins)
                    then(dve.tensor_tensor(mraw[:, s, :], mraw[:, s, :], sink, ALU.max))
                    then(dve.tensor_scalar(nmax[:, s, :], mraw[:, s, :], -1.0, None, ALU.mult))
                    dve.tensor_tensor(snk[:, s, :], sink, nmax[:, s, :], ALU.add).then_inc(maxed, 1)
                else:
                    dve.tensor_reduce(nmax[:, s, 0:1], v.pair[p % 2][:, :u.width], AX.X, ALU.max, negate=True).then_inc(maxed, 1)
                if p >= 2:
                    turn_out(p - 2)
                if p >= 3:
                    out(p - 3)
            turn_out(n_units - 2)
            out(n_units - 3)
            turn_out(n_units - 1)
            out(n_units - 2)
            out(n_units - 1)

        @block.tensor
        def _(pe):
            pe.wait_ge(upto_set, 1)
            logs = v.log_f[:, :, :].rearrange("p t h -> p (t h)")
            pe.matmul(v.bank[7][:, 0:NT * BH], upto[:, :], logs, start=True, stop=True)
            pe.matmul(v.bank[7][:, NT * BH:2 * NT * BH], ones[:, :], logs, start=True, stop=True).then_inc(cum_ready, 1)
            pe.wait_ge(columns, 1)
            for n, (blocks, _, _) in enumerate(moves):
                if n >= TRB:
                    pe.wait_ge(tr_dve if n % 2 else tr_act, (n - TRB) // 2 + 1)
                for src, r, a in blocks:
                    mm = pe.transpose(v.bank[n % TRB][r, a * P:(a + 1) * P], src, v.ident[:, :])
                mm.then_inc(tr_ready, 1)
            pe.wait_ge(tr_act, (len(moves) + 1) // 2)
            pe.wait_ge(tr_dve, len(moves) // 2)

            def scores(p):
                u = units[p]
                if p >= 2:
                    pe.wait_ge(exped, exped_upto[p - 1])
                ts, pair = slice(u.i * P, (u.i + 1) * P), v.pair[p % 2]
                if u.window:
                    r = slice(u.g * HD, (u.g + 1) * HD)
                    for a in range(HALF):
                        mm = pe.matmul(pair[:, a * u.keys:(a + 1) * u.keys], qaT[r, a, ts], kaT[r, (u.i + 1) * P - u.keys:(u.i + 1) * P],
                                       start=True, stop=True)
                else:
                    mm = score_products(pe, v, pair, qbT[0:BAUG, u.h, ts], kbT[0:BAUG, u.h, :], u.width, True)
                mm.then_inc(scored, 1)

            def turn(p):
                u = units[p]
                pe.wait_ge(exped, exped_upto[p + 1])
                if p:
                    pe.wait_ge(low_read, p)
                for c in range(0, min(u.width, N), P):
                    mm = pe.transpose(v.bank[4][:, c:c + P], probs[:, p % 3, c:c + P], v.ident[:, :])
                mm.then_inc(turned_low, 1)
                if halves[p] > 1:
                    if high_upto[p]:
                        pe.wait_ge(high_read, high_upto[p])
                    for c in range(N, u.width, P):
                        mm = pe.transpose(v.bank[5][:, c - N:c - N + P], probs[:, p % 3, c:c + P], v.ident[:, :])
                    mm.then_inc(turned_high, 1)

            def weigh(p):
                u = units[p]
                pe.wait_ge(low_read, p + 1)
                if high_upto[p + 1]:
                    pe.wait_ge(high_read, high_upto[p + 1])
                if p >= 2:
                    pe.wait_ge(weigh_read, p - 1)
                for c, j, a, first, last in u.blocks:
                    if u.window:
                        vals = v.kvf[:, j, (AKV + u.g) * HD:(AKV + u.g + 1) * HD]
                    else:
                        vals = v.vb[:, j, u.h * HD:(u.h + 1) * HD]
                    mm = pe.matmul(v.bank[6 + p % 2][:, a * HD:(a + 1) * HD], aT[:, p % 2, c:c + P], vals, start=first, stop=last)
                mm.then_inc(weighed, 1)

            for p in range(n_units):
                scores(p)
                if p >= 2:
                    turn(p - 2)
                if p >= 3:
                    weigh(p - 3)
            turn(n_units - 2)
            weigh(n_units - 3)
            turn(n_units - 1)
            weigh(n_units - 2)
            weigh(n_units - 1)


def turn_mixers2_stage(v):
    def chunk(t, k):
        return (v.out_a if k < 4 else v.out_b)[:, t, k % 4 * P:(k % 4 + 1) * P]
    turn_rows_stage(v, chunk)


def output2_stage(v):
    act = (v.act_hi, v.act_lo)
    tiles = sum((group("nat", v.d["w_out_2"], ND, c, c + N, act) for c in (0, N)), [])
    add_rows_stage(v, tiles, (0, N))


def mlp_stage(v):
    nc, at, sem, d = v.nc, v.mem.at, v.sem, v.d
    hid = (at("hid_hi", FREE, [P, ND, S], F32R), at("hid_lo", FREE + 32, [P, ND, S], F32R))
    SLOTS = 7
    sq = at("hid", FREE + 64, [P, SLOTS, N])
    act_ops = (v.act_hi, v.act_lo)
    PARTS = DFF // D
    tiles = []
    for c in range(PARTS):
        for g in range(2):
            tiles += group("tr", d["w_up_2"], ND, c * D + g * N, c * D + (g + 1) * N, act_ops)
        for g in range(2):
            tiles += group("nat", d["w_down_2"][c * D:(c + 1) * D, :], ND, g * N, (g + 1) * N, hid)
    ready, free = sem("bank_ready"), sem("bank_free")
    squared, hi_done, lo_done, stored = sem("squared"), sem("hid_hi_done"), sem("hid_lo_done"), sem("stored")
    act_steps = {}

    def place(i):
        return i % 16 // 2, slice(i % 2 * N, i % 2 * N + N)

    def up_part(c, g):
        def run(act):
            def relu(u):
                i = 16 * c + 8 * g + u
                act.wait_ge(ready, 32 * c + 8 * g + u + 1)
                if i >= SLOTS:
                    act.wait_ge(lo_done, i - SLOTS + 1)
                act.activation(sq[:, i % SLOTS, :], v.bank[u][:, :], ACT.Relu).then_inc(free, 1)

            def high(u):
                i = 16 * c + 8 * g + u
                k, t = place(i)
                act.wait_ge(squared, i + 1)
                act.activation(hid[0][:, k, t], sq[:, i % SLOTS, :], ACT.Copy).then_inc(hi_done, 1)

            for u in range(8):
                relu(u)
                if u >= 4:
                    high(u - 4)
            for u in range(4, 8):
                high(u)
        return run

    for c in range(PARTS):
        for g in range(2):
            act_steps[32 * c + 8 * (g + 1) + 1] = [up_part(c, g)]
    for c in range(PARTS):
        for k in range(ND):
            tiles[32 * c + 16 + k].after = (lo_done, 16 * c + 2 * k + 2)

    def dve_program(dve):
        def low(i):
            k, t = place(i)
            dve.wait_ge(hi_done, i + 1)
            dve.tensor_tensor(hid[1][:, k, t], sq[:, i % SLOTS, :], hid[0][:, k, t].bitcast(F32), ALU.subtract).then_inc(lo_done, 1)

        for c in range(PARTS):
            for g in range(2):
                for u in range(8):
                    i = 16 * c + 8 * g + u
                    dve.wait_ge(free, 32 * c + 8 * g + u + 1)
                    x = sq[:, i % SLOTS, :]
                    dve.tensor_tensor(x, x, x, ALU.mult).then_inc(squared, 1)
                    if u >= 4:
                        low(i - 4)
                for u in range(4, 8):
                    low(16 * c + 8 * g + u)
            for g in range(2):
                for t in range(NT):
                    dve.wait_ge(ready, 32 * c + 16 + 8 * g + t + 1)
                    x = v.xres[:, t, g * N:(g + 1) * N]
                    dve.tensor_tensor(x, v.bank[t], x, ALU.add).then_inc(free, 1)

    def store(act):
        for g in range(2):
            for t in range(NT):
                act.wait_ge(free, 32 * (PARTS - 1) + 16 + 8 * g + t + 1)
                act.dma_start(d["out"][t * P:(t + 1) * P, g * N:(g + 1) * N], v.xres[:, t, g * N:(g + 1) * N]).then_inc(stored, 16)
        act.wait_ge(stored, 16 * 2 * NT)

    dense_stage(v, tiles, dve_program, act_steps, act_after=store, sems=(ready, free))


def constants_stage(v):
    nc, d = v.nc, v.d
    loaded, made = v.sem("constants"), v.sem("constants_bf")
    with nc.Block() as block:
        @block.sync
        def _(sp):
            sp.dma_start(v.ident[:, :], d["ident"]).then_inc(loaded, 16)
            sp.dma_start(v.mask_f[:, :], d["mask"]).then_inc(loaded, 16)

        @block.vector
        def _(dve):
            dve.wait_ge(loaded, 32)
            dve.tensor_copy(v.ident_bf[:, :], v.ident[:, :]).then_inc(made, 1)
            dve.tensor_copy(v.mask_bf[:, :], v.mask_f[:, :]).then_inc(made, 1)


def program(nc, dram, out, until=99, dump=None):
    with ExitStack() as ctx:
        d = dict(dram)
        for name, shape, dt in (("gateT", (2, ND, P, S), F32), ("hog", (S, HG_W), F32), ("xn", (S, D), F32),
                                ("slot_table", (NSLOT_BLK * P, 2), I32), ("y", ((TOPK + 1) * S, D), F32)):
            d[name] = nc.dram_tensor(f"scratch_{name}", shape, dt).ap()
        d["out"] = out
        v = Env(nc, ctx, d)
        constants_stage(v)
        norm_stage(v, d["norm_mix"], load_from=d["x"])
        block1_tensors(v)
        stages = [project1_stage, hgrn_stage]
        stages += [globals_stage for globals_stage in MORE]
        for n, stage in enumerate(stages):
            if n < until:
                stage(v)
                if len(v.sems) > 80:
                    v.recycle_sems()
        if dump:
            dump(v)


def norm_attention2(v):
    norm_stage(v, v.d["attn_norm_g_2"])


def norm_mlp2(v):
    norm_stage(v, v.d["mlp_norm_g_2"])


MORE = [diff_attention_stage, turn_mixers_stage, branch_stage, output1_stage, router_stage, experts_stage, combine_stage,
        norm_attention2, project2_stage, attention2_stage, turn_mixers2_stage, output2_stage, norm_mlp2, mlp_stage]


def constants():
    i = np.arange(P)
    half = DA_D // 2
    inv = (10000.0 ** (-np.arange(half) / half)).astype(np.float32)
    ang = (np.arange(S, dtype=np.float32)[:, None] * inv[None, :]).astype(np.float64)
    keep = np.ones((1, S), np.float32)
    keep[0, ::CHUNK] = 0.0
    slopes = np.exp2(-(8.0 / AH) * (np.arange(AH, dtype=np.float32) + 1.0)).astype(np.float32)
    dist = (P + i)[:, None] - np.arange(2 * P)[None, :]
    band = (dist >= 0) & (dist < P)
    alibi = np.where(band[None], -slopes[:, None, None] * dist[None].astype(np.float32), np.float32(NEG))
    token = np.arange(NT)[None, :] * P + i[:, None]
    slot = np.arange(NSLOT_BLK * P)
    return {
        "ident": np.eye(P, dtype=np.float32),
        "upper": (i[:, None] < i[None, :]).astype(np.float32),
        "rope_cos": np.cos(ang).astype(np.float32), "rope_sin": np.sin(ang).astype(np.float32),
        "chunk_keep": keep,
        "causal_st": ((i % CHUNK)[:, None] <= np.arange(CHUNK)[None, :]).astype(np.int32),
        "mask": np.where(i[None, :] <= i[:, None], 0.0, NEG).astype(np.float32),
        "alibi": np.ascontiguousarray(alibi.transpose(1, 0, 2)).astype(np.float32),
        "token_rows": np.ascontiguousarray(np.stack(np.broadcast_arrays(token[:, None, :], token[:, None, :] + S * np.arange(TOPK)[None, :, None]),
                                                    axis=-1)).astype(np.int32),
        "slot_init": np.stack([0 * slot, TOPK * S + slot % (2 * P)], axis=-1).astype(np.int32),
        "firsts": np.concatenate([np.arange(NG, 0, -1), np.arange(NE8, 0, -1), np.arange(0, NSLOT_BLK),
                                  np.arange(NT) * P, 2 * np.arange(NBLK // 2)]).astype(np.float32)[None, :],
    }


_ROWS = ("norm_mix", "hg_out_norm", "da_q_norm", "da_k_norm", "da_out_norm", "norm_moe", "b_router_group", "b_router_expert",
         "attn_norm_g_2", "b_forget_2", "q_norm_a_2", "k_norm_a_2", "sink_logits_2", "q_norm_b_2", "k_norm_b_2", "mlp_norm_g_2")


def layout(inputs):
    out = {}
    for name, a in inputs.items():
        a = np.asarray(a)
        if name in _ROWS:
            a = a.reshape(1, -1)
        elif name not in ("hg_lb",) and a.shape[0] == 1:
            a = a.reshape(a.shape[1:])
        out[name] = np.ascontiguousarray(a)
    out.update(constants())
    return out


def kernel(**inputs):
    from concourse import bacc
    from concourse.bass_utils import run_bass_kernel_spmd

    arrays = layout(inputs)
    nc = bacc.Bacc("TRN2", target_bir_lowering=False, num_devices=1)
    dram = {name: nc.dram_tensor(f"in_{name}", a.shape, mybir.dt.from_np(a.dtype), kind="ExternalInput").ap()
            for name, a in arrays.items()}
    out = nc.dram_tensor("out", (S, D), F32, kind="ExternalOutput").ap()
    program(nc, dram, out)
    got = run_bass_kernel_spmd(nc, [{f"in_{name}": a for name, a in arrays.items()}], core_ids=[0])
    return got.results[0]["out"].reshape(1, S, D)
```

```python
from contextlib import ExitStack
import math

import numpy as np
import concourse.bass as bass
import concourse.mybir as mybir
from concourse.alu_op_type import AluOpType as ALU

ACT = mybir.ActivationFunctionType
AX = mybir.AxisListType
F32, F32R, BF16, I32 = mybir.dt.float32, mybir.dt.float32r, mybir.dt.bfloat16, mybir.dt.int32

P = 128
S, D = 1024, 1024
NT, ND = S // P, D // P
N = 512
EPS = 1e-6
KB = 1024

HG_H, HG_D, CHUNK = 4, 128, 64
NCH = S // CHUNK
DA_H, DA_D = 4, 64
LAM_INIT = 0.8 - 0.6 * math.exp(-0.3 * 0)
NG, NE8, NE = 4, 8, 32
FF = 512
TOPK = 2
NBLK = (S * TOPK + NE * (P - 1)) // P
NBLK += NBLK % 2
NSLOT_BLK = NBLK + 2
HD, AH, AKV, BH = 64, 8, 2, 8
BAUG = HD + 4 + 2 * NT
DFF = 4 * D
NEG = -1e30

RING = 4


def chain(eng, sem):
    n = [0]

    def done(ins):
        n[0] += 1
        ins.then_inc(sem, 1)
        return n[0]

    def then(ins):
        eng.wait_ge(sem, done(ins))

    return done, then


def inverse_root(dve, then, r, ms, root, tmp):
    then(dve.reciprocal(r, root))
    then(dve.tensor_tensor(tmp, r, r, ALU.mult))
    then(dve.tensor_tensor(tmp, tmp, ms, ALU.mult))
    then(dve.tensor_scalar(tmp, tmp, -0.5, 1.5, ALU.mult, ALU.add))
    then(dve.tensor_tensor(r, r, tmp, ALU.mult))


class Mem:

    def __init__(self, nc, base):
        self.nc, self.base, self.n = nc, base, 0

    def at(self, name, kb, shape, dt=F32):
        self.n += 1
        return self.nc.alloc_sbuf_tensor_at(f"{name}_{self.n}", list(shape), dt, offset=self.base + (int(kb * KB) + 31) // 32 * 32)


RINGS, CONST, ACTS, FREE, XRES = 0, 24, 32, 96, 175


class Env:

    def __init__(self, nc, ctx, dram):
        self.nc, self.ctx, self.d, self.nsem = nc, ctx, dram, 0
        base = (nc.sbuf_base + 31) // 32 * 32
        ctx.enter_context(nc.sbuf_tensor("arena", [P, 207 * KB // 4], F32))
        self.mem = Mem(nc, base)
        self.pair = [ctx.enter_context(nc.psum_tensor(f"banks{i}", [P, 2 * N], F32)) for i in range(4)]
        self.bank = [self.pair[i // 2][:, i % 2 * N:i % 2 * N + N] for i in range(8)]
        at = self.mem.at
        self.w_raw = at("w_raw", RINGS, [P, RING, N])
        self.w_hi = at("w_hi", RINGS + 8, [P, RING, N], F32R)
        self.w_lo = at("w_lo", RINGS + 16, [P, RING, N], F32R)
        self.act_hi = at("act_hi", ACTS, [P, ND, S], F32R)
        self.act_lo = at("act_lo", ACTS + 32, [P, ND, S], F32R)
        self.xres = at("xres", XRES, [P, NT, D])
        self.ident = at("ident", CONST, [P, P])
        self.ident_bf = at("ident_bf", CONST + 0.5, [P, P], BF16)
        self.mask_bf = at("mask_bf", CONST + 0.75, [P, P], BF16)
        self.mask_f = at("mask_f", CONST + 1, [P, P])

        self.sems = []

    def sem(self, name):
        self.nsem += 1
        self.sems.append(self.nc.alloc_semaphore(name=f"{name}_{self.nsem}"))
        return self.sems[-1]

    def recycle_sems(self):
        self.nc.clear_and_free_semaphores(self.sems)
        self.nc.all_engine_barrier()
        self.sems = []


def norm_stage(v, gain, load_from=None):
    nc, at, sem = v.nc, v.mem.at, v.sem
    gain_b = at("gain_b", FREE, [P, D])
    junk = at("junk", FREE + 4, [P, D])
    xs = at("xs", FREE + 8, [P, 2, D])
    ss = at("ss", FREE + 16, [P, NT])
    ms = at("ms", FREE + 16.1, [P, NT])
    rt = at("rt", FREE + 16.2, [P, NT])
    rstd, tmp = at("rstd", FREE + 16.3, [P, NT]), at("rstd_tmp", FREE + 16.4, [P, NT])
    gain_in, x_in = sem("gain_in"), [sem(f"x_in{t}") for t in range(NT)] if load_from is not None else None
    sq_done, ms_done, rt_done, link = sem("sq_done"), sem("ms_done"), sem("rt_done"), sem("dve_link")
    xs_done, tr_done, hi_done, lo_done = sem("xs_done"), sem("tr_done"), sem("hi_done"), sem("lo_done")

    def hi_of(h, t):
        return v.act_hi[:, 4 * h:4 * h + 4, t * P:(t + 1) * P]

    def lo_of(h, t):
        return v.act_lo[:, 4 * h:4 * h + 4, t * P:(t + 1) * P]

    def tr_bank(n):
        return v.bank[n % 4][:, :].rearrange("p (c t) -> p c t", c=4)

    with nc.Block() as block:
        @block.sync
        def _(sp):
            if load_from is not None:
                for t in range(NT):
                    sp.dma_start(v.xres[:, t, :], load_from[t * P:(t + 1) * P, :]).then_inc(x_in[t], 16)
            sp.dma_start(gain_b[:, :], gain.broadcast_to([P, D])).then_inc(gain_in, 16)

        @block.scalar
        def _(act):
            def evacuate_hi(t):
                for h in range(2):
                    n = 2 * t + h
                    act.wait_ge(tr_done, n + 1)
                    act.activation(hi_of(h, t), tr_bank(n), ACT.Copy).then_inc(hi_done, 1)

            for t in range(NT):
                if load_from is not None:
                    act.wait_ge(x_in[t], 16)
                if t:
                    act.wait_ge(sq_done, t)
                act.activation(junk[:, :], v.xres[:, t, :], ACT.Square, accum_out=ss[:, t:t + 1]).then_inc(sq_done, 1)
                act.wait_ge(ms_done, t + 1)
                act.activation(rt[:, t:t + 1], ms[:, t:t + 1], ACT.Sqrt).then_inc(rt_done, 1)
                if t:
                    evacuate_hi(t - 1)
            evacuate_hi(NT - 1)

        @block.vector
        def _(dve):
            def evacuate_lo(t):
                for h in range(2):
                    n = 2 * t + h
                    dve.wait_ge(hi_done, n + 1)
                    dve.tensor_tensor(lo_of(h, t), tr_bank(n), hi_of(h, t).bitcast(F32), ALU.subtract).then_inc(lo_done, 1)

            _, then = chain(dve, link)
            dve.wait_ge(gain_in, 16)
            for t in range(NT):
                dve.wait_ge(sq_done, t + 1)
                dve.tensor_scalar(ms[:, t:t + 1], ss[:, t:t + 1], 1.0 / D, EPS, ALU.mult, ALU.add).then_inc(ms_done, 1)
                dve.wait_ge(rt_done, t + 1)
                col = slice(t, t + 1)
                inverse_root(dve, then, rstd[:, col], ms[:, col], rt[:, col], tmp[:, col])
                if t >= 2:
                    dve.wait_ge(tr_done, 2 * (t - 1))
                dve.scalar_tensor_tensor(out=xs[:, t % 2, :], in0=v.xres[:, t, :], scalar=rstd[:, t:t + 1],
                                         in1=gain_b[:, :], op0=ALU.mult, op1=ALU.mult).then_inc(xs_done, 1)
                if t:
                    evacuate_lo(t - 1)
            evacuate_lo(NT - 1)

        @block.tensor
        def _(pe):
            for t in range(NT):
                pe.wait_ge(xs_done, t + 1)
                for h in range(2):
                    n = 2 * t + h
                    if n >= 4:
                        pe.wait_ge(lo_done, n - 3)
                    for c in range(4):
                        k = 4 * h + c
                        last = pe.transpose(v.bank[n % 4][:, c * P:(c + 1) * P], xs[:, t % 2, k * P:(k + 1) * P], v.ident[:, :])
                    last.then_inc(tr_done, 1)


class Tile:

    def __init__(self, kind, parts, cols, act, k, first, last, b0=0):
        self.kind, self.parts, self.cols, self.act, self.k = kind, parts, cols, act, k
        self.first, self.last, self.b0 = first, last, b0
        self.after = None
        self.units = NT if kind == "nat" else 2 * (cols // P)


def dense_stage(v, tiles, dve_program, act_steps=None, act_after=None, sp_before=None, sp_steps=None, sems=None):
    nc, sem = v.nc, v.sem
    landed = [sem(f"w_landed{i}") for i in range(RING)]
    hi_done, lo_done, used = sem("w_hi_done"), sem("w_lo_done"), sem("w_used")
    ready, free = sems
    act_steps, sp_steps = act_steps or {}, sp_steps or {}

    with nc.Block() as block:
        @block.sync
        def _(sp):
            if sp_before:
                sp_before(sp)
            for n, tile in enumerate(tiles):
                if n >= RING:
                    sp.wait_ge(lo_done, n - RING + 1)
                for ap, c0, c1 in tile.parts:
                    sp.dma_start(v.w_raw[:, n % RING, c0:c1], ap).then_inc(landed[n % RING], 16)
                for f in sp_steps.get(n, ()):
                    f(sp)

        count, arrived, spent, n_used, n_banks = [0] * RING, [], [], 0, 0
        for n, tile in enumerate(tiles):
            count[n % RING] += 16 * len(tile.parts)
            arrived.append(count[n % RING])
            if tile.last:
                n_banks += tile.units
            else:
                n_used += 1
            spent.append((ready, n_banks) if tile.last else (used, n_used))

        @block.scalar
        def _(act):
            for n, tile in enumerate(tiles):
                act.wait_ge(landed[n % RING], arrived[n])
                if n >= RING:
                    act.wait_ge(*spent[n - RING])
                act.activation(v.w_hi[:, n % RING, :tile.cols], v.w_raw[:, n % RING, :tile.cols], ACT.Copy).then_inc(hi_done, 1)
                for f in act_steps.get(n, ()):
                    f(act)
            if act_after:
                act_after(act)

        @block.gpsimd
        def _(pool):
            for n, tile in enumerate(tiles):
                pool.wait_ge(hi_done, n + 1)
                pool.tensor_tensor(v.w_lo[:, n % RING, :tile.cols], v.w_raw[:, n % RING, :tile.cols],
                                   v.w_hi[:, n % RING, :tile.cols].bitcast(F32), ALU.subtract).then_inc(lo_done, 1)

        @block.vector
        def _(dve):
            dve_program(dve)

        @block.tensor
        def _(pe):
            freed = [0] * 8
            banks = 0
            for n, tile in enumerate(tiles):
                pe.wait_ge(lo_done, n + 1)
                if tile.after:
                    pe.wait_ge(*tile.after)
                hi, lo = tile.act
                w_hi, w_lo = v.w_hi[:, n % RING, :tile.cols], v.w_lo[:, n % RING, :tile.cols]
                for u in range(tile.units):
                    b = tile.b0 + u
                    if tile.first and freed[b]:
                        pe.wait_ge(free, freed[b])
                    if tile.kind == "nat":
                        t = slice(u * P, (u + 1) * P)
                        out = v.bank[b][:, :tile.cols]
                        prods = [(hi[:, tile.k, t], w_hi), (hi[:, tile.k, t], w_lo), (lo[:, tile.k, t], w_hi)]
                    else:
                        c, t = slice(u // 2 * P, u // 2 * P + P), slice(u % 2 * N, u % 2 * N + N)
                        out = v.bank[b][:, :]
                        prods = [(w_hi[:, c], hi[:, tile.k, t]), (w_hi[:, c], lo[:, tile.k, t]), (w_lo[:, c], hi[:, tile.k, t])]
                    for i, (left, right) in enumerate(prods):
                        mm = pe.matmul(out, left, right, start=(tile.first and i == 0), stop=(tile.last and i == 2))
                    if tile.last:
                        banks += 1
                        freed[b] = banks
                        mm.then_inc(ready, 1)
                    elif u == tile.units - 1:
                        mm.then_inc(used, 1)


def rows(w, k, c0, c1):
    return w[k * P:(k + 1) * P, c0:c1]


def group(kind, w, k_tiles, c0, c1, act, k0=0, b0=0):
    return [Tile(kind, [(rows(w, k, c0, c1), 0, c1 - c0)], c1 - c0, act, k0 + k, k == 0, k == k_tiles - 1, b0)
            for k in range(k_tiles)]


class Heads:

    def __init__(self, v, name, dst, heads, at_kb):
        at, sem = v.mem.at, v.sem
        self.dst, self.h = dst, heads
        self.sq = at(name + "_sq", at_kb, [P, heads * HD])
        self.ss = at(name + "_ss", at_kb + 2, [P, NT, heads])
        self.rt = at(name + "_rt", at_kb + 2.25, [P, NT, heads])
        self.r = at(name + "_r", at_kb + 2.5, [P, NT, heads])
        self.tmp = at(name + "_tmp", at_kb + 2.75, [P, NT, heads])
        self.ms_done, self.rt_done = sem(name + "_ms"), sem(name + "_rt")

    def take(self, dve, then, bank, t, free):
        x = self.dst(t)
        src = bank.rearrange("p (h d) -> p h d", h=self.h)
        dve.tensor_copy(x, src).then_inc(free, 1)

    def stat(self, dve, then, t):
        x = self.dst(t)
        sq = self.sq[:, :].rearrange("p (h d) -> p h d", h=self.h)
        then(dve.tensor_tensor(sq, x, x, ALU.mult))
        then(dve.tensor_reduce(self.ss[:, t, :], sq, AX.X, ALU.add))

    def mean(self, dve):
        dve.tensor_scalar(self.ss[:, :, :], self.ss[:, :, :], 1.0 / HD, EPS, ALU.mult, ALU.add).then_inc(self.ms_done, 1)

    def root(self, act):
        act.wait_ge(self.ms_done, 1)
        act.activation(self.rt[:, :, :], self.ss[:, :, :], ACT.Sqrt).then_inc(self.rt_done, 1)

    def inverse(self, dve, then):
        dve.wait_ge(self.rt_done, 1)
        inverse_root(dve, then, self.r[:, :, :], self.ss[:, :, :], self.rt[:, :, :], self.tmp[:, :, :])

    def scale(self, dve, then, t, gain):
        x = self.dst(t)
        then(dve.tensor_tensor(x, x, self.r[:, t, :].unsqueeze(2).broadcast_to([P, self.h, HD]), ALU.mult))
        then(dve.tensor_tensor(x, x, gain.unsqueeze(1).broadcast_to([P, self.h, HD]), ALU.mult))


def rotate(dve, done, then, x, cos, sin, tmp):
    half = HD // 2
    h = x.shape[1]
    x1, x2 = x[:, :, :half], x[:, :, half:]
    c = cos.unsqueeze(1).broadcast_to([P, h, half])
    s = sin.unsqueeze(1).broadcast_to([P, h, half])
    t = [tmp[:, i, :].rearrange("p (h d) -> p h d", h=h) for i in range(4)]
    done(dve.tensor_tensor(t[0], x1, c, ALU.mult))
    done(dve.tensor_tensor(t[1], x2, s, ALU.mult))
    done(dve.tensor_tensor(t[2], x1, s, ALU.mult))
    then(dve.tensor_tensor(t[3], x2, c, ALU.mult))
    done(dve.tensor_tensor(x1, t[0], t[1], ALU.subtract))
    then(dve.tensor_tensor(x2, t[2], t[3], ALU.add))


HG_W, DA_W = HG_H * HG_D, DA_H * 2 * DA_D
COL = dict(zip(("hq", "hf", "hi", "hog", "dq", "dk", "dv", "gate_hg", "gate_da"),
               np.cumsum([0] + [HG_W] * 4 + [DA_W] * 3 + [D]).tolist()))


def block1_tensors(v):
    at = v.mem.at
    v.hqT = at("hqT", FREE, [P, HG_H, S])
    v.hfT = at("hfT", FREE + 16, [P, HG_H, S])
    v.hv = at("hv", FREE + 32, [P, NT, HG_W])
    v.dq = at("dq", FREE + 48, [P, NT, DA_W])
    v.dk = at("dk", FREE + 64, [P, NT, DA_W])
    v.dv = at("dv", FREE + 80, [P, NT, DA_W])


def project1_stage(v):
    nc, at, sem, d = v.nc, v.mem.at, v.sem, v.d
    act_ops = (v.act_hi, v.act_lo)
    w_in = d["w_in"]
    order = ["dq", "dv", "dk", "hf", "hog", "gate_hg", "gate_hg+", "gate_da", "gate_da+", "hq", "hi"]
    tiles = []
    for name in order:
        c0 = COL[name.rstrip("+")] + (N if name.endswith("+") else 0)
        tiles += group("tr" if name[:2] in ("hq", "hf", "ga") else "nat", w_in, ND, c0, c0 + N, act_ops)
    index = {name: g for g, name in enumerate(order)}

    temps = FREE + 96
    q_heads = Heads(v, "dq", lambda t: v.dq[:, t, :].rearrange("p (h d) -> p h d", d=DA_D), 8, temps)
    k_heads = Heads(v, "dk", lambda t: v.dk[:, t, :].rearrange("p (h d) -> p h d", d=DA_D), 8, temps + 3)
    rot = at("rot", temps + 6, [P, 4, 256])
    SLOTS = 2
    stage = at("stage", temps + 10, [P, SLOTS, N])
    cos, sin = at("cos", 29, [P, NT, DA_D // 2]), at("sin", 30, [P, NT, DA_D // 2])
    gains = at("gains", 28, [P, 2, DA_D])
    ready, free = sem("bank_ready"), sem("bank_free")
    tables, link = sem("tables"), sem("dve_link")
    staged, stored = sem("gate_staged"), [sem(f"gate_stored{i}") for i in range(SLOTS)]

    def load_tables(sp):
        sp.dma_start(cos[:, :, :], d["rope_cos"].rearrange("(t p) c -> p t c", p=P)).then_inc(tables, 16)
        sp.dma_start(sin[:, :, :], d["rope_sin"].rearrange("(t p) c -> p t c", p=P)).then_inc(tables, 16)
        sp.dma_start(gains[:, 0, :], d["da_q_norm"].broadcast_to([P, DA_D])).then_inc(tables, 16)
        sp.dma_start(gains[:, 1, :], d["da_k_norm"].broadcast_to([P, DA_D])).then_inc(tables, 16)

    n_staged = [0]

    def banks_to_dram(g, func, dst):
        def run(act):
            for b in range(8):
                i = n_staged[0]
                n_staged[0] += 1
                act.wait_ge(ready, 8 * g + b + 1)
                if i >= SLOTS:
                    act.wait_ge(stored[i % SLOTS], 16 * (i // SLOTS))
                act.activation(stage[:, i % SLOTS, :], v.bank[b][:, :], func).then_inc(free, 1)
                act.wait_ge(free, 8 * g + b + 1)
                act.dma_start(dst(b), stage[:, i % SLOTS, :]).then_inc(stored[i % SLOTS], 16)
        return run

    def gate_rows(gate, more):
        return lambda b: v.d["gateT"][gate, more * 4 + b // 2, :, (b % 2) * N:(b % 2) * N + N]

    steps = {}

    def after(g, offset, f):
        steps.setdefault(8 * (g + 1) + offset, []).append(f)

    def keep_decay(act):
        for b in range(8):
            act.wait_ge(ready, 8 * index["hf"] + b + 1)
            act.activation(v.hfT[:, b // 2, (b % 2) * N:(b % 2) * N + N], v.bank[b][:, :], ACT.Sigmoid).then_inc(free, 1)

    after(index["dq"], 6, q_heads.root)
    after(index["dk"], 6, k_heads.root)
    after(index["hf"], 2, keep_decay)
    last = []
    for name, func, dst in (("hog", ACT.Silu, lambda b: v.d["hog"][b * P:(b + 1) * P, :]),
                            ("gate_hg", ACT.Sigmoid, gate_rows(0, 0)), ("gate_hg+", ACT.Sigmoid, gate_rows(0, 1)),
                            ("gate_da", ACT.Sigmoid, gate_rows(1, 0)), ("gate_da+", ACT.Sigmoid, gate_rows(1, 1))):
        g = index[name]
        if 8 * (g + 1) < len(tiles):
            after(g, 2, banks_to_dram(g, func, dst))
        else:
            last.append(banks_to_dram(g, func, dst))

    def act_after(act):
        for f in last:
            f(act)
        for i in range(SLOTS):
            act.wait_ge(stored[i], 16 * ((n_staged[0] + SLOTS - 1 - i) // SLOTS))

    def dve_program(dve):
        done, then = chain(dve, link)

        def copy(name, dst):
            for b in range(8):
                n = 8 * index[name] + b + 1
                dve.wait_ge(ready, n)
                dve.tensor_copy(dst(b), v.bank[b][:, :]).then_inc(free, 1)

        def norm(name, heads, gain):
            n = 8 * index[name]
            for t in range(NT):
                dve.wait_ge(ready, n + t + 1)
                heads.take(dve, then, v.bank[t][:, :], t, free)
            dve.wait_ge(free, n + NT)
            for t in range(NT):
                heads.stat(dve, then, t)
            heads.mean(dve)
            heads.inverse(dve, then)
            for t in range(NT):
                heads.scale(dve, then, t, gains[:, gain, :])
                rotate(dve, done, then, heads.dst(t), cos[:, t, :], sin[:, t, :], rot)

        dve.wait_ge(tables, 64)
        then(dve.tensor_scalar(gains[:, 0, :], gains[:, 0, :], DA_D ** -0.5, None, ALU.mult))
        norm("dq", q_heads, 0)
        copy("dv", lambda b: v.dv[:, b, :])
        norm("dk", k_heads, 1)
        copy("hq", lambda b: v.hqT[:, b // 2, (b % 2) * N:(b % 2) * N + N])
        copy("hi", lambda b: v.hv[:, b, :])

    dense_stage(v, tiles, dve_program, steps, act_after, sp_before=load_tables, sems=(ready, free))


def hgrn_stage(v):
    nc, at, sem, d = v.nc, v.mem.at, v.sem, v.d
    o = at("o_raw", ACTS, [P, NT, HG_W])
    sets = [dict((name, at(f"{name}{i}", ACTS + 16 + 16 * i + 4 * j, [P, S]))
                 for j, name in enumerate(("q_rel", "k_rel", "q_dec", "k_end"))) for i in range(2)]
    b_ = at("b", ACTS + 48, [P, S])
    sq = at("sq", ACTS + 52, [P, NT, HG_D])
    keep = at("keep", ACTS + 56, [P, S])
    k_rows = at("k_rows", ACTS + 60, [P, NT, P])
    from_mid, to_end, e_mid, e_b = (at(n, RINGS + 4 * i, [P, S]) for i, n in enumerate(("from_mid", "to_end", "e_mid", "e_b")))
    hog = at("hog", RINGS + 16, [P, 2, NT, HG_D])
    scT = at("scT", FREE + 96, [P, 2, NT, CHUNK])
    st = at("state", FREE + 100, [P, NCH, P])
    causal = at("causal", FREE + 108, [P, CHUNK], I32)
    lb = at("lb", FREE + 108.5, [P, 2, HG_H])
    lbt = at("lbt", FREE + 108.75, [P, 4, HG_H])
    dec = at("dec", FREE + 109, [P, 2, NCH])
    gain = at("hg_gain", FREE + 109.5, [P, HG_D])
    ssum, root, inv, itmp = (at(f"o_{n}", FREE + 110 + 0.125 * i, [P, HG_H, NT]) for i, n in enumerate(("ssum", "root", "inv", "tmp")))
    v.o_hg = at("o_hg", FREE, [P, NT, HG_W])

    consts, link, lb_exp, sig = sem("consts"), sem("dve_link"), sem("lb_exp"), sem("sig")
    f_done, ln_done, to_exp, exps, ops = sem("f_done"), sem("ln_done"), sem("to_exp"), sem("exps"), sem("operands")
    scores, scT_done, tr_done, rows_done = sem("scores"), sem("scT_done"), sem("tr_done"), sem("rows_done")
    u_done, state_done, o_done, o_read = sem("u_done"), sem("state_done"), sem("o_done"), sem("o_read")
    sum_done, root_done, gated, normed, zero = sem("sum_done"), sem("root_done"), sem("gated"), sem("normed"), sem("zero")
    hog_in = [sem(f"hog_in{i}") for i in range(2)]

    def by_chunk(x):
        return x.rearrange("p (c t) -> p c t", t=CHUNK)

    def head(x, h):
        return x[:, :, h * HG_D:(h + 1) * HG_D]

    def own_sum(c):
        return v.bank[((2, 3), (1, 5))[c // 8][c % 2]][:, (c // 2 % 4) * P:(c // 2 % 4 + 1) * P]

    def in_place_of_f(h):
        return v.hfT[:, h, :].rearrange("p (t c) -> p t c", t=NT)

    with nc.Block() as block:
        @block.sync
        def _(sp):
            sp.dma_start(keep[:, :], d["chunk_keep"].broadcast_to([P, S])).then_inc(consts, 16)
            sp.dma_start(causal[:, :], d["causal_st"]).then_inc(consts, 16)
            with nc.allow_non_contiguous_dma("lower bounds by partition"):
                sp.dma_start(lbt[:, 0:2, :], d["hg_lb"].rearrange("r (h p) -> p r h", p=P)).then_inc(consts, 16)
            sp.dma_start(gain[:, :], d["hg_out_norm"].broadcast_to([P, HG_D])).then_inc(consts, 16)
            for h in range(HG_H):
                if h >= 2:
                    sp.wait_ge(gated, 2 * h - 2)
                sp.dma_start(hog[:, h % 2, :, :], d["hog"][:, h * HG_D:(h + 1) * HG_D].rearrange("(t p) c -> p t c", p=P)).then_inc(hog_in[h % 2], 16)

        @block.scalar
        def _(act):
            act.wait_ge(lb_exp, 1)
            act.activation(lbt[:, 2:4, :], lbt[:, 2:4, :], ACT.Exp).then_inc(sig, 1)

            def log(h):
                act.wait_ge(f_done, h + 1)
                act.activation(v.hfT[:, h, :], v.hfT[:, h, :], ACT.Ln).then_inc(ln_done, 1)

            def exponentials(h):
                act.wait_ge(to_exp, 2 * h + 1)
                act.activation(e_mid[:, :], from_mid[:, :], ACT.Exp).then_inc(exps, 1)
                act.activation(e_b[:, :], b_[:, :], ACT.Exp).then_inc(exps, 1)
                act.wait_ge(exps, 4 * h + 1)
                act.activation(from_mid[:, :], from_mid[:, :], ACT.Exp, scale=-1.0).then_inc(exps, 1)
                act.wait_ge(to_exp, 2 * h + 2)
                act.activation(to_end[:, :], to_end[:, :], ACT.Exp).then_inc(exps, 1)

            def rows(h):
                for half in range(2):
                    n = 2 * h + half
                    act.wait_ge(tr_done, n + 1)
                    if h:
                        act.wait_ge(u_done, 2 * h)
                    act.activation(k_rows[:, 4 * half:4 * half + 4, :],
                                   v.bank[0][:, :].rearrange("p (t c) -> p t c", t=4), ACT.Copy).then_inc(rows_done, 1)

            def out(h):
                for half in range(2):
                    n = 2 * h + half
                    act.wait_ge(o_done, n + 1)
                    act.activation(o[:, 4 * half:4 * half + 4, h * P:(h + 1) * P],
                                   v.bank[6 + half][:, :].rearrange("p (t c) -> p t c", t=4), ACT.Copy).then_inc(o_read, 1)

            log(0)
            exponentials(0)
            for h in range(HG_H):
                if h + 1 < HG_H:
                    log(h + 1)
                rows(h)
                if h + 1 < HG_H:
                    exponentials(h + 1)
                out(h)
            act.wait_ge(sum_done, 1)
            act.activation(root[:, :, :], ssum[:, :, :], ACT.Sqrt).then_inc(root_done, 1)

        @block.gpsimd
        def _(pool):
            pool.wait_ge(consts, 64)
            for h in range(HG_H):
                og = hog[:, h % 2, :, :]
                pool.wait_ge(hog_in[h % 2], 16 * (h // 2 + 1))
                pool.tensor_tensor(og, og, gain[:, :].unsqueeze(1).broadcast_to([P, NT, HG_D]), ALU.mult).then_inc(gated, 1)
                pool.wait_ge(gated, 2 * h + 1)
                pool.wait_ge(o_read, 2 * h + 2)
                pool.tensor_tensor(in_place_of_f(h), head(o, h), og, ALU.mult).then_inc(gated, 1)

        @block.vector
        def _(dve):
            done, then = chain(dve, link)
            dve.memset(scT[:, :, :, :], 0.0).then_inc(zero, 1)
            dve.wait_ge(consts, 64)
            then(dve.tensor_tensor(lb[:, 0, :], lbt[:, 0, :], lbt[:, 1, :], ALU.max))
            dve.tensor_tensor(lbt[:, 2:4, :], lbt[:, 0:2, :], lb[:, 0:1, :].broadcast_to([P, 2, HG_H]), ALU.subtract).then_inc(lb_exp, 1)
            dve.wait_ge(sig, 1)
            then(dve.tensor_tensor(lb[:, 1, :], lbt[:, 2, :], lbt[:, 3, :], ALU.add))
            then(dve.reciprocal(lb[:, 1, :], lb[:, 1, :]))
            then(dve.tensor_tensor(lb[:, 0, :], lbt[:, 2, :], lb[:, 1, :], ALU.mult))
            then(dve.tensor_scalar(lb[:, 1, :], lb[:, 0, :], -1.0, 1.0, ALU.mult, ALU.add))

            def gates(h):
                if h >= 2:
                    dve.wait_ge(o_done, 2 * (h - 1))
                f = v.hfT[:, h, :]
                then(dve.tensor_scalar(f, f, lb[:, 1, h:h + 1], lb[:, 0, h:h + 1], ALU.mult, ALU.add))
                dve.tensor_scalar(sets[h % 2]["k_end"][:, :], f, -1.0, 1.0, ALU.mult, ALU.add).then_inc(f_done, 1)

            def sums(h):
                dve.wait_ge(ln_done, h + 1)
                then(dve.tensor_tensor_scan(b_[:, :], keep[:, :], v.hfT[:, h, :], 0.0, ALU.mult, ALU.add))
                b = by_chunk(b_[:, :])
                mid, end = (b[:, :, c:c + 1].broadcast_to([P, NCH, CHUNK]) for c in (CHUNK // 2 - 1, CHUNK - 1))
                dve.tensor_tensor(by_chunk(from_mid[:, :]), b, mid, ALU.subtract).then_inc(to_exp, 1)
                dve.tensor_tensor(by_chunk(to_end[:, :]), end, b, ALU.subtract).then_inc(to_exp, 1)

            def operands(h):
                s, q = sets[h % 2], v.hqT[:, h, :]
                k = s["k_end"][:, :]
                for i, (name, src, e) in enumerate((("q_rel", q, e_mid), ("q_dec", q, e_b), ("k_rel", k, from_mid), ("k_end", k, to_end))):
                    dve.wait_ge(exps, 4 * h + i + 1)
                    if i == 3:
                        dve.wait_ge(ops, 4 * h + 3)
                    dve.tensor_tensor(s[name][:, :], src, e[:, :], ALU.mult).then_inc(ops, 1)
                    if i == 1:
                        then(dve.tensor_copy(dec[:, h % 2, :], by_chunk(e_b[:, :])[:, :, CHUNK - 1:CHUNK].rearrange("p c o -> p (c o)")))
                dve.wait_ge(ops, 4 * h + 4)

            def causal_scores(h):
                dve.wait_ge(scores, h + 1)
                if h >= 2:
                    dve.wait_ge(o_done, 2 * (h - 1))
                dve.copy_predicated(scT[:, h % 2, :, :], causal[:, :].unsqueeze(1).broadcast_to([P, NT, CHUNK]),
                                    v.bank[4][:, :].rearrange("p (t c) -> p t c", t=NT)).then_inc(scT_done, 1)

            def states(h, half):
                dve.wait_ge(u_done, 2 * h + half + 1)
                for c in range(8 * half, 8 * half + 8):
                    u = own_sum(c)
                    if c == 0:
                        if h:
                            dve.wait_ge(o_done, 2 * h)
                        ins = dve.tensor_copy(st[:, 0, :], u)
                    else:
                        dve.wait_ge(state_done, NCH * h + c)
                        ins = dve.scalar_tensor_tensor(out=st[:, c, :], in0=st[:, c - 1, :], scalar=dec[:, h % 2, c:c + 1], in1=u,
                                                       op0=ALU.mult, op1=ALU.add)
                    ins.then_inc(state_done, 1)

            def squares(h):
                dve.wait_ge(o_read, 2 * h + 2)
                then(dve.tensor_tensor(sq[:, :, :], head(o, h), head(o, h), ALU.mult))
                then(dve.tensor_reduce(ssum[:, h, :], sq[:, :, :], AX.X, ALU.add))

            gates(0)
            sums(0)
            for h in range(HG_H):
                operands(h)
                if h + 1 < HG_H:
                    gates(h + 1)
                causal_scores(h)
                if h:
                    squares(h - 1)
                states(h, 0)
                if h + 1 < HG_H:
                    sums(h + 1)
                states(h, 1)
            squares(HG_H - 1)
            dve.tensor_scalar(ssum[:, :, :], ssum[:, :, :], 1.0 / HG_D, EPS, ALU.mult, ALU.add).then_inc(sum_done, 1)
            dve.wait_ge(root_done, 1)
            inverse_root(dve, then, inv[:, :, :], ssum[:, :, :], root[:, :, :], itmp[:, :, :])
            for h in range(HG_H):
                dve.wait_ge(gated, 2 * h + 2)
                dve.tensor_tensor(head(v.o_hg, h), in_place_of_f(h), inv[:, h, :].unsqueeze(2).broadcast_to([P, NT, HG_D]),
                                  ALU.mult).then_inc(normed, 1)

        @block.tensor
        def _(pe):
            def chunk_rows(c):
                return slice(c % 2 * CHUNK, c % 2 * CHUNK + CHUNK)

            for h in range(HG_H):
                s = sets[h % 2]
                hc = slice(h * P, (h + 1) * P)
                pe.wait_ge(ops, 4 * h + 3)
                if h:
                    pe.wait_ge(scT_done, h)
                for c in range(NCH):
                    t = slice(c * CHUNK, (c + 1) * CHUNK)
                    mm = pe.matmul(v.bank[4][chunk_rows(c), c // 2 * CHUNK:(c // 2 + 1) * CHUNK],
                                   s["k_rel"][:, t], s["q_rel"][:, t], start=True, stop=True)
                mm.then_inc(scores, 1)
                pe.wait_ge(ops, 4 * h + 4)
                for half in range(2):
                    if h or half:
                        pe.wait_ge(rows_done, 2 * h + half)
                    for t in range(4):
                        tt = 4 * half + t
                        mm = pe.transpose(v.bank[0][:, t * P:(t + 1) * P], s["k_end"][:, tt * P:(tt + 1) * P], v.ident[:, :])
                    mm.then_inc(tr_done, 1)
                for c in range(NCH):
                    n = 2 * h + c // 8
                    if c % 8 == 0:
                        pe.wait_ge(rows_done, n + 1)
                        if h:
                            pe.wait_ge(state_done, 8 * n - 8)
                    r = chunk_rows(c)
                    mm = pe.matmul(own_sum(c), k_rows[r, c // 2, :], v.hv[r, c // 2, hc], start=True, stop=True)
                    if c % 8 == 7:
                        mm.then_inc(u_done, 1)
                pe.wait_ge(scT_done, h + 1)
                for half in range(2):
                    n = 2 * h + half
                    if h:
                        pe.wait_ge(o_read, n - 1)
                    for c in range(8 * half, 8 * half + 8):
                        r, tt = chunk_rows(c), c // 2
                        out = v.bank[6 + half][r, (tt % 4) * P:(tt % 4 + 1) * P]
                        mm = pe.matmul(out, scT[r, h % 2, tt, :], v.hv[r, tt, hc], start=True, stop=(c == 0))
                        if c:
                            pe.wait_ge(state_done, NCH * h + c)
                            mm = pe.matmul(out, s["q_dec"][:, c * CHUNK:(c + 1) * CHUNK], st[:, c - 1, :], start=False, stop=True)
                    mm.then_inc(o_done, 1)


def split_scores(pe, v, pair, q_hi, k_hi, q_both, k_both, nk):
    for c0 in range(0, nk, N):
        c = slice(c0, min(c0 + N, nk))
        pe.matmul(pair[:, c], q_hi, k_hi[:, c], start=True, stop=False)
        mm = pe.matmul(pair[:, c], q_both, k_both[:, c], start=False, stop=(c.stop < nk))
    return pe.matmul(pair[:, nk - P:nk], v.ident_bf[:, :], v.mask_bf[:, :], start=False, stop=True)


def diff_attention_stage(v):
    nc, at, sem, d = v.nc, v.mem.at, v.sem, v.d
    q_both = [at(f"q_both{a}", ACTS + 16 * a, [P, DA_H, S], F32R) for a in range(2)]
    k_both = [at(f"k_both{a}", ACTS + 32 + 16 * a, [P, DA_H, S], F32R) for a in range(2)]
    k_hi = at("k_hi", FREE + 16, [P, DA_H, S], F32R)
    probs = at("probs", RINGS, [P, 2, 2, S])
    a_ = at("a", RINGS + 16, [P, 2, S])
    aT = at("aT", FREE + 96, [P, 2, S])
    o = v.dq
    v.o_da = v.dq
    small = FREE + 104
    lam_in = at("lam_in", small, [P, 4, DA_D])
    lam_pr = at("lam_pr", small + 1, [P, 2, DA_D])
    lam = at("lam", small + 1.5, [P, 4])
    gain = at("da_gain", small + 2, [P, 2 * DA_D])
    nmax, sums, inv, coef = (at(n, small + 3 + 0.25 * i, [P, 4, 2]) for i, n in enumerate(("nmax", "sums", "inv", "coef")))
    ssum, root, rinv, itmp = (at(f"oda_{i}", small + 4 + 0.25 * i, [P, NT, DA_H]) for i in range(4))
    junk = at("junk", small + 5, [P, 2 * DA_D])

    link, lam_loaded, lam_dot, lam_exp = sem("dve_link"), sem("lam_loaded"), sem("lam_dot"), sem("lam_exp")
    tr_ready, q_split, k_high, k_low, k_moved = sem("tr_ready"), sem("q_hi"), sem("k_hi"), sem("k_lo"), sem("k_moved")
    q_low = sem("q_lo")
    scored, maxed, exped, mixed = sem("scored"), sem("maxed"), sem("exped"), sem("mixed")
    turned_low, turned_high, low_read, high_read = sem("turned_low"), sem("turned_high"), sem("low_read"), sem("high_read")
    weighed, weigh_read, squared, scaled = sem("weighed"), sem("weigh_read"), sem("squared"), sem("scaled")
    sum_done, root_done = sem("sum_done"), sem("root_done")
    units = [(i, h) for i in range(NT) for h in range(DA_H)]
    n_units = len(units)
    highs = np.cumsum([0] + [int(i >= 4) for i, _ in units]).tolist()
    LOW, HIGH = v.bank[4], v.bank[5]

    def half_rows(a):
        return slice(a * DA_D, (a + 1) * DA_D)

    def prepares(p):
        i, h = units[p]
        return i + 1 if h == 1 and i + 1 < NT else None

    with nc.Block() as block:
        @block.sync
        def _(sp):
            sp.dma_start(lam_in[:, :, :], d["da_lambda"].rearrange("(o a) c -> o a c", o=1).broadcast_to([P, 4, DA_D])).then_inc(lam_loaded, 16)
            sp.dma_start(gain[:, :], d["da_out_norm"].broadcast_to([P, 2 * DA_D])).then_inc(lam_loaded, 16)

        def tile_of(x, t):
            return x[:, :, t * P:(t + 1) * P]

        def heads(bank, r):
            return bank[r, :].rearrange("p (h t) -> p h t", h=DA_H)

        @block.scalar
        def _(act):
            def prepare(t):
                act.wait_ge(tr_ready, 2 * t + 1)
                for a in range(2):
                    r = half_rows(a)
                    act.activation(tile_of(q_both[a][r], t), heads(LOW, r), ACT.Copy).then_inc(q_split, 1)
                act.wait_ge(tr_ready, 2 * t + 2)
                act.activation(tile_of(k_hi, t), heads(HIGH, slice(0, P)), ACT.Copy).then_inc(k_high, 1)
                for a in range(2):
                    act.activation(tile_of(k_both[a][half_rows(1 - a)], t), heads(HIGH, half_rows(a)), ACT.Copy).then_inc(k_moved, 1)

            def turn_out(p):
                act.wait_ge(turned_low, p + 1)
                if p >= 2:
                    act.wait_ge(weighed, p - 1)
                c = min((units[p][0] + 1) * P, N)
                act.activation(aT[:, p % 2, :c], LOW[:, :c], ACT.Copy).then_inc(low_read, 1)

            def square(p):
                i, h = units[p]
                act.wait_ge(weigh_read, p + 1)
                if p:
                    act.wait_ge(squared, p)
                act.activation(junk[:, :], o[:, i, h * P:(h + 1) * P], ACT.Square, accum_out=ssum[:, i, h:h + 1]).then_inc(squared, 1)

            prepare(0)
            act.wait_ge(lam_dot, 1)
            act.activation(lam[:, 0:2], lam[:, 0:2], ACT.Exp).then_inc(lam_exp, 1)
            for p, (i, h) in enumerate(units):
                nk = (i + 1) * P
                for a in range(2):
                    act.wait_ge(maxed, 2 * p + a + 1)
                    if p >= 2:
                        act.wait_ge(mixed, p - 1)
                    act.activation(probs[:, p % 2, a, :nk], v.pair[a][:, :nk], ACT.Exp, bias=nmax[:, p % 4, a:a + 1],
                                   accum_out=sums[:, p % 4, a:a + 1]).then_inc(exped, 1)
                if p >= 2:
                    turn_out(p - 2)
                if prepares(p):
                    prepare(prepares(p))
                if p >= 4:
                    square(p - 4)
            turn_out(n_units - 2)
            turn_out(n_units - 1)
            for p in range(n_units - 4, n_units):
                square(p)
            act.wait_ge(sum_done, 1)
            act.activation(root[:, :, :], ssum[:, :, :], ACT.Sqrt).then_inc(root_done, 1)

        def weight_rows(pool, t):
            pool.wait_ge(squared, DA_H * (t + 1))
            x = o[:, t, :].rearrange("p (h c) -> p h c", h=DA_H)
            pool.tensor_tensor(x, x, gain[:, :].unsqueeze(1).broadcast_to([P, DA_H, 2 * DA_D]), ALU.mult).then_inc(scaled, 1)

        @block.gpsimd
        def _(pool):
            pool.wait_ge(lam_dot, 1)
            for t in range(NT):
                weight_rows(pool, t)

        @block.vector
        def _(dve):
            done, then = chain(dve, link)

            def prepare(t):
                for a in range(2):
                    r, other = half_rows(a), half_rows(1 - a)
                    dve.wait_ge(q_split, 2 * t + a + 1)
                    dve.tensor_tensor(tile_of(q_both[a][other], t), heads(LOW, r), tile_of(q_both[a][r], t).bitcast(F32), ALU.subtract).then_inc(q_low, 1)
                dve.wait_ge(k_high, t + 1)
                dve.wait_ge(k_moved, 2 * t + 2)
                for a in range(2):
                    r = half_rows(a)
                    dve.tensor_tensor(tile_of(k_both[a][r], t), heads(HIGH, r), tile_of(k_hi[r], t).bitcast(F32), ALU.subtract).then_inc(k_low, 1)

            def mix(p):
                s, nk = p % 4, (units[p][0] + 1) * P
                dve.wait_ge(exped, 2 * p + 2)
                then(dve.reciprocal(inv[:, s, :], sums[:, s, :]))
                then(dve.scalar_tensor_tensor(out=coef[:, s, 0:1], in0=sums[:, s, 0:1], scalar=inv[:, s, 1:2], in1=lam[:, 3:4],
                                              op0=ALU.mult, op1=ALU.mult))
                if p >= 2:
                    dve.wait_ge(turned_low, p - 1)
                    if highs[p - 1]:
                        dve.wait_ge(turned_high, highs[p - 1])
                dve.scalar_tensor_tensor(out=a_[:, p % 2, :nk], in0=probs[:, p % 2, 1, :nk], scalar=coef[:, s, 0:1],
                                         in1=probs[:, p % 2, 0, :nk], op0=ALU.mult, op1=ALU.add).then_inc(mixed, 1)

            def turn_out(p):
                nk = (units[p][0] + 1) * P
                if nk > N:
                    dve.wait_ge(turned_high, highs[p + 1])
                    if p >= 2:
                        dve.wait_ge(weighed, p - 1)
                    dve.tensor_copy(aT[:, p % 2, N:nk], HIGH[:, :nk - N]).then_inc(high_read, 1)

            def out(p):
                i, h = units[p]
                dve.wait_ge(weighed, p + 1)
                dve.tensor_scalar(o[:, i, h * P:(h + 1) * P], v.bank[6 + p % 2][:, 0:P], inv[:, p % 4, 0:1], None,
                                  ALU.mult).then_inc(weigh_read, 1)

            dve.wait_ge(lam_loaded, 32)
            pairs = lam_in[:, :, :].rearrange("p (a b) c -> p a b c", b=2)
            then(dve.tensor_tensor(lam_pr[:, :, :], pairs[:, :, 0, :], pairs[:, :, 1, :], ALU.mult))
            then(dve.tensor_scalar(gain[:, :], gain[:, :], 1.0 - LAM_INIT, None, ALU.mult))
            dve.tensor_reduce(lam[:, 0:2], lam_pr[:, :, :], AX.X, ALU.add).then_inc(lam_dot, 1)
            prepare(0)
            dve.wait_ge(lam_exp, 1)
            then(dve.tensor_tensor(lam[:, 2:3], lam[:, 1:2], lam[:, 0:1], ALU.subtract))
            then(dve.tensor_scalar(lam[:, 3:4], lam[:, 2:3], -LAM_INIT, None, ALU.add))
            for p, (i, h) in enumerate(units):
                nk = (i + 1) * P
                for a in range(2):
                    dve.wait_ge(scored, 2 * p + a + 1)
                    dve.tensor_reduce(nmax[:, p % 4, a:a + 1], v.pair[a][:, :nk], AX.X, ALU.max, negate=True).then_inc(maxed, 1)
                if p >= 1:
                    mix(p - 1)
                if p >= 2:
                    turn_out(p - 2)
                if prepares(p):
                    prepare(prepares(p))
                if p >= 3:
                    out(p - 3)
            mix(n_units - 1)
            turn_out(n_units - 2)
            out(n_units - 3)
            turn_out(n_units - 1)
            out(n_units - 2)
            out(n_units - 1)
            dve.wait_ge(squared, n_units)
            dve.tensor_scalar(ssum[:, :, :], ssum[:, :, :], 1.0 / (2 * DA_D), EPS, ALU.mult, ALU.add).then_inc(sum_done, 1)
            dve.wait_ge(root_done, 1)
            inverse_root(dve, then, rinv[:, :, :], ssum[:, :, :], root[:, :, :], itmp[:, :, :])
            dve.wait_ge(scaled, NT)
            x = o[:, :, :].rearrange("p t (h c) -> p (t h) c", c=2 * DA_D)
            then(dve.tensor_tensor(x, x, rinv[:, :, :].rearrange("p t h -> p (t h)").unsqueeze(2).broadcast_to([P, NT * DA_H, 2 * DA_D]), ALU.mult))

        @block.tensor
        def _(pe):
            def prepare(t):
                for bank, src in ((LOW, v.dq), (HIGH, v.dk)):
                    for h in range(DA_H):
                        mm = pe.transpose(bank[:, h * P:(h + 1) * P], src[:, t, h * P:(h + 1) * P], v.ident[:, :])
                    mm.then_inc(tr_ready, 1)

            def scores(p):
                i, h = units[p]
                if h == 0:
                    pe.wait_ge(q_low, 2 * i + 2)
                    pe.wait_ge(k_low, 2 * i + 2)
                    pe.wait_ge(k_moved, 2 * i + 2)
                t = slice(i * P, (i + 1) * P)
                for a in range(2):
                    if p:
                        pe.wait_ge(exped, 2 * (p - 1) + a + 1)
                    r = half_rows(a)
                    split_scores(pe, v, v.pair[a], q_both[a][r, h, t], k_hi[r, h, :], q_both[a][:, h, t], k_both[a][:, h, :],
                                 (i + 1) * P).then_inc(scored, 1)

            def free_banks(p):
                if p >= 0:
                    pe.wait_ge(low_read, p + 1)
                    if highs[p + 1]:
                        pe.wait_ge(high_read, highs[p + 1])

            def turn(p):
                pe.wait_ge(mixed, p + 1)
                free_banks(p - 1)
                i = units[p][0]
                for j in range(i + 1):
                    bank, c = (LOW, HIGH)[j // 4], slice(j % 4 * P, (j % 4 + 1) * P)
                    mm = pe.transpose(bank[:, c], a_[:, p % 2, j * P:(j + 1) * P], v.ident[:, :])
                    if j == min(i, 3):
                        mm.then_inc(turned_low, 1)
                if i >= 4:
                    mm.then_inc(turned_high, 1)

            def weigh(p):
                i, h = units[p]
                free_banks(p)
                if p >= 2:
                    pe.wait_ge(weigh_read, p - 1)
                for j in range(i + 1):
                    mm = pe.matmul(v.bank[6 + p % 2][:, 0:P], aT[:, p % 2, j * P:(j + 1) * P], v.dv[:, j, h * P:(h + 1) * P],
                                   start=(j == 0), stop=(j == i))
                mm.then_inc(weighed, 1)

            prepare(0)
            for p in range(n_units):
                scores(p)
                t = prepares(p - 1) if p else None
                if t:
                    pe.wait_ge(q_low, 2 * t + 2)
                    pe.wait_ge(k_low, 2 * t + 2)
                    pe.wait_ge(k_moved, 2 * t + 2)
                if p >= 2:
                    turn(p - 2)
                if prepares(p):
                    free_banks(p - 2)
                    prepare(prepares(p))
                if p >= 3:
                    weigh(p - 3)
            turn(n_units - 2)
            weigh(n_units - 3)
            turn(n_units - 1)
            weigh(n_units - 2)
            weigh(n_units - 1)


def turn_rows_stage(v, chunk, arrive=None, sp_program=None):
    nc, sem = v.nc, v.sem
    turned, hi_done, lo_done = sem("turned"), sem("hi_done"), sem("lo_done")

    def part(x, h, t):
        return x[:, 4 * h:4 * h + 4, t * P:(t + 1) * P]

    def bank(n):
        return v.bank[n % 8].rearrange("p (c t) -> p c t", c=4)

    with nc.Block() as block:
        @block.sync
        def _(sp):
            if sp_program:
                sp_program(sp)

        @block.scalar
        def _(act):
            for n in range(2 * NT):
                act.wait_ge(turned, n + 1)
                act.activation(part(v.act_hi, n % 2, n // 2), bank(n), ACT.Copy).then_inc(hi_done, 1)

        @block.vector
        def _(dve):
            for n in range(2 * NT):
                dve.wait_ge(hi_done, n + 1)
                dve.tensor_tensor(part(v.act_lo, n % 2, n // 2), bank(n), part(v.act_hi, n % 2, n // 2).bitcast(F32),
                                  ALU.subtract).then_inc(lo_done, 1)

        @block.tensor
        def _(pe):
            for n in range(2 * NT):
                t, h = n // 2, n % 2
                if arrive and h == 0:
                    arrive(pe, t)
                if n >= 8:
                    pe.wait_ge(lo_done, n - 7)
                for c in range(4):
                    mm = pe.transpose(v.bank[n % 8][:, c * P:(c + 1) * P], chunk(t, 4 * h + c), v.ident[:, :])
                mm.then_inc(turned, 1)


def turn_mixers_stage(v):
    def chunk(t, k):
        return (v.o_hg if k < 4 else v.o_da)[:, t, k % 4 * P:(k % 4 + 1) * P]
    turn_rows_stage(v, chunk)


def branch_stage(v):
    nc, at, sem, d = v.nc, v.mem.at, v.sem, v.d
    v.mix_hi, v.mix_lo = at("mix_hi", FREE, [P, ND, S], F32R), at("mix_lo", FREE + 32, [P, ND, S], F32R)
    hg = at("hg_part", FREE + 64, [P, 8, N])
    gate = at("gate", FREE + 80, [P, 8, N])
    m = at("m", FREE + 96, [P, 2, N])
    W = 2 * P
    act = (v.act_hi, v.act_lo)
    tiles = []
    for g in range(D // W):
        c0, c1 = g * W, (g + 1) * W
        tiles += group("tr", d["w_branch_hg"], HG_W // P, c0, c1, act, 0, 0)
        tiles += group("tr", d["w_branch_da"], DA_W // P, c0, c1, act, HG_W // P, 4)
    ready, free, link = sem("bank_ready"), sem("bank_free"), sem("dve_link")
    gate_in = [sem(f"gate_in{i}") for i in range(8)]
    m_done, hi_done = sem("m_done"), sem("mix_hi_done")
    used = []
    for g in range(D // W):
        used += [(g, side, u) for side in range(2) for u in range(4)]

    def load_gate(n):
        g, side, u = used[n]

        def run(sp):
            if n >= 8:
                sp.wait_ge(free, n - 7)
            sp.dma_start(gate[:, n % 8, :], d["gateT"][side, 2 * g + u // 2, :, u % 2 * N:u % 2 * N + N]).then_inc(gate_in[n % 8], 16)
        return run

    sp_steps = {n: [load_gate(n)] for n in range(len(used))}
    act_steps = {}

    def hi_part(g):
        def run(act_):
            for u in range(4):
                i = 4 * g + u
                act_.wait_ge(m_done, i + 1)
                act_.activation(v.mix_hi[:, 2 * g + u // 2, u % 2 * N:u % 2 * N + N], m[:, i % 2, :], ACT.Copy).then_inc(hi_done, 1)
        return run

    for g in range(D // W - 1):
        act_steps[8 * (g + 1) + 2] = [hi_part(g)]

    def dve_program(dve):
        done, then = chain(dve, link)
        for g in range(D // W):
            for side in range(2):
                for u in range(4):
                    n = 8 * g + 4 * side + u
                    dve.wait_ge(gate_in[n % 8], 16 * (n // 8 + 1))
                    dve.wait_ge(ready, n + 1)
                    if side == 0:
                        dve.tensor_tensor(hg[:, 4 * (g % 2) + u, :], v.bank[u], gate[:, n % 8, :], ALU.mult).then_inc(free, 1)
                        continue
                    i = 4 * g + u
                    if i >= 2:
                        dve.wait_ge(lo_done, i - 1)
                    dve.tensor_tensor(m[:, i % 2, :], v.bank[4 + u], gate[:, n % 8, :], ALU.mult).then_inc(free, 1)
                    dve.wait_ge(free, n + 1)
                    dve.tensor_tensor(m[:, i % 2, :], m[:, i % 2, :], hg[:, 4 * (g % 2) + u, :], ALU.add).then_inc(m_done, 1)
                    if i:
                        low(dve, i - 1)
        low(dve, 4 * (D // W) - 1)

    lo_done = sem("mix_lo_done")

    def low(dve, i):
        g, u = i // 4, i % 4
        dve.wait_ge(hi_done, i + 1)
        c, t = 2 * g + u // 2, slice(u % 2 * N, u % 2 * N + N)
        dve.tensor_tensor(v.mix_lo[:, c, t], m[:, i % 2, :], v.mix_hi[:, c, t].bitcast(F32), ALU.subtract).then_inc(lo_done, 1)

    dense_stage(v, tiles, dve_program, act_steps, act_after=hi_part(D // W - 1), sp_steps=sp_steps, sems=(ready, free))


def add_rows_stage(v, tiles, groups_of, load_from=None, to_dram=None):
    nc, sem = v.nc, v.sem
    ready, free = sem("bank_ready"), sem("bank_free")
    x_in = sem("x_in")

    def load(sp):
        if load_from is not None:
            sp.dma_start(v.xres[:, :, :], load_from.rearrange("(t p) c -> p t c", p=P)).then_inc(x_in, 16)

    def dve_program(dve):
        if load_from is not None:
            dve.wait_ge(x_in, 16)
        for g, c0 in enumerate(groups_of):
            for t in range(NT):
                dve.wait_ge(ready, 8 * g + t + 1)
                x = v.xres[:, t, c0:c0 + N]
                dve.tensor_tensor(x, v.bank[t], x, ALU.add).then_inc(free, 1)

    dense_stage(v, tiles, dve_program, sp_steps={RING: [load]}, sems=(ready, free))


def output1_stage(v):
    act = (v.mix_hi, v.mix_lo)
    tiles = sum((group("nat", v.d["w_out"], ND, c, c + N, act) for c in (0, N)), [])
    add_rows_stage(v, tiles, (0, N), load_from=v.d["x"])


def router_stage(v):
    nc, at, sem, d = v.nc, v.mem.at, v.sem, v.d
    f = FREE
    gain_b, junk = at("gain_b", f, [P, D]), at("junk", f + 4, [P, D])
    xs = at("xs", f + 8, [P, 2, D])
    xT = at("xT", f + 16, [P, 2, ND, P])
    wr = at("w_router", f + 24, [P, ND, NG + NE])
    bias = at("b_router", f + 25.5, [P, NG + NE])
    lg = at("logits", f + 26, [P, NT, NG + NE])
    upper, ones = at("upper", f + 28, [P, P]), at("ones", f + 28.5, [P, P])
    n_first = NG + NE8 + NSLOT_BLK + NT + NBLK // 2
    firsts = at("firsts", f + 29, [P, n_first])
    ss, ms, rt, rstd, tmp = (at(f"r{i}", f + 30 + 0.125 * i, [P, NT]) for i in range(5))
    A = [at(f"route{i}", f + 31 + i, [P, NT * NE]) for i in range(12)]
    B = [at(f"small{i}", f + 43 + 0.25 * i, [P, NT * NE8]) for i in range(12)]
    cmp_ = at("cmp", f + 48, [P, NSLOT_BLK * NE])
    token_rows = at("token_rows", f + 56, [P, TOPK, NT, 2], I32)
    v.e_w = at("e_w", CONST + 2, [P, TOPK, NT])
    v.dest = at("dest", CONST + 2.25, [P, TOPK, NT], I32)
    v.blk_e = at("blk_e", CONST + 2.5, [1, NSLOT_BLK], I32)
    v.turns = at("turns", CONST + 2.75, [1, 8], I32)
    v.slots = at("slots", CONST + 3, [P, NSLOT_BLK, 2], I32)

    const_in, slots_init = sem("const_in"), sem("slots_init")
    sq_done, ms_done, rt_done, link = sem("sq_done"), sem("ms_done"), sem("rt_done"), sem("dve_link")
    xs_done, stored, turned, xT_done, logit, logit_read = (sem(n) for n in ("xs_done", "stored", "turned", "xT_done", "logit", "logit_read"))
    x_exp, exped, chosen, ranked, ones_set = sem("x_exp"), sem("exped"), sem("chosen"), sem("ranked"), sem("ones_set")
    placed, scattered, listed = sem("placed"), sem("scattered"), sem("listed")
    store_n = [sem(f"store{i}") for i in range(2)]

    def first(a, n):
        return firsts[:, a:a + n]

    f_group, f_expert, f_block, f_tile, f_turn = (first(a, n) for a, n in zip(
        np.cumsum([0, NG, NE8, NSLOT_BLK, NT]).tolist(), (NG, NE8, NSLOT_BLK, NT, NBLK // 2)))

    with nc.Block() as block:
        @block.sync
        def _(sp):
            sp.dma_start(gain_b[:, :], d["norm_moe"].broadcast_to([P, D])).then_inc(const_in, 16)
            sp.dma_start(wr[:, :, 0:NG], d["w_router_group"].rearrange("(k p) n -> p k n", p=P)).then_inc(const_in, 16)
            sp.dma_start(wr[:, :, NG:], d["w_router_expert"].rearrange("(k p) n -> p k n", p=P)).then_inc(const_in, 16)
            sp.dma_start(bias[:, 0:NG], d["b_router_group"].broadcast_to([P, NG])).then_inc(const_in, 16)
            sp.dma_start(bias[:, NG:], d["b_router_expert"].broadcast_to([P, NE])).then_inc(const_in, 16)
            sp.dma_start(upper[:, :], d["upper"]).then_inc(const_in, 16)
            sp.dma_start(firsts[:, :], d["firsts"].broadcast_to([P, n_first])).then_inc(const_in, 16)
            sp.dma_start(token_rows[:, :, :, :], d["token_rows"]).then_inc(const_in, 16)
            sp.dma_start(d["slot_table"], d["slot_init"]).then_inc(slots_init, 16)
            for t in range(NT):
                sp.wait_ge(xs_done, t + 1)
                sp.dma_start(d["xn"][t * P:(t + 1) * P, :], xs[:, t % 2, :]).then_inc(store_n[t % 2], 16)
            for i in range(2):
                sp.wait_ge(store_n[i], 16 * NT // 2)
            sp.wait_ge(scattered, 16 * TOPK * NT)
            with nc.allow_non_contiguous_dma("slots of a block by partition"):
                sp.dma_start(v.slots[:, :, :], d["slot_table"].rearrange("(b p) o -> p b o", p=P)).then_inc(listed, 16)
            sp.wait_ge(listed, 16)

        @block.gpsimd
        def _(pool):
            pool.wait_ge(slots_init, 16)
            pool.wait_ge(const_in, 128)
            pool.wait_ge(placed, 1)
            for k in range(TOPK):
                for t in range(NT):
                    pool.indirect_dma_start(d["slot_table"], bass.IndirectOffsetOnAxis(ap=v.dest[:, k, t:t + 1], axis=0),
                                            token_rows[:, k, t, :], None).then_inc(scattered, 16)

        @block.scalar
        def _(act):
            for t in range(NT):
                if t:
                    act.wait_ge(sq_done, t)
                act.activation(junk[:, :], v.xres[:, t, :], ACT.Square, accum_out=ss[:, t:t + 1]).then_inc(sq_done, 1)
                act.wait_ge(ms_done, t + 1)
                act.activation(rt[:, t:t + 1], ms[:, t:t + 1], ACT.Sqrt).then_inc(rt_done, 1)
                for h in range(2):
                    act.wait_ge(turned, 2 * t + h + 1)
                    if t >= 2:
                        act.wait_ge(logit, t - 1)
                    act.activation(xT[:, t % 2, 4 * h:4 * h + 4, :], v.bank[(2 * t + h) % 4].rearrange("p (c t) -> p c t", c=4),
                                   ACT.Copy).then_inc(xT_done, 1)
            act.wait_ge(x_exp, 1)
            act.activation(B[1][:, 0:NT * NG], B[0][:, 0:NT * NG], ACT.Exp).then_inc(exped, 1)
            act.wait_ge(x_exp, 2)
            act.activation(B[11][:, 0:NT], B[10][:, 0:NT], ACT.Exp).then_inc(exped, 1)

        @block.vector
        def _(dve):
            done, then = chain(dve, link)
            dve.memset(ones[:, :], 1.0).then_inc(ones_set, 1)
            dve.wait_ge(const_in, 128)
            for t in range(NT):
                col = slice(t, t + 1)
                dve.wait_ge(sq_done, t + 1)
                dve.tensor_scalar(ms[:, col], ss[:, col], 1.0 / D, EPS, ALU.mult, ALU.add).then_inc(ms_done, 1)
                dve.wait_ge(rt_done, t + 1)
                inverse_root(dve, then, rstd[:, col], ms[:, col], rt[:, col], tmp[:, col])
                if t >= 2:
                    dve.wait_ge(turned, 2 * (t - 1))
                    dve.wait_ge(store_n[t % 2], 16 * (t // 2))
                dve.scalar_tensor_tensor(out=xs[:, t % 2, :], in0=v.xres[:, t, :], scalar=rstd[:, col], in1=gain_b[:, :],
                                         op0=ALU.mult, op1=ALU.mult).then_inc(xs_done, 1)
                if t:
                    dve.wait_ge(logit, t)
                    then(dve.tensor_tensor(lg[:, t - 1, :], v.bank[4 + (t - 1) % 2][:, 0:NG + NE], bias[:, :], ALU.add))
            dve.wait_ge(logit, NT)
            then(dve.tensor_tensor(lg[:, NT - 1, :], v.bank[4 + (NT - 1) % 2][:, 0:NG + NE], bias[:, :], ALU.add))

            def grid(x, n):
                return x[:, 0:NT * n].rearrange("p (t n) -> p t n", n=n)

            def over(x, n):
                return x[:, 0:NT].unsqueeze(2).broadcast_to([P, NT, n])

            def row(x, n):
                return x.unsqueeze(1).broadcast_to([P, NT, n])

            def first_max(values, n, order, hot, top, t1, t2):
                then(dve.tensor_reduce(top, values, AX.X, ALU.max))
                then(dve.tensor_tensor(t1, values, top.unsqueeze(2).broadcast_to([P, NT, n]), ALU.is_equal))
                then(dve.tensor_tensor(t1, t1, row(order, n), ALU.mult))
                then(dve.tensor_reduce(t2, t1, AX.X, ALU.max))
                then(dve.tensor_tensor(hot, t1, t2.unsqueeze(2).broadcast_to([P, NT, n]), ALU.is_equal))

            G, E = lg[:, :, 0:NG], lg[:, :, NG:].rearrange("p t (g e) -> p t g e", g=NG)
            g_hot, g_top, g_w = grid(B[2], NG), B[3][:, 0:NT], B[4][:, 0:NT]
            first_max(G, NG, f_group, g_hot, g_top, grid(B[5], NG), B[6][:, 0:NT])
            dve.tensor_tensor(grid(B[0], NG), G, g_top.unsqueeze(2).broadcast_to([P, NT, NG]), ALU.subtract).then_inc(x_exp, 1)
            dve.wait_ge(exped, 1)
            then(dve.tensor_reduce(g_w, grid(B[1], NG), AX.X, ALU.add))
            then(dve.reciprocal(g_w, g_w))
            four = "p (t g e) -> p t g e"
            masked = A[0][:, :].rearrange(four, t=NT, g=NG)
            eg = grid(B[7], NE8)
            for t in range(NT):
                done(dve.tensor_tensor(masked[:, t], E[:, t], g_hot[:, t].unsqueeze(2).broadcast_to([P, NG, NE8]), ALU.mult))
            dve.wait_ge(link, done(dve.memset(tmp[:, :], 0.0)))
            then(dve.tensor_reduce(eg, masked.rearrange("p t g e -> p t e g"), AX.X, ALU.add))
            hot = [grid(B[8], NE8), grid(B[9], NE8)]
            first_max(eg, NE8, f_expert, hot[0], ss[:, :], grid(B[5], NE8), B[6][:, 0:NT])
            then(dve.scalar_tensor_tensor(out=eg, in0=hot[0], scalar=-3e38, in1=eg, op0=ALU.mult, op1=ALU.add))
            first_max(eg, NE8, f_expert, hot[1], ms[:, :], grid(B[5], NE8), B[6][:, 0:NT])
            dve.tensor_tensor(B[10][:, 0:NT], ms[:, :], ss[:, :], ALU.subtract).then_inc(x_exp, 1)
            dve.wait_ge(exped, 2)
            then(dve.tensor_scalar(rt[:, :], B[11][:, 0:NT], 1.0, None, ALU.add))
            then(dve.reciprocal(rt[:, :], rt[:, :]))
            then(dve.tensor_tensor(v.e_w[:, 0, :], rt[:, :], g_w, ALU.mult))
            then(dve.tensor_tensor(v.e_w[:, 1, :], v.e_w[:, 0, :], B[11][:, 0:NT], ALU.mult))
            pick = [A[1], A[2]]
            for k in range(TOPK):
                for t in range(NT):
                    done(dve.tensor_tensor(pick[k][:, :].rearrange(four, t=NT, g=NG)[:, t], hot[k][:, t].unsqueeze(1).broadcast_to([P, NG, NE8]),
                                           g_hot[:, t].unsqueeze(2).broadcast_to([P, NG, NE8]), ALU.mult))
            dve.wait_ge(link, done(dve.memset(tmp[:, :], 0.0)))
            dve.tensor_tensor(A[3][:, :], A[1][:, :], A[2][:, :], ALU.add).then_inc(chosen, 1)
            dve.wait_ge(ranked, 1)
            count, blocks, upto = A[4][:, 0:NE], A[5][:, 0:NE], A[6][:, 0:NE]
            then(dve.tensor_copy(count, v.bank[1][:, 0:NE]))
            c3 = cmp_[:, 0:NE * NT].rearrange("p (e n) -> p e n", n=NT)
            then(dve.tensor_tensor(c3, count.unsqueeze(2).broadcast_to([P, NE, NT]), f_tile.unsqueeze(1).broadcast_to([P, NE, NT]), ALU.is_gt))
            then(dve.tensor_reduce(blocks, c3, AX.X, ALU.add))
            then(dve.tensor_tensor_scan(upto, ones[:, 0:NE], blocks, 0.0, ALU.mult, ALU.add))
            c3 = cmp_[0:1, :].rearrange("p (b e) -> p b e", e=NE)
            then(dve.tensor_tensor(c3, upto[0:1].unsqueeze(1).broadcast_to([1, NSLOT_BLK, NE]),
                                   f_block[0:1].unsqueeze(2).broadcast_to([1, NSLOT_BLK, NE]), ALU.is_le))
            then(dve.tensor_reduce(A[7][0:1, 0:NSLOT_BLK], c3, AX.X, ALU.add))
            then(dve.tensor_scalar(v.blk_e[:, :], A[7][0:1, 0:NSLOT_BLK], float(NE - 1), None, ALU.min))
            then(dve.tensor_scalar(A[8][0:1, 0:NBLK // 2], f_turn[0:1], upto[0:1, NE - 1:NE], None, ALU.is_lt))
            then(dve.tensor_reduce(A[9][0:1, 0:1], A[8][0:1, 0:NBLK // 2], AX.X, ALU.add))
            then(dve.tensor_copy(v.turns[:, 0:1], A[9][0:1, 0:1]))
            then(dve.tensor_tensor(blocks, upto, blocks, ALU.subtract))
            then(dve.tensor_scalar(blocks, blocks, float(P), None, ALU.mult))
            r3 = v.bank[0][:, 0:NT * NE].rearrange("p (t e) -> p t e", e=NE)
            s3 = A[10][:, :].rearrange("p (t e) -> p t e", e=NE)
            then(dve.tensor_tensor(s3, r3, blocks.unsqueeze(1).broadcast_to([P, NT, NE]), ALU.add))
            for k in range(TOPK):
                p3 = pick[k][:, :].rearrange("p (t e) -> p t e", e=NE)
                then(dve.tensor_tensor(p3, p3, s3, ALU.mult))
                then(dve.tensor_reduce(B[k][:, 0:NT], p3, AX.X, ALU.add))
                ins = dve.tensor_copy(v.dest[:, k, :], B[k][:, 0:NT])
                if k:
                    ins.then_inc(placed, 1)
                else:
                    then(ins)

        @block.tensor
        def _(pe):
            pe.wait_ge(const_in, 128)
            for t in range(NT):
                pe.wait_ge(xs_done, t + 1)
                for h in range(2):
                    n = 2 * t + h
                    if n >= 4:
                        pe.wait_ge(xT_done, n - 3)
                    for c in range(4):
                        k = 4 * h + c
                        mm = pe.transpose(v.bank[n % 4][:, c * P:(c + 1) * P], xs[:, t % 2, k * P:(k + 1) * P], v.ident[:, :])
                    mm.then_inc(turned, 1)
                pe.wait_ge(xT_done, 2 * t + 2)
                if t >= 2:
                    pe.wait_ge(link, logit_links(t - 2))
                for k in range(ND):
                    mm = pe.matmul(v.bank[4 + t % 2][:, 0:NG + NE], xT[:, t % 2, k, :], wr[:, k, :], start=(k == 0), stop=(k == ND - 1))
                mm.then_inc(logit, 1)
            pe.wait_ge(chosen, 1)
            pe.wait_ge(ones_set, 1)
            M = A[3][:, :].rearrange("p (t e) -> p t e", e=NE)
            for t in range(NT):
                out = v.bank[0][:, t * NE:(t + 1) * NE]
                for j in range(t):
                    pe.matmul(out, ones[:, :], M[:, j, :], start=(j == 0), stop=False)
                pe.matmul(out, upper[:, :], M[:, t, :], start=(t == 0), stop=True)
            for j in range(NT):
                mm = pe.matmul(v.bank[1][:, 0:NE], ones[:, :], M[:, j, :], start=(j == 0), stop=(j == NT - 1))
            mm.then_inc(ranked, 1)


def logit_links(t):
    return 5 * (t + 2) + t + 1


def experts_stage(v):
    nc, at, sem, d = v.nc, v.mem.at, v.sem, v.d
    TILES, SLOTS, COLS = 6, 4, 4 * N
    SHARE = 1280
    HALF = FF // 2
    raw = [at(f"w_raw{r}", ACTS + 8 * r, [P, COLS]) for r in range(TILES)]
    o = ACTS + 8 * TILES
    hi = [at(f"w_hi{s}", o + 8 * s, [P, COLS], F32R) for s in range(SLOTS)]
    lo = [at(f"w_lo{s}", o + 8 * (SLOTS + s), [P, COLS], F32R) for s in range(SLOTS)]
    o += 16 * SLOTS
    hid = at("hid", o, [P, 2, HALF])
    silu = at("silu", o + 2, [P, 2, HALF])
    hidT = [at(f"hidT{i}", o + 4 + 2 * i, [P, FF // P, P], F32R) for i in range(2)]
    y = [at(f"y{i}", o + 8 + 4 * i, [P, D]) for i in range(2)]
    xg = [at(f"xg{i}", RINGS + 4 * i, [P, D]) for i in range(2)]
    xT = [[at(f"xT{i}{j}", RINGS + 8 + 8 * i + 4 * j, [P, ND, P], F32R) for j in range(2)] for i in range(2)]
    warm = at("warm", CONST + 5.75, [P, 8])
    idx = [at(f"idx{i}", CONST + 6 + 0.125 * i, [P, 2], I32) for i in range(4)]
    b_x, b_h, b_hT, pair_y = v.bank[0:2], v.bank[2:4], v.bank[4:6], v.pair[3]

    landed = [sem(f"w_landed{r}") for r in range(TILES)]
    hi_done, lo_dve, lo_pool, w_used = sem("w_hi_done"), sem("w_lo_dve"), sem("w_lo_pool"), sem("w_used")
    x_in, y_out = [sem(f"x_in{i}") for i in range(2)], [sem(f"y_out{i}") for i in range(2)]
    idx_set, idx_seen, x_turned, x_hi, x_lo = (sem(n) for n in ("idx_set", "idx_seen", "x_turned", "x_hi", "x_lo"))
    silu_done, hid_done, h_turned, hidT_hi, hidT_lo, y_read = (sem(n) for n in ("silu_done", "hid_done", "h_turned", "hidT_hi", "hidT_lo", "y_read"))
    y_zero, y_seen = sem("y_zero"), sem("y_seen")

    def turns(eng):
        return eng.value_load(v.turns[0:1, 0:1], min_val=1, max_val=NBLK // 2)

    def slot(p, r):
        return (TILES * p + r) % SLOTS

    def low(eng, r, p, done):
        s, c = slot(p, r), (slice(0, SHARE) if done is lo_dve else slice(SHARE, COLS))
        eng.tensor_tensor(lo[s][:, c], raw[r][:, c], hi[s][:, c].bitcast(F32), ALU.subtract).then_inc(done, 1)

    def wait_split(eng, n):
        eng.wait_ge(lo_dve, n + 3)
        eng.wait_ge(lo_pool, n + 3)

    with nc.Block() as block:
        @block.sync
        def _(sp):
            n_turns = turns(sp)

            def load(e, r):
                if r < 4:
                    src = d["w3" if r % 2 else "w1"][bass.ds(e, 1), :, r // 2 * HALF:(r // 2 + 1) * HALF]
                else:
                    src = d["w2"][bass.ds(e, 1), (r - 4) * HALF:(r - 3) * HALF, :]
                n = HALF if r < 4 else D
                sp.dma_start(raw[r][:, :].rearrange("p (k n) -> p k n", n=n), src.rearrange("o (k p) n -> p (o k) n", p=P)).then_inc(landed[r], 16)

            def expert(b):
                return sp.value_load(v.blk_e[0:1, b], min_val=0, max_val=NE - 1)

            e = expert(slice(0, 1))
            for r in range(4):
                load(e, r)
            with sp.Fori(0, n_turns) as i:
                for p in range(2):
                    b = 2 * i + p
                    e = expert(bass.ds(b, 1))
                    for r in (4, 5):
                        wait_split(sp, TILES * b + r - TILES)
                        load(e, r)
                    e = expert(bass.ds(b + 1, 1))
                    for r in range(4):
                        wait_split(sp, TILES * b + r)
                        load(e, r)

        @block.gpsimd
        def _(pool):
            n_turns = turns(pool)

            def index(j, slots, count):
                pool.tensor_copy(idx[j][:, :], slots).then_inc(idx_set, 1)
                pool.wait_ge(idx_set, count)
                pool.sem_inc(idx_seen, 1)

            def gather(p):
                pool.indirect_dma_start(xg[p][:, :], None, d["xn"], bass.IndirectOffsetOnAxis(ap=idx[p][:, 0:1], axis=0)).then_inc(x_in[p], 16)

            def scatter(p):
                pool.indirect_dma_start(d["y"], bass.IndirectOffsetOnAxis(ap=idx[2 + p][:, 1:2], axis=0), y[p][:, :], None).then_inc(y_out[p], 16)

            index(0, v.slots[:, 0, :], 1)
            gather(0)
            for p in range(2):
                pool.memset(y[p][:, :], 0.0).then_inc(y_zero, 1)
                pool.wait_ge(y_zero, p + 1)
                index(2 + p, v.slots[:, NBLK + p, :], 2 + p)
                scatter(p)
            pool.sem_inc(lo_pool, 2)
            for r in range(4):
                pool.wait_ge(hi_done, r + 1)
                low(pool, r, 0, lo_pool)
            with pool.Fori(0, n_turns) as i:
                for p in range(2):
                    b = 2 * i + p
                    pool.wait_ge(x_turned, 2 * b + 2)
                    index(1 - p, v.slots[:, bass.ds(b + 1, 1), :].rearrange("p o c -> p (o c)"), 2 * b + 4)
                    gather(1 - p)
                    for m in range(4, 10):
                        pool.wait_ge(hi_done, TILES * b + m + 1)
                        low(pool, m % TILES, (p + m // TILES) % 2, lo_pool)
                    pool.wait_ge(y_read, b + 2)
                    pool.wait_ge(y_out[p], 16 * i + 16)
                    pool.sem_inc(y_seen, 1)
                    index(2 + p, v.slots[:, bass.ds(b, 1), :].rearrange("p o c -> p (o c)"), 2 * b + 5)
                    scatter(p)
            for p in range(2):
                pool.wait_ge(y_out[p], 16 * n_turns + 16)

        @block.scalar
        def _(act):
            n_turns = turns(act)

            def high(r, p):
                s = slot(p, r)
                act.activation(hi[s][:, :], raw[r][:, :], ACT.Copy).then_inc(hi_done, 1)

            def x_high(p, count):
                for c in range(2):
                    act.wait_ge(x_turned, count + c + 1)
                    act.activation(xT[p][0][:, 4 * c:4 * c + 4, :], b_x[c].rearrange("p (k t) -> p k t", t=P), ACT.Copy).then_inc(x_hi, 1)

            def gate(half, b):
                act.wait_ge(w_used, TILES * b + 2 * half + 2)
                act.wait_ge(hid_done, 2 * b + half + 1)
                act.activation(silu[:, half, :], b_h[half][:, 0:HALF], ACT.Silu).then_inc(silu_done, 1)

            def h_high(half, b):
                act.wait_ge(h_turned, 2 * b + half + 1)
                act.activation(hidT[0][:, 2 * half:2 * half + 2, :], b_hT[half][:, 0:HALF].rearrange("p (k t) -> p k t", t=P),
                               ACT.Copy).then_inc(hidT_hi, 1)

            for r in range(4):
                act.wait_ge(landed[r], 16)
                high(r, 0)
            x_high(0, 0)
            with act.Fori(0, n_turns) as i:
                act.activation(warm[:, :], v.e_w[:, 0, :], ACT.Silu)
                for p in range(2):
                    b = 2 * i + p

                    def split(r, q):
                        act.wait_ge(landed[r], 16 * b + 16 + 16 * q)
                        act.wait_ge(w_used, TILES * b + TILES * q + r - 3)
                        high(r, (p + q) % 2)

                    split(4, 0)
                    gate(0, b)
                    split(5, 0)
                    h_high(0, b)
                    split(0, 1)
                    gate(1, b)
                    split(1, 1)
                    h_high(1, b)
                    x_high(1 - p, 2 * b + 2)
                    split(2, 1)
                    split(3, 1)

        @block.vector
        def _(dve):
            n_turns = turns(dve)

            def x_low(p, count):
                for c in range(2):
                    dve.wait_ge(x_hi, count + c + 1)
                    dve.tensor_tensor(xT[p][1][:, 4 * c:4 * c + 4, :], b_x[c].rearrange("p (k t) -> p k t", t=P),
                                      xT[p][0][:, 4 * c:4 * c + 4, :].bitcast(F32), ALU.subtract).then_inc(x_lo, 1)

            def times(half, b):
                dve.wait_ge(silu_done, 2 * b + half + 1)
                dve.tensor_tensor(hid[:, half, :], silu[:, half, :], b_h[half][:, HALF:], ALU.mult).then_inc(hid_done, 1)

            def h_low(half, b):
                dve.wait_ge(hidT_hi, 2 * b + half + 1)
                dve.tensor_tensor(hidT[1][:, 2 * half:2 * half + 2, :], b_hT[half][:, 0:HALF].rearrange("p (k t) -> p k t", t=P),
                                  hidT[0][:, 2 * half:2 * half + 2, :].bitcast(F32), ALU.subtract).then_inc(hidT_lo, 1)

            dve.sem_inc(hid_done, 2)
            dve.sem_inc(hidT_lo, 2)
            dve.sem_inc(lo_dve, 2)
            dve.sem_inc(y_read, 1)
            for r in range(4):
                dve.wait_ge(hi_done, r + 1)
                low(dve, r, 0, lo_dve)
            x_low(0, 0)
            with dve.Fori(0, n_turns) as i:
                for p in range(2):
                    b = 2 * i + p

                    def split(r, q):
                        dve.wait_ge(hi_done, TILES * b + TILES * q + r + 1)
                        low(dve, r, (p + q) % 2, lo_dve)

                    split(4, 0)
                    times(0, b)
                    split(5, 0)
                    h_low(0, b)
                    split(0, 1)
                    times(1, b)
                    h_low(1, b)
                    split(1, 1)
                    x_low(1 - p, 2 * b + 2)
                    split(2, 1)
                    dve.wait_ge(w_used, TILES * b + TILES)
                    dve.wait_ge(y_out[p], 16 * i + 16)
                    dve.tensor_copy(y[p][:, :], pair_y[:, :]).then_inc(y_read, 1)
                    split(3, 1)

        @block.tensor
        def _(pe):
            n_turns = turns(pe)

            def three(out, left, right, first, last):
                pe.matmul(out, left[0], right[0], start=first, stop=False)
                pe.matmul(out, left[0], right[1], start=False, stop=False)
                return pe.matmul(out, left[1], right[0], start=False, stop=last)

            def turn_x(p):
                for c in range(2):
                    for k in range(4 * c, 4 * c + 4):
                        mm = pe.transpose(b_x[c][:, k % 4 * P:(k % 4 + 1) * P], xg[p][:, k * P:(k + 1) * P], v.ident[:, :])
                    mm.then_inc(x_turned, 1)

            def up(r, p, b):
                s = slot(p, r)
                wait_split(pe, TILES * b + r)
                for k in range(ND):
                    c = slice(k * HALF, (k + 1) * HALF)
                    mm = three(b_h[r // 2][:, r % 2 * HALF:(r % 2 + 1) * HALF], [x[:, k, :] for x in xT[p]], [w[s][:, c] for w in (hi, lo)],
                               k == 0, k == ND - 1)
                mm.then_inc(w_used, 1)

            def turn_h(half, b):
                pe.wait_ge(hid_done, 2 * b + half + 3)
                pe.wait_ge(hidT_lo, 2 * b + half + 1)
                for k in range(2):
                    mm = pe.transpose(b_hT[half][:, k * P:(k + 1) * P], hid[:, half, k * P:(k + 1) * P], v.ident[:, :])
                mm.then_inc(h_turned, 1)

            def down(r, p, b):
                s, half = slot(p, r), r - 4
                wait_split(pe, TILES * b + r)
                pe.wait_ge(hidT_lo, 2 * b + half + 3)
                for k in range(2):
                    for c in range(D // N):
                        cols = slice(k * D + c * N, k * D + (c + 1) * N)
                        mm = three(pair_y[:, c * N:(c + 1) * N], [h[:, 2 * half + k, :] for h in hidT], [w[s][:, cols] for w in (hi, lo)],
                                   half + k == 0, half + k == 2)
                mm.then_inc(w_used, 1)

            pe.wait_ge(x_in[0], 16)
            turn_x(0)
            with pe.Fori(0, n_turns) as i:
                for p in range(2):
                    b = 2 * i + p
                    pe.wait_ge(x_lo, 2 * b + 2)
                    pe.wait_ge(hid_done, 2 * b + 1)
                    up(0, p, b)
                    up(1, p, b)
                    pe.wait_ge(hid_done, 2 * b + 2)
                    up(2, p, b)
                    turn_h(0, b)
                    up(3, p, b)
                    pe.wait_ge(y_read, b + 1)
                    down(4, p, b)
                    turn_h(1, b)
                    pe.wait_ge(x_in[1 - p], 16 * i + 16 + 16 * p)
                    turn_x(1 - p)
                    down(5, p, b)


def combine_stage(v):
    nc, at, sem, d = v.nc, v.mem.at, v.sem, v.d
    SLOTS = 3
    y = at("y_rows", ACTS, [P, SLOTS, TOPK, D])
    t1 = at("t1", ACTS + 32, [P, 2, D])
    y_in, link, added = [sem(f"y_in{i}") for i in range(SLOTS)], sem("dve_link"), sem("added")
    with nc.Block() as block:
        @block.sync
        def _(sp):
            rows_of = d["y"].rearrange("(k t p) c -> t p k c", p=P, t=NT)
            for t in range(NT):
                if t >= SLOTS:
                    sp.wait_ge(added, t - SLOTS + 1)
                sp.dma_start(y[:, t % SLOTS, :, :], rows_of[t, :, 0:TOPK, :]).then_inc(y_in[t % SLOTS], 16)

        @block.vector
        def _(dve):
            done, then = chain(dve, link)
            for t in range(NT):
                s = t % SLOTS
                dve.wait_ge(y_in[s], 16 * (t // SLOTS + 1))
                then(dve.tensor_scalar(t1[:, t % 2, :], y[:, s, 0, :], v.e_w[:, 0, t:t + 1], None, ALU.mult))
                then(dve.scalar_tensor_tensor(out=t1[:, t % 2, :], in0=y[:, s, 1, :], scalar=v.e_w[:, 1, t:t + 1], in1=t1[:, t % 2, :],
                                              op0=ALU.mult, op1=ALU.add))
                dve.tensor_tensor(v.xres[:, t, :], v.xres[:, t, :], t1[:, t % 2, :], ALU.add).then_inc(added, 1)


QA_W, KVA_W, B_W = AH * HD, 2 * AKV * HD, BH * HD
COL2 = dict(zip(("qa", "kva", "qb", "kb", "vb", "f"), np.cumsum([0, QA_W, KVA_W, B_W, B_W, B_W]).tolist()))
KVF_W = KVA_W + BH


def block2_tensors(v):
    at = v.mem.at
    v.qa = at("qa", FREE, [P, NT, QA_W])
    v.kvf = at("kvf", FREE + 16, [P, NT, KVF_W])
    v.vb = at("vb", FREE + 24.5, [P, NT, B_W])
    v.qb = at("qb_aug", FREE + 40.5, [P, NT, BH, BAUG])
    v.kb = at("kb_aug", FREE + 61.5, [P, NT, BH, BAUG])
    v.log_f = at("log_f", CONST + 7.5, [P, NT, BH])


def project2_stage(v):
    nc, at, sem, d = v.nc, v.mem.at, v.sem, v.d
    block2_tensors(v)
    act_ops, w = (v.act_hi, v.act_lo), d["w_in_2"]
    order = ["kva", "qa", "qb", "kb", "vb"]
    index = {name: g for g, name in enumerate(order)}
    tiles = [Tile("nat", [(rows(w, k, COL2["kva"], COL2["kva"] + KVA_W), 0, KVA_W), (rows(w, k, COL2["f"], COL2["f"] + BH), KVA_W, KVF_W)],
                  KVF_W, act_ops, k, k == 0, k == ND - 1) for k in range(ND)]
    for name in order[1:]:
        tiles += group("nat", w, ND, COL2[name], COL2[name] + N, act_ops)

    gains = at("gains2", CONST + 3, [P, 4, HD])
    bias = at("b_forget", CONST + 2, [P, BH])
    z, e, u, dif, corr = (at(f"forget{i}", CONST + kb, [P, NT, BH]) for i, kb in enumerate((2.25, 2.5, 2.75, 7, 7.25)))

    def heads_of(name, dst, heads):
        return Heads(v, name, dst, heads, CONST + 4)

    plain = "p (h d) -> p h d"
    heads = {"kva": heads_of("ka", lambda t: v.kvf[:, t, 0:AKV * HD].rearrange(plain, d=HD), AKV),
             "qa": heads_of("qa", lambda t: v.qa[:, t, :].rearrange(plain, d=HD), AH),
             "qb": heads_of("qb", lambda t: v.qb[:, t, :, 0:HD], BH),
             "kb": heads_of("kb", lambda t: v.kb[:, t, :, 0:HD], BH)}
    ready, free, link, tables = sem("bank_ready"), sem("bank_free"), sem("dve_link"), sem("tables")
    saved = sem("xres_saved")
    e_arg, e_done, u_set, ln_done = sem("e_arg"), sem("e_done"), sem("u_set"), sem("ln_done")

    def load_tables(sp):
        for i, name in enumerate(("k_norm_a_2", "q_norm_a_2", "q_norm_b_2", "k_norm_b_2")):
            sp.dma_start(gains[:, i, :], d[name].broadcast_to([P, HD])).then_inc(tables, 16)
        sp.dma_start(bias[:, :], d["b_forget_2"].broadcast_to([P, BH])).then_inc(tables, 16)

    def save_xres(sp):
        sp.dma_start(d["xres"].rearrange("(t p) c -> p t c", p=P), v.xres[:, :, :]).then_inc(saved, 16)

    def forget_exp(act):
        act.wait_ge(e_arg, 1)
        act.activation(e[:, :, :], e[:, :, :], ACT.Exp).then_inc(e_done, 1)

    def forget_ln(act):
        act.wait_ge(u_set, 1)
        act.activation(z[:, :, :], u[:, :, :], ACT.Ln).then_inc(ln_done, 1)

    steps = {8 + 2: [forget_exp], 8 + 3: [forget_ln]}
    for name, h in heads.items():
        steps.setdefault(8 * (index[name] + 1) + (4 if name == "kva" else 6), []).append(h.root)

    def dve_program(dve):
        done, then = chain(dve, link)
        dve.wait_ge(tables, 80)
        for i in (1, 2):
            then(dve.tensor_scalar(gains[:, i, :], gains[:, i, :], HD ** -0.5, None, ALU.mult))
        g = index["kva"]
        for t in range(NT):
            dve.wait_ge(ready, 8 * g + t + 1)
            dve.tensor_copy(v.kvf[:, t, :], v.bank[t][:, 0:KVF_W]).then_inc(free, 1)
        dve.wait_ge(free, 8 * g + NT)
        then(dve.tensor_tensor(z[:, :, :], v.kvf[:, :, KVA_W:], bias[:, :].unsqueeze(1).broadcast_to([P, NT, BH]), ALU.add))
        dve.scalar_tensor_tensor(out=e[:, :, :], in0=z[:, :, :], scalar=-1.0, in1=z[:, :, :], op0=ALU.mult, op1=ALU.min).then_inc(e_arg, 1)
        then(dve.tensor_scalar(v.log_f[:, :, :], z[:, :, :], 0.0, None, ALU.min))
        dve.wait_ge(e_done, 1)
        dve.tensor_scalar(u[:, :, :], e[:, :, :], 1.0, None, ALU.add).then_inc(u_set, 1)
        dve.wait_ge(u_set, 1)
        then(dve.scalar_tensor_tensor(out=dif[:, :, :], in0=u[:, :, :], scalar=-1.0, in1=e[:, :, :], op0=ALU.add, op1=ALU.subtract))
        then(dve.reciprocal(corr[:, :, :], u[:, :, :]))
        then(dve.tensor_tensor(corr[:, :, :], dif[:, :, :], corr[:, :, :], ALU.mult))
        dve.wait_ge(ln_done, 1)
        then(dve.tensor_tensor(corr[:, :, :], corr[:, :, :], z[:, :, :], ALU.subtract))
        then(dve.tensor_tensor(v.log_f[:, :, :], v.log_f[:, :, :], corr[:, :, :], ALU.add))
        for i, name in enumerate(("kva", "qa", "qb", "kb")):
            h, g = heads[name], index[name]
            if name == "kb":
                dve.wait_ge(saved, 16)
            if name != "kva":
                for t in range(NT):
                    dve.wait_ge(ready, 8 * g + t + 1)
                    if name == "qa":
                        dve.tensor_copy(v.qa[:, t, :].rearrange("p (a g d) -> p g a d", g=AKV, d=HD),
                                        v.bank[t].rearrange("p (g a d) -> p g a d", g=AKV, d=HD)).then_inc(free, 1)
                    else:
                        h.take(dve, then, v.bank[t][:, :], t, free)
                dve.wait_ge(free, 8 * g + NT)
            for t in range(NT):
                h.stat(dve, then, t)
            h.mean(dve)
            h.inverse(dve, then)
            for t in range(NT):
                h.scale(dve, then, t, gains[:, i, :])
        g = index["vb"]
        for t in range(NT):
            dve.wait_ge(ready, 8 * g + t + 1)
            dve.tensor_copy(v.vb[:, t, :], v.bank[t][:, :]).then_inc(free, 1)

    dense_stage(v, tiles, dve_program, steps, sp_before=load_tables, sp_steps={RING: [save_xres]}, sems=(ready, free))


class ForgetUnit:

    def __init__(self, h, i):
        self.h, self.i, self.window = h, i, False
        self.width, self.exps = (i + 1) * P, 1
        self.blocks = [(j * P, j, 0, j == 0, j == i) for j in range(i + 1)]


class WindowUnit:

    def __init__(self, g, i):
        self.g, self.i, self.window = g, i, True
        self.keys = min(2, i + 1) * P
        self.width, self.exps = self.keys * (AH // AKV), AH // AKV + 1
        first = max(0, i - 1)
        self.blocks = [(a * self.keys + (j - first) * P, j, a, j == first, j == i) for a in range(AH // AKV) for j in range(first, i + 1)]


def attention2_stage(v):
    nc, at, sem, d = v.nc, v.mem.at, v.sem, v.d
    k_hi, k_both = at("kb_hi", ACTS, [P, BH, S], F32R), at("kb_both", ACTS + 32, [P, BH, S], F32R)
    o = FREE + 82.5
    q_hi = [at(f"qb_hi{i}", o + 8 * i, [P, BH, P], F32R) for i in range(2)]
    q_both = [at(f"qb_both{i}", o + 8 * i + 4, [P, BH, P], F32R) for i in range(2)]
    qaT = [at(f"qaT{g}", o + 16 + 2 * g, [P, AH // AKV, P]) for g in range(AKV)]
    kaT = at("kaT", o + 20, [P, S])
    probs, aT = at("probs", RINGS, [P, 3, S]), at("probsT", RINGS + 12, [P, 2, S])
    alibi = [at("alibi0", o + 24, [P, AH // AKV, 2 * P]), at("alibi1", RINGS + 20, [P, AH // AKV, 2 * P])]
    v.out_a, v.out_b = v.qa, v.qb[:, :, :, :].rearrange("p t h c -> p t (h c)")
    small = CONST + 2
    upto, ones = at("upto", small, [P, P]), at("ones", small + 0.5, [P, P])
    sinks = at("sinks", small + 1, [P, AH])
    mraw, nmax, snk, sums, inv = (at(n, small + 1.25 + 0.125 * i, [P, 4, 4]) for i, n in enumerate(("mraw", "nmax", "snk", "sums", "inv")))
    c_hi = at("c_hi", small + 2, [P, NT, BH], F32R)
    c_lo = at("c_lo", small + 2.25, [P, NT, BH])
    R, R_hi = at("R", RINGS, [P, NT, BH, NT]), at("R_hi", RINGS + 2, [P, NT, BH, NT], F32R)

    HALF = AH // AKV
    units = []
    for i in range(NT):
        for g in range(AKV):
            units += [ForgetUnit(h, i) for h in range(4 * g, 4 * g + 4)] + [WindowUnit(g, i)]
    n_units, per_tile = len(units), len(units) // NT
    exped_upto = np.cumsum([0] + [u.exps for u in units]).tolist()
    halves = [-(-u.width // N) for u in units]
    high_upto = np.cumsum([0] + [n - 1 for n in halves]).tolist()
    LOW, HIGH = v.bank[4], v.bank[5]
    AHEAD = (7, 2, -1)
    STEPS, OF_ACT, OF_DVE = 3, (4, 4, AKV + 1), (2, 2, 0)

    consts, link, cum_ready, columns = sem("consts"), sem("dve_link"), sem("cum_ready"), sem("columns")
    alibi_in, tr_ready, prep_act, prep_dve = sem("alibi_in"), sem("tr_ready"), sem("prep_act"), sem("prep_dve")
    upto_set = sem("upto_set")
    scored, maxed, exped = sem("scored"), sem("maxed"), sem("exped")
    turned_low, turned_high, low_read, high_read = sem("turned_low"), sem("turned_high"), sem("low_read"), sem("high_read")
    weighed, weigh_read = sem("weighed"), sem("weigh_read")

    def prepares(p):
        for step, n in enumerate(AHEAD):
            if p >= 0 and (p + n) % per_tile == 0 and 0 < (p + n) // per_tile < NT:
                return (p + n) // per_tile, step

    def prepared(t, step):
        return sum(OF_ACT) * t + sum(OF_ACT[:step + 1]), sum(OF_DVE) * t + sum(OF_DVE[:step + 1])

    def blocks(bank, r):
        return bank[r, :].rearrange("p (a t) -> p a t", t=P)

    def tile(t):
        return slice(t * P, (t + 1) * P)

    TOP, BOTTOM = slice(0, HD), slice(HD, 2 * HD)

    with nc.Block() as block:
        @block.sync
        def _(sp):
            sp.dma_start(upto[:, :], d["upper"]).then_inc(consts, 16)
            sp.dma_start(sinks[:, :], d["sink_logits_2"].broadcast_to([P, AH])).then_inc(consts, 16)
            for g in range(AKV):
                sp.dma_start(alibi[g][:, :, :], d["alibi"][:, g * HALF:(g + 1) * HALF, :]).then_inc(alibi_in, 16)

        @block.scalar
        def _(act):
            def prepare(t, step):
                for b, bank in enumerate((LOW, HIGH)):
                    act.wait_ge(tr_ready, 2 * STEPS * t + 2 * step + b + 1)
                    heads = slice(4 * b, 4 * b + 4)
                    if step == 0:
                        moves = ((q_hi[t % 2][0:BAUG, heads, :], bank, slice(0, BAUG)), (q_both[t % 2][TOP, heads, :], bank, TOP))
                    elif step == 1:
                        moves = ((k_hi[0:BAUG, heads, tile(t)], bank, slice(0, BAUG)), (k_both[BOTTOM, heads, tile(t)], bank, TOP))
                    elif b == 0:
                        moves = tuple((qaT[g][r, :, :], bank, r) for g, r in enumerate((TOP, BOTTOM)))
                    else:
                        moves = ((kaT[:, tile(t)].rearrange("p (a t) -> p a t", t=P), bank[:, 0:P], slice(0, P)),)
                    for dst, src, r in moves:
                        act.activation(dst, blocks(src, r), ACT.Copy).then_inc(prep_act, 1)

            def turn_out(p):
                act.wait_ge(turned_low, p + 1)
                if p >= 2:
                    act.wait_ge(weighed, p - 1)
                c = min(units[p].width, N)
                act.activation(aT[:, p % 2, :c], LOW[:, :c], ACT.Copy).then_inc(low_read, 1)

            for step in range(STEPS):
                prepare(0, step)
            for p, u in enumerate(units):
                if p >= 2:
                    turn_out(p - 2)
                act.wait_ge(maxed, p + 1)
                s, q = p % 4, probs[:, p % 3, :]
                if u.window:
                    for a in range(HALF):
                        c = slice(a * u.keys, (a + 1) * u.keys)
                        act.activation(q[:, c], q[:, c], ACT.Exp, bias=nmax[:, s, a:a + 1], accum_out=sums[:, s, a:a + 1]).then_inc(exped, 1)
                    act.activation(snk[:, s, :], snk[:, s, :], ACT.Exp).then_inc(exped, 1)
                else:
                    if p >= 3:
                        act.wait_ge(turned_low, p - 2)
                        if high_upto[p - 2]:
                            act.wait_ge(turned_high, high_upto[p - 2])
                    act.activation(q[:, :u.width], v.pair[p % 2][:, :u.width], ACT.Exp, bias=nmax[:, s, 0:1],
                                   accum_out=sums[:, s, 0:1]).then_inc(exped, 1)
                if prepares(p):
                    prepare(*prepares(p))
            for p in (n_units - 2, n_units - 1):
                turn_out(p)

        @block.vector
        def _(dve):
            done, then = chain(dve, link)

            def prepare(t, step):
                for b, bank in enumerate((LOW, HIGH)):
                    heads = slice(4 * b, 4 * b + 4)
                    if step < 2:
                        dve.wait_ge(prep_act, prepared(t, step)[0] - 2 + 2 * b)
                    if step == 0:
                        lo, hi = q_both[t % 2][BOTTOM, heads, :], q_both[t % 2][TOP, heads, :]
                    elif step == 1:
                        lo, hi = k_both[TOP, heads, tile(t)], k_hi[TOP, heads, tile(t)]
                    if step < 2:
                        dve.tensor_tensor(lo, blocks(bank, TOP), hi.bitcast(F32), ALU.subtract).then_inc(prep_dve, 1)

            def turn_out(p):
                if halves[p] < 2:
                    return
                dve.wait_ge(turned_high, high_upto[p + 1])
                if p >= 2:
                    dve.wait_ge(weighed, p - 1)
                c = units[p].width
                dve.tensor_copy(aT[:, p % 2, N:c], HIGH[:, :c - N]).then_inc(high_read, 1)

            def out(p):
                u, s = units[p], p % 4
                dve.wait_ge(weighed, p + 1)
                if u.window:
                    then(dve.tensor_tensor(inv[:, s, :], sums[:, s, :], snk[:, s, :], ALU.add))
                    then(dve.reciprocal(inv[:, s, :], inv[:, s, :]))
                    c = u.g * HALF * HD
                    dve.tensor_tensor(v.out_a[:, u.i, c:c + HALF * HD].rearrange("p (a d) -> p a d", d=HD),
                                      v.bank[6 + p % 2].rearrange("p (a g d) -> p a g d", g=AKV, d=HD)[:, :, u.g, :],
                                      inv[:, s, :].unsqueeze(2).broadcast_to([P, HALF, HD]), ALU.mult).then_inc(weigh_read, 1)
                else:
                    then(dve.reciprocal(inv[:, s, 0:1], sums[:, s, 0:1]))
                    dve.tensor_scalar(v.out_b[:, u.i, u.h * HD:(u.h + 1) * HD], v.bank[6 + p % 2][:, u.h % 2 * HD:(u.h % 2 + 1) * HD], inv[:, s, 0:1], None,
                                      ALU.mult).then_inc(weigh_read, 1)

            def col(x, c):
                return x[:, :, :, HD + c:HD + c + 1].rearrange("p t h o -> p t (h o)")

            dve.wait_ge(consts, 32)
            done(dve.memset(ones[:, :], 1.0))
            dve.tensor_tensor(upto[:, :], upto[:, :], v.ident[:, :], ALU.add).then_inc(upto_set, 1)
            for g, r in enumerate((BOTTOM, TOP)):
                done(dve.memset(qaT[g][r, :, :], 0.0))
            done(dve.memset(v.kb[:, :, :, HD + 4:], 0.0))
            then(dve.memset(R[:, :, :, :], 0.0))
            for x, c in ((v.qb, 0), (v.qb, 3), (v.kb, 1), (v.kb, 2)):
                done(dve.memset(col(x, c), 1.0))
            for t in range(NT):
                done(dve.memset(v.kb[:, t, :, HD + 4:].rearrange("p h (a j) -> p h a j", a=2)[:, :, :, t:t + 1], 1.0))
            dve.wait_ge(cum_ready, 1)
            own = v.bank[7][:, 0:NT * BH].rearrange("p (t h) -> p t h", h=BH)
            total = v.bank[7][:, NT * BH:2 * NT * BH].rearrange("p (t h) -> p t h", h=BH)
            then(dve.tensor_copy(c_hi[:, :, :], own))
            hi = c_hi[:, :, :].bitcast(F32)
            then(dve.tensor_tensor(c_lo[:, :, :], own, hi, ALU.subtract))
            done(dve.tensor_copy(col(v.qb, 1), hi))
            done(dve.tensor_copy(col(v.qb, 2), c_lo[:, :, :]))
            done(dve.tensor_scalar(col(v.kb, 0), hi, -1.0, None, ALU.mult))
            done(dve.tensor_scalar(col(v.kb, 3), c_lo[:, :, :], -1.0, None, ALU.mult))
            for i in range(1, NT):
                then(dve.tensor_tensor(R[:, i, :, 0:i], R[:, i - 1, :, 0:i], total[:, i - 1, :].unsqueeze(2).broadcast_to([P, BH, i]), ALU.add))
            then(dve.tensor_copy(R_hi[:, :, :, :], R[:, :, :, :]))
            done(dve.tensor_copy(v.qb[:, :, :, HD + 4:HD + 4 + NT], R_hi[:, :, :, :].bitcast(F32)))
            dve.tensor_tensor(v.qb[:, :, :, HD + 4 + NT:], R[:, :, :, :], R_hi[:, :, :, :].bitcast(F32), ALU.subtract).then_inc(columns, 1)
            for step in range(STEPS):
                prepare(0, step)
            dve.wait_ge(alibi_in, 32)
            dve.wait_ge(columns, 1)
            for p, u in enumerate(units):
                dve.wait_ge(scored, p + 1)
                s, q = p % 4, probs[:, p % 3, :]
                if u.window:
                    if p >= 3:
                        dve.wait_ge(turned_low, p - 2)
                        if high_upto[p - 2]:
                            dve.wait_ge(turned_high, high_upto[p - 2])
                    sink = sinks[:, u.g * HALF:(u.g + 1) * HALF]
                    for a in range(HALF):
                        c = slice(a * u.keys, (a + 1) * u.keys)
                        ins = dve.tensor_tensor_reduce(q[:, c], v.pair[p % 2][:, c], alibi[u.g][:, a, 2 * P - u.keys:], 1.0, -3.0e38,
                                                       ALU.add, ALU.max, mraw[:, s, a:a + 1])
                        (done if a < HALF - 1 else then)(ins)
                    then(dve.tensor_tensor(mraw[:, s, :], mraw[:, s, :], sink, ALU.max))
                    then(dve.tensor_scalar(nmax[:, s, :], mraw[:, s, :], -1.0, None, ALU.mult))
                    dve.tensor_tensor(snk[:, s, :], sink, nmax[:, s, :], ALU.add).then_inc(maxed, 1)
                else:
                    dve.tensor_reduce(nmax[:, s, 0:1], v.pair[p % 2][:, :u.width], AX.X, ALU.max, negate=True).then_inc(maxed, 1)
                if p >= 2:
                    turn_out(p - 2)
                if prepares(p):
                    prepare(*prepares(p))
                if p >= 3:
                    out(p - 3)
            turn_out(n_units - 2)
            out(n_units - 3)
            turn_out(n_units - 1)
            out(n_units - 2)
            out(n_units - 1)

        @block.tensor
        def _(pe):
            pe.wait_ge(upto_set, 1)
            logs = v.log_f[:, :, :].rearrange("p t h -> p (t h)")
            pe.matmul(v.bank[7][:, 0:NT * BH], upto[:, :], logs, start=True, stop=True)
            pe.matmul(v.bank[7][:, NT * BH:2 * NT * BH], ones[:, :], logs, start=True, stop=True).then_inc(cum_ready, 1)

            def prepare(t, step):
                for b, bank in enumerate((LOW, HIGH)):
                    if step < 2:
                        src, n = (v.qb, v.kb)[step], BAUG
                        parts = [src[:, t, 4 * b + a, :] for a in range(4)]
                    elif b == 0:
                        n, parts = P, [v.qa[:, t, a * P:(a + 1) * P] for a in range(HALF)]
                    else:
                        n, parts = P, [v.kvf[:, t, 0:P]]
                    for a, x in enumerate(parts):
                        mm = pe.transpose(bank[0:n, a * P:(a + 1) * P], x, v.ident[:, :])
                    mm.then_inc(tr_ready, 1)

            def wait_prepared(t, step):
                n_act, n_dve = prepared(t, step)
                pe.wait_ge(prep_act, n_act)
                pe.wait_ge(prep_dve, n_dve)

            def scores(p):
                u = units[p]
                if p % per_tile == 0:
                    wait_prepared(u.i, 1)
                if p % per_tile == 4:
                    wait_prepared(u.i, 2)
                if p >= 2:
                    pe.wait_ge(exped, exped_upto[p - 1])
                pair, s = v.pair[p % 2], u.i % 2
                if u.window:
                    for a in range(HALF):
                        mm = pe.matmul(pair[:, a * u.keys:(a + 1) * u.keys], qaT[u.g][:, a, :], kaT[:, (u.i + 1) * P - u.keys:(u.i + 1) * P],
                                       start=True, stop=True)
                else:
                    mm = split_scores(pe, v, pair, q_hi[s][0:BAUG, u.h, :], k_hi[0:BAUG, u.h, :], q_both[s][:, u.h, :], k_both[:, u.h, :], u.width)
                mm.then_inc(scored, 1)

            def free_banks(p):
                if p >= 0:
                    pe.wait_ge(low_read, p + 1)
                    if high_upto[p + 1]:
                        pe.wait_ge(high_read, high_upto[p + 1])

            def turn(p):
                u = units[p]
                pe.wait_ge(exped, exped_upto[p + 1])
                free_banks(p - 1)
                for c in range(0, u.width, P):
                    bank = (LOW, HIGH)[c // N]
                    mm = pe.transpose(bank[:, c % N:c % N + P], probs[:, p % 3, c:c + P], v.ident[:, :])
                    if c + P == min(u.width, N):
                        mm.then_inc(turned_low, 1)
                if halves[p] > 1:
                    mm.then_inc(turned_high, 1)

            def weigh(p):
                u = units[p]
                free_banks(p)
                if p >= 2:
                    pe.wait_ge(weigh_read, p - 1)
                for c, j, a, first, last in u.blocks:
                    if u.window:
                        vals = v.kvf[:, j, AKV * HD:2 * AKV * HD]
                    else:
                        vals = v.vb[:, j, u.h // 2 * P:(u.h // 2 + 1) * P]
                    mm = pe.matmul(v.bank[6 + p % 2][:, a * P:(a + 1) * P], aT[:, p % 2, c:c + P], vals, start=first, stop=last)
                mm.then_inc(weighed, 1)

            pe.wait_ge(columns, 1)
            for step in range(STEPS):
                prepare(0, step)
                wait_prepared(0, step)
            for p in range(n_units):
                scores(p)
                if prepares(p - 1):
                    wait_prepared(*prepares(p - 1))
                if p >= 2:
                    turn(p - 2)
                if prepares(p):
                    free_banks(p - 2)
                    prepare(*prepares(p))
                if p >= 3:
                    weigh(p - 3)
            turn(n_units - 2)
            weigh(n_units - 3)
            turn(n_units - 1)
            weigh(n_units - 2)
            weigh(n_units - 1)


def turn_mixers2_stage(v):
    def chunk(t, k):
        return (v.out_a if k < 4 else v.out_b)[:, t, k % 4 * P:(k % 4 + 1) * P]
    turn_rows_stage(v, chunk)


def output2_stage(v):
    act = (v.act_hi, v.act_lo)
    tiles = sum((group("nat", v.d["w_out_2"], ND, c, c + N, act) for c in (0, N)), [])
    add_rows_stage(v, tiles, (0, N), load_from=v.d["xres"])


def mlp_stage(v):
    nc, at, sem, d = v.nc, v.mem.at, v.sem, v.d
    hid = (at("hid_hi", FREE, [P, ND, S], F32R), at("hid_lo", FREE + 32, [P, ND, S], F32R))
    SLOTS = 7
    sq = at("hid", FREE + 64, [P, SLOTS, N])
    act_ops = (v.act_hi, v.act_lo)
    PARTS = DFF // D
    tiles = []
    for c in range(PARTS):
        for g in range(2):
            tiles += group("tr", d["w_up_2"], ND, c * D + g * N, c * D + (g + 1) * N, act_ops)
        for g in range(2):
            tiles += group("nat", d["w_down_2"][c * D:(c + 1) * D, :], ND, g * N, (g + 1) * N, hid)
    ready, free = sem("bank_ready"), sem("bank_free")
    squared, hi_done, lo_done, stored = sem("squared"), sem("hid_hi_done"), sem("hid_lo_done"), sem("stored")
    act_steps = {}

    def place(i):
        return i % 16 // 2, slice(i % 2 * N, i % 2 * N + N)

    def up_part(c, g):
        def run(act):
            def relu(u):
                i = 16 * c + 8 * g + u
                act.wait_ge(ready, 32 * c + 8 * g + u + 1)
                if i >= SLOTS:
                    act.wait_ge(lo_done, i - SLOTS + 1)
                act.activation(sq[:, i % SLOTS, :], v.bank[u][:, :], ACT.Relu).then_inc(free, 1)

            def high(u):
                i = 16 * c + 8 * g + u
                k, t = place(i)
                act.wait_ge(squared, i + 1)
                act.activation(hid[0][:, k, t], sq[:, i % SLOTS, :], ACT.Copy).then_inc(hi_done, 1)

            for u in range(8):
                relu(u)
                if u >= 4:
                    high(u - 4)
            for u in range(4, 8):
                high(u)
        return run

    for c in range(PARTS):
        for g in range(2):
            act_steps[32 * c + 8 * (g + 1) + 1] = [up_part(c, g)]
    for c in range(PARTS):
        for k in range(ND):
            tiles[32 * c + 16 + k].after = (lo_done, 16 * c + 2 * k + 2)

    def dve_program(dve):
        def low(i):
            k, t = place(i)
            dve.wait_ge(hi_done, i + 1)
            dve.tensor_tensor(hid[1][:, k, t], sq[:, i % SLOTS, :], hid[0][:, k, t].bitcast(F32), ALU.subtract).then_inc(lo_done, 1)

        for c in range(PARTS):
            for g in range(2):
                for u in range(8):
                    i = 16 * c + 8 * g + u
                    dve.wait_ge(free, 32 * c + 8 * g + u + 1)
                    x = sq[:, i % SLOTS, :]
                    dve.tensor_tensor(x, x, x, ALU.mult).then_inc(squared, 1)
                    if u >= 4:
                        low(i - 4)
                for u in range(4, 8):
                    low(16 * c + 8 * g + u)
            for g in range(2):
                for t in range(NT):
                    dve.wait_ge(ready, 32 * c + 16 + 8 * g + t + 1)
                    x = v.xres[:, t, g * N:(g + 1) * N]
                    dve.tensor_tensor(x, v.bank[t], x, ALU.add).then_inc(free, 1)

    def store(act):
        for g in range(2):
            for t in range(NT):
                act.wait_ge(free, 32 * (PARTS - 1) + 16 + 8 * g + t + 1)
                act.dma_start(d["out"][t * P:(t + 1) * P, g * N:(g + 1) * N], v.xres[:, t, g * N:(g + 1) * N]).then_inc(stored, 16)
        act.wait_ge(stored, 16 * 2 * NT)

    dense_stage(v, tiles, dve_program, act_steps, act_after=store, sems=(ready, free))


def constants_stage(v):
    nc, d = v.nc, v.d
    loaded, made = v.sem("constants"), v.sem("constants_bf")
    with nc.Block() as block:
        @block.sync
        def _(sp):
            sp.dma_start(v.ident[:, :], d["ident"]).then_inc(loaded, 16)
            sp.dma_start(v.mask_f[:, :], d["mask"]).then_inc(loaded, 16)

        @block.vector
        def _(dve):
            dve.wait_ge(loaded, 32)
            dve.tensor_copy(v.ident_bf[:, :], v.ident[:, :]).then_inc(made, 1)
            dve.tensor_copy(v.mask_bf[:, :], v.mask_f[:, :]).then_inc(made, 1)


def program(nc, dram, out, until=99, dump=None):
    with ExitStack() as ctx:
        d = dict(dram)
        for name, shape, dt in (("gateT", (2, ND, P, S), F32), ("hog", (S, HG_W), F32), ("xn", (S, D), F32),
                                ("slot_table", (NSLOT_BLK * P, 2), I32), ("y", ((TOPK + 1) * S, D), F32), ("xres", (S, D), F32)):
            d[name] = nc.dram_tensor(f"scratch_{name}", shape, dt).ap()
        d["out"] = out
        v = Env(nc, ctx, d)
        constants_stage(v)
        norm_stage(v, d["norm_mix"], load_from=d["x"])
        block1_tensors(v)
        stages = [project1_stage, hgrn_stage]
        stages += [globals_stage for globals_stage in MORE]
        for n, stage in enumerate(stages):
            if n < until:
                stage(v)
                if len(v.sems) > 80:
                    v.recycle_sems()
        if dump:
            dump(v)


def norm_attention2(v):
    norm_stage(v, v.d["attn_norm_g_2"])


def norm_mlp2(v):
    norm_stage(v, v.d["mlp_norm_g_2"])


MORE = [diff_attention_stage, turn_mixers_stage, branch_stage, output1_stage, router_stage, experts_stage, combine_stage,
        norm_attention2, project2_stage, attention2_stage, turn_mixers2_stage, output2_stage, norm_mlp2, mlp_stage]


def constants():
    i = np.arange(P)
    half = DA_D // 2
    inv = (10000.0 ** (-np.arange(half) / half)).astype(np.float32)
    ang = (np.arange(S, dtype=np.float32)[:, None] * inv[None, :]).astype(np.float64)
    keep = np.ones((1, S), np.float32)
    keep[0, ::CHUNK] = 0.0
    slopes = np.exp2(-(8.0 / AH) * (np.arange(AH, dtype=np.float32) + 1.0)).astype(np.float32)
    dist = (P + i)[:, None] - np.arange(2 * P)[None, :]
    band = (dist >= 0) & (dist < P)
    alibi = np.where(band[None], -slopes[:, None, None] * dist[None].astype(np.float32), np.float32(NEG))
    token = np.arange(NT)[None, :] * P + i[:, None]
    slot = np.arange(NSLOT_BLK * P)
    return {
        "ident": np.eye(P, dtype=np.float32),
        "upper": (i[:, None] < i[None, :]).astype(np.float32),
        "rope_cos": np.cos(ang).astype(np.float32), "rope_sin": np.sin(ang).astype(np.float32),
        "chunk_keep": keep,
        "causal_st": ((i % CHUNK)[:, None] <= np.arange(CHUNK)[None, :]).astype(np.int32),
        "mask": np.where(i[None, :] <= i[:, None], 0.0, NEG).astype(np.float32),
        "alibi": np.ascontiguousarray(alibi.transpose(1, 0, 2)).astype(np.float32),
        "token_rows": np.ascontiguousarray(np.stack(np.broadcast_arrays(token[:, None, :], token[:, None, :] + S * np.arange(TOPK)[None, :, None]),
                                                    axis=-1)).astype(np.int32),
        "slot_init": np.stack([0 * slot, TOPK * S + slot % (2 * P)], axis=-1).astype(np.int32),
        "firsts": np.concatenate([np.arange(NG, 0, -1), np.arange(NE8, 0, -1), np.arange(0, NSLOT_BLK),
                                  np.arange(NT) * P, 2 * np.arange(NBLK // 2)]).astype(np.float32)[None, :],
    }


_ROWS = ("norm_mix", "hg_out_norm", "da_q_norm", "da_k_norm", "da_out_norm", "norm_moe", "b_router_group", "b_router_expert",
         "attn_norm_g_2", "b_forget_2", "q_norm_a_2", "k_norm_a_2", "sink_logits_2", "q_norm_b_2", "k_norm_b_2", "mlp_norm_g_2")


def layout(inputs):
    out = {}
    for name, a in inputs.items():
        a = np.asarray(a)
        if name in _ROWS:
            a = a.reshape(1, -1)
        elif name not in ("hg_lb",) and a.shape[0] == 1:
            a = a.reshape(a.shape[1:])
        out[name] = np.ascontiguousarray(a)
    out.update(constants())
    return out


def kernel(**inputs):
    from concourse import bacc
    from concourse.bass_utils import run_bass_kernel_spmd

    arrays = layout(inputs)
    nc = bacc.Bacc("TRN2", target_bir_lowering=False, num_devices=1)
    dram = {name: nc.dram_tensor(f"in_{name}", a.shape, mybir.dt.from_np(a.dtype), kind="ExternalInput").ap()
            for name, a in arrays.items()}
    out = nc.dram_tensor("out", (S, D), F32, kind="ExternalOutput").ap()
    program(nc, dram, out)
    got = run_bass_kernel_spmd(nc, [{f"in_{name}": a for name, a in arrays.items()}], core_ids=[0])
    return got.results[0]["out"].reshape(1, S, D)
```

```python
from contextlib import ExitStack
import math

import numpy as np
import concourse.bass as bass
import concourse.mybir as mybir
from concourse.alu_op_type import AluOpType as ALU

ACT = mybir.ActivationFunctionType
AX = mybir.AxisListType
F32, F32R, BF16, I32 = mybir.dt.float32, mybir.dt.float32r, mybir.dt.bfloat16, mybir.dt.int32

P = 128
S, D = 1024, 1024
NT, ND = S // P, D // P
N = 512
EPS = 1e-6
KB = 1024

HG_H, HG_D, CHUNK = 4, 128, 64
NCH = S // CHUNK
DA_H, DA_D = 4, 64
LAM_INIT = 0.8 - 0.6 * math.exp(-0.3 * 0)
NG, NE8, NE = 4, 8, 32
FF = 512
TOPK = 2
NBLK = (S * TOPK + NE * (P - 1)) // P
NBLK += NBLK % 2
NSLOT_BLK = NBLK + 2
HD, AH, AKV, BH = 64, 8, 2, 8
BAUG = HD + 4 + 2 * NT
DFF = 4 * D
NEG = -1e30

RING = 4


def chain(eng, sem):
    n = [0]

    def done(ins):
        n[0] += 1
        ins.then_inc(sem, 1)
        return n[0]

    def then(ins):
        eng.wait_ge(sem, done(ins))

    return done, then


def inverse_root(dve, then, r, ms, root, tmp):
    then(dve.reciprocal(r, root))
    then(dve.tensor_tensor(tmp, r, r, ALU.mult))
    then(dve.tensor_tensor(tmp, tmp, ms, ALU.mult))
    then(dve.tensor_scalar(tmp, tmp, -0.5, 1.5, ALU.mult, ALU.add))
    then(dve.tensor_tensor(r, r, tmp, ALU.mult))


class Mem:

    def __init__(self, nc, base):
        self.nc, self.base, self.n = nc, base, 0

    def at(self, name, kb, shape, dt=F32):
        self.n += 1
        return self.nc.alloc_sbuf_tensor_at(f"{name}_{self.n}", list(shape), dt, offset=self.base + (int(kb * KB) + 31) // 32 * 32)


RINGS, CONST, ACTS, FREE, XRES = 0, 24, 32, 96, 175


class Env:

    def __init__(self, nc, ctx, dram):
        self.nc, self.ctx, self.d, self.nsem = nc, ctx, dram, 0
        base = (nc.sbuf_base + 31) // 32 * 32
        ctx.enter_context(nc.sbuf_tensor("arena", [P, 207 * KB // 4], F32))
        self.mem = Mem(nc, base)
        self.pair = [ctx.enter_context(nc.psum_tensor(f"banks{i}", [P, 2 * N], F32)) for i in range(4)]
        self.bank = [self.pair[i // 2][:, i % 2 * N:i % 2 * N + N] for i in range(8)]
        at = self.mem.at
        self.w_raw = at("w_raw", RINGS, [P, RING, N])
        self.w_hi = at("w_hi", RINGS + 8, [P, RING, N], F32R)
        self.w_lo = at("w_lo", RINGS + 16, [P, RING, N], F32R)
        self.act_hi = at("act_hi", ACTS, [P, ND, S], F32R)
        self.act_lo = at("act_lo", ACTS + 32, [P, ND, S], F32R)
        self.xres = at("xres", XRES, [P, NT, D])
        self.ident = at("ident", CONST, [P, P])
        self.ident_bf = at("ident_bf", CONST + 0.5, [P, P], BF16)
        self.mask_bf = at("mask_bf", CONST + 0.75, [P, P], BF16)
        self.mask_f = at("mask_f", CONST + 1, [P, P])

        self.sems = []

    def sem(self, name):
        self.nsem += 1
        self.sems.append(self.nc.alloc_semaphore(name=f"{name}_{self.nsem}"))
        return self.sems[-1]

    def recycle_sems(self):
        self.nc.clear_and_free_semaphores(self.sems)
        self.nc.all_engine_barrier()
        self.sems = []


class Prelude:

    def __init__(self, sync, scalar, vector, tensor, ready, gpsimd=None, act_steps=None, pe_steps=None, rest=None):
        self.sync, self.scalar, self.vector, self.tensor, self.ready, self.gpsimd = sync, scalar, vector, tensor, ready, gpsimd
        self.act_steps, self.pe_steps, self.rest = act_steps or {}, pe_steps or {}, rest


def norm_rows(v, gain, load_from=None, experts=False):
    nc, at, sem, d = v.nc, v.mem.at, v.sem, v.d
    gain_b = at("gain_b", FREE, [P, D])
    junk = at("junk", FREE + 4, [P, D])
    XS = 3
    xs = at("xs", FREE + 8, [P, XS, D])
    ss = at("ss", FREE + 20, [P, NT])
    ms = at("ms", FREE + 20.1, [P, NT])
    rt = at("rt", FREE + 20.2, [P, NT])
    rstd, tmp = at("rstd", FREE + 20.3, [P, NT]), at("rstd_tmp", FREE + 20.4, [P, NT])
    SLOTS, HALF = 5, NT // 2
    y = at("y_rows", FREE + 24, [P, SLOTS, TOPK, D]) if experts else None
    groups = [range(0, 2), range(2, HALF), range(HALF, HALF + 2), range(HALF + 2, NT)]
    HALF_GROUPS = 2
    rows_in = [sem(f"rows_in{t}") for t in range(NT)] if experts or load_from is not None else None
    gain_in, first_times, first_added, added = sem("gain_in"), sem("first_times"), sem("first_added"), sem("added")
    sq_done, ms_done, rt_done, link = sem("sq_done"), sem("ms_done"), sem("rt_done"), sem("dve_link")
    xs_done, tr_done, hi_done, lo_done = sem("xs_done"), sem("tr_done"), sem("hi_done"), sem("lo_done")

    def columns(tiles):
        return slice(tiles[0], tiles[-1] + 1)

    def hi_of(h, t):
        return v.act_hi[:, 4 * h:4 * h + 4, t * P:(t + 1) * P]

    def lo_of(h, t):
        return v.act_lo[:, 4 * h:4 * h + 4, t * P:(t + 1) * P]

    def tr_bank(n):
        return tr_banks(n)[:, :].rearrange("p (c t) -> p c t", c=4)

    def tr_banks(n):
        return v.bank[n if n < NT else HALF + n % HALF]

    def sync(sp, first_weights):
        if experts:
            rows_of = d["y"].rearrange("(k t p) c -> t p k c", p=P, t=NT)

        def load_rows(t):
            if load_from is not None:
                sp.dma_start(v.xres[:, t, :], load_from[t * P:(t + 1) * P, :]).then_inc(rows_in[t], 16)
            if experts:
                if t >= SLOTS:
                    sp.wait_ge(added, t - SLOTS + 1)
                sp.dma_start(y[:, t % SLOTS, :, :], rows_of[t, :, 0:TOPK, :]).then_inc(rows_in[t], 16)

        for t in range(2):
            load_rows(t)
        sp.dma_start(gain_b[:, :], gain.broadcast_to([P, D])).then_inc(gain_in, 16)
        for t in range(2, HALF):
            load_rows(t)
        first_weights(sp)
        for t in range(HALF, NT):
            load_rows(t)

    def gpsimd(pool, first_weights):
        if experts:
            for t in range(HALF):
                pool.wait_ge(first_times, t + 1)
                x = v.xres[:, t, :]
                pool.tensor_tensor(x, x, y[:, t % SLOTS, 0, :], ALU.add).then_inc(first_added, 1)
        first_weights(pool)

    def evacuate_hi(act, t):
        for h in range(2):
            n = 2 * t + h
            act.wait_ge(tr_done, n + 1)
            act.activation(hi_of(h, t), tr_bank(n), ACT.Copy).then_inc(hi_done, 1)

    def scalar(act, first_weights):
        def weigh_first(tiles):
            for t in tiles:
                act.wait_ge(rows_in[t], 16)
                x = y[:, t % SLOTS, 0, :]
                act.activation(x, x, ACT.Copy, scale=v.e_w[:, 0, t:t + 1]).then_inc(first_times, 1)

        if experts:
            weigh_first(groups[0])
        for g, tiles in enumerate(groups):
            if experts and g + 1 < HALF_GROUPS:
                weigh_first(groups[g + 1])
            for t in tiles:
                if experts:
                    act.wait_ge(added, t + 1)
                elif load_from is not None:
                    act.wait_ge(rows_in[t], 16)
                if t:
                    act.wait_ge(sq_done, t)
                act.activation(junk[:, :], v.xres[:, t, :], ACT.Square, accum_out=ss[:, t:t + 1]).then_inc(sq_done, 1)
            act.wait_ge(ms_done, g + 1)
            act.activation(rt[:, columns(tiles)], ms[:, columns(tiles)], ACT.Sqrt).then_inc(rt_done, 1)
            if g == HALF_GROUPS - 1:
                for t in range(HALF):
                    evacuate_hi(act, t)
                first_weights(act)

    def vector(dve):
        _, then = chain(dve, link)

        def add_experts(tiles):
            for t in tiles:
                dve.wait_ge(rows_in[t], 16)
                x = v.xres[:, t, :]
                if t < HALF:
                    dve.wait_ge(first_added, t + 1)
                else:
                    then(dve.scalar_tensor_tensor(out=x, in0=y[:, t % SLOTS, 0, :], scalar=v.e_w[:, 0, t:t + 1], in1=x, op0=ALU.mult, op1=ALU.add))
                dve.scalar_tensor_tensor(out=x, in0=y[:, t % SLOTS, 1, :], scalar=v.e_w[:, 1, t:t + 1], in1=x, op0=ALU.mult, op1=ALU.add).then_inc(added, 1)

        def evacuate_lo(t):
            for h in range(2):
                n = 2 * t + h
                dve.wait_ge(hi_done, n + 1)
                dve.tensor_tensor(lo_of(h, t), tr_bank(n), hi_of(h, t).bitcast(F32), ALU.subtract).then_inc(lo_done, 1)

        if experts:
            add_experts(groups[0])
        dve.wait_ge(gain_in, 16)
        for g, tiles in enumerate(groups):
            col = columns(tiles)
            if experts and g == HALF_GROUPS:
                add_experts(tiles)
            dve.wait_ge(sq_done, tiles[-1] + 1)
            dve.tensor_scalar(ms[:, col], ss[:, col], 1.0 / D, EPS, ALU.mult, ALU.add).then_inc(ms_done, 1)
            if experts and g + 1 < len(groups) and g + 1 != HALF_GROUPS:
                add_experts(groups[g + 1])
            dve.wait_ge(rt_done, g + 1)
            inverse_root(dve, then, rstd[:, col], ms[:, col], rt[:, col], tmp[:, col])
            for t in tiles:
                if t >= XS:
                    dve.wait_ge(tr_done, 2 * (t - XS + 1))
                if experts:
                    dve.wait_ge(added, t + 1)
                dve.scalar_tensor_tensor(out=xs[:, t % XS, :], in0=v.xres[:, t, :], scalar=rstd[:, t:t + 1],
                                         in1=gain_b[:, :], op0=ALU.mult, op1=ALU.mult).then_inc(xs_done, 1)
            if g == HALF_GROUPS - 1:
                for t in range(HALF):
                    evacuate_lo(t)
        for t in range(HALF, NT):
            evacuate_lo(t)

    def turn(pe, t):
        pe.wait_ge(xs_done, t + 1)
        for h in range(2):
            n = 2 * t + h
            if n >= NT + HALF:
                pe.wait_ge(lo_done, n - HALF + 1)
            for c in range(4):
                k = 4 * h + c
                last = pe.transpose(tr_banks(n)[:, c * P:(c + 1) * P], xs[:, t % XS, k * P:(k + 1) * P], v.ident[:, :])
            last.then_inc(tr_done, 1)

    def tensor(pe):
        for t in range(HALF):
            turn(pe, t)

    BEHIND = 2 if not experts else 4
    act_steps = {RING + BEHIND + i: lambda act, t=HALF + i: evacuate_hi(act, t) for i in range(HALF)}
    pe_steps = {BEHIND + i: lambda pe, t=HALF + i: turn(pe, t) for i in range(HALF)}
    return Prelude(sync, scalar, vector, tensor, [(hi_done, NT), (lo_done, NT)], gpsimd, act_steps, pe_steps, [(hi_done, 2 * NT), (lo_done, 2 * NT)])


class Tile:

    def __init__(self, kind, parts, cols, act, k, first, last, b0=0):
        self.kind, self.parts, self.cols, self.act, self.k = kind, parts, cols, act, k
        self.first, self.last, self.b0 = first, last, b0
        self.after = None
        self.units = NT if kind == "nat" else 2 * (cols // P)


def dense_stage(v, tiles, dve_program, act_steps=None, act_after=None, sp_before=None, sp_steps=None, sems=None, prelude=None):
    nc, sem = v.nc, v.sem
    landed = [sem(f"w_landed{i}") for i in range(RING)]
    hi_done, lo_done, used = sem("w_hi_done"), sem("w_lo_done"), sem("w_used")
    ready, free = sems
    act_steps, sp_steps = act_steps or {}, sp_steps or {}
    turns = [(tile, range(tile.units), n) for n, tile in enumerate(tiles)]
    twice = 1 + [tile.last for tile in tiles].index(True) if prelude and prelude.rest else 0
    turns = [(t, range(t.units // 2), None) for t in tiles[:twice]] + [(t, range(t.units // 2, t.units), n) for t, _, n in turns[:twice]] + turns[twice:]

    with nc.Block() as block:
        @block.sync
        def _(sp):
            def load(sp, i):
                if i >= RING:
                    sp.wait_ge(lo_done, i - RING + 1)
                for ap, c0, c1 in turns[i][0].parts:
                    sp.dma_start(v.w_raw[:, i % RING, c0:c1], ap).then_inc(landed[i % RING], 16)

            def first_weights(sp):
                for i in range(RING):
                    load(sp, i)

            if twice:
                prelude.sync(sp, first_weights)
            elif prelude:
                prelude.sync(sp)
            if sp_before:
                sp_before(sp)
            for i, (tile, units, n) in enumerate(turns):
                if i >= RING or not twice:
                    load(sp, i)
                for f in sp_steps.get(n, ()):
                    f(sp)

        count, arrived, spent, n_used, n_banks = [0] * RING, [], [], 0, 0
        for i, (tile, units, n) in enumerate(turns):
            count[i % RING] += 16 * len(tile.parts)
            arrived.append(count[i % RING])
            if tile.last:
                n_banks += len(units)
            else:
                n_used += 1
            spent.append((ready, n_banks) if tile.last else (used, n_used))

        @block.scalar
        def _(act):
            def high(act, i):
                cols = turns[i][0].cols
                act.wait_ge(landed[i % RING], arrived[i])
                if i >= RING:
                    act.wait_ge(*spent[i - RING])
                act.activation(v.w_hi[:, i % RING, :cols], v.w_raw[:, i % RING, :cols], ACT.Copy).then_inc(hi_done, 1)

            def first_weights(act):
                for i in range(RING):
                    high(act, i)

            if twice:
                prelude.scalar(act, first_weights)
            elif prelude:
                prelude.scalar(act)
            for i, (tile, units, n) in enumerate(turns):
                if prelude and i in prelude.act_steps:
                    prelude.act_steps[i](act)
                if i >= RING or not twice:
                    high(act, i)
                for f in act_steps.get(n, ()):
                    f(act)
            if act_after:
                act_after(act)

        @block.gpsimd
        def _(pool):
            def low(pool, i):
                cols = turns[i][0].cols
                pool.wait_ge(hi_done, i + 1)
                pool.tensor_tensor(v.w_lo[:, i % RING, :cols], v.w_raw[:, i % RING, :cols],
                                   v.w_hi[:, i % RING, :cols].bitcast(F32), ALU.subtract).then_inc(lo_done, 1)

            def first_weights(pool):
                for i in range(RING):
                    low(pool, i)

            if twice:
                prelude.gpsimd(pool, first_weights)
            for i in range(RING if twice else 0, len(turns)):
                low(pool, i)

        @block.vector
        def _(dve):
            if prelude:
                prelude.vector(dve)
            dve_program(dve)

        @block.tensor
        def _(pe):
            freed = [0] * 8
            banks = 0
            if prelude:
                prelude.tensor(pe)
                for s, count in prelude.ready:
                    pe.wait_ge(s, count)
            for i, (tile, units, n) in enumerate(turns):
                if i == twice and twice:
                    for s, count in prelude.rest:
                        pe.wait_ge(s, count)
                pe.wait_ge(lo_done, i + 1)
                if tile.after:
                    pe.wait_ge(*tile.after)
                hi, lo = tile.act
                w_hi, w_lo = v.w_hi[:, i % RING, :tile.cols], v.w_lo[:, i % RING, :tile.cols]
                for u in units:
                    b = tile.b0 + u
                    if tile.first and freed[b]:
                        pe.wait_ge(free, freed[b])
                    if tile.kind == "nat":
                        t = slice(u * P, (u + 1) * P)
                        out = v.bank[b][:, :tile.cols]
                        prods = [(hi[:, tile.k, t], w_hi), (hi[:, tile.k, t], w_lo), (lo[:, tile.k, t], w_hi)]
                    else:
                        half, c = divmod(u, tile.units // 2)
                        c, t = slice(c * P, c * P + P), slice(half * N, half * N + N)
                        out = v.bank[b][:, :]
                        prods = [(w_hi[:, c], hi[:, tile.k, t]), (w_hi[:, c], lo[:, tile.k, t]), (w_lo[:, c], hi[:, tile.k, t])]
                    for j, (left, right) in enumerate(prods):
                        mm = pe.matmul(out, left, right, start=(tile.first and j == 0), stop=(tile.last and j == 2))
                    if tile.last:
                        banks += 1
                        freed[b] = banks
                        mm.then_inc(ready, 1)
                    elif u == units[-1]:
                        mm.then_inc(used, 1)
                if prelude and i in prelude.pe_steps:
                    prelude.pe_steps[i](pe)


def rows(w, k, c0, c1):
    return w[k * P:(k + 1) * P, c0:c1]


def group(kind, w, k_tiles, c0, c1, act, k0=0, b0=0):
    return [Tile(kind, [(rows(w, k, c0, c1), 0, c1 - c0)], c1 - c0, act, k0 + k, k == 0, k == k_tiles - 1, b0)
            for k in range(k_tiles)]


class Heads:

    def __init__(self, v, name, dst, heads, at_kb):
        at, sem = v.mem.at, v.sem
        self.dst, self.h = dst, heads
        self.sq = at(name + "_sq", at_kb, [P, heads * HD])
        self.ss = at(name + "_ss", at_kb + 2, [P, NT, heads])
        self.rt = at(name + "_rt", at_kb + 2.25, [P, NT, heads])
        self.r = at(name + "_r", at_kb + 2.5, [P, NT, heads])
        self.tmp = at(name + "_tmp", at_kb + 2.75, [P, NT, heads])
        self.ms_done, self.rt_done = sem(name + "_ms"), sem(name + "_rt")

    def take(self, dve, then, bank, t, free):
        x = self.dst(t)
        src = bank.rearrange("p (h d) -> p h d", h=self.h)
        dve.tensor_copy(x, src).then_inc(free, 1)

    def stat(self, dve, then, t):
        x = self.dst(t)
        sq = self.sq[:, :].rearrange("p (h d) -> p h d", h=self.h)
        then(dve.tensor_tensor(sq, x, x, ALU.mult))
        then(dve.tensor_reduce(self.ss[:, t, :], sq, AX.X, ALU.add))

    def mean(self, dve):
        dve.tensor_scalar(self.ss[:, :, :], self.ss[:, :, :], 1.0 / HD, EPS, ALU.mult, ALU.add).then_inc(self.ms_done, 1)

    def root(self, act):
        act.wait_ge(self.ms_done, 1)
        act.activation(self.rt[:, :, :], self.ss[:, :, :], ACT.Sqrt).then_inc(self.rt_done, 1)

    def inverse(self, dve, then):
        dve.wait_ge(self.rt_done, 1)
        inverse_root(dve, then, self.r[:, :, :], self.ss[:, :, :], self.rt[:, :, :], self.tmp[:, :, :])

    def scale(self, dve, then, t, gain):
        x = self.dst(t)
        then(dve.tensor_tensor(x, x, self.r[:, t, :].unsqueeze(2).broadcast_to([P, self.h, HD]), ALU.mult))
        then(dve.tensor_tensor(x, x, gain.unsqueeze(1).broadcast_to([P, self.h, HD]), ALU.mult))


def rotate(dve, done, then, x, cos, sin, tmp):
    half = HD // 2
    h = x.shape[1]
    x1, x2 = x[:, :, :half], x[:, :, half:]
    c = cos.unsqueeze(1).broadcast_to([P, h, half])
    s = sin.unsqueeze(1).broadcast_to([P, h, half])
    t = [tmp[:, i, :].rearrange("p (h d) -> p h d", h=h) for i in range(4)]
    done(dve.tensor_tensor(t[0], x1, c, ALU.mult))
    done(dve.tensor_tensor(t[1], x2, s, ALU.mult))
    done(dve.tensor_tensor(t[2], x1, s, ALU.mult))
    then(dve.tensor_tensor(t[3], x2, c, ALU.mult))
    done(dve.tensor_tensor(x1, t[0], t[1], ALU.subtract))
    then(dve.tensor_tensor(x2, t[2], t[3], ALU.add))


HG_W, DA_W = HG_H * HG_D, DA_H * 2 * DA_D
COL = dict(zip(("hq", "hf", "hi", "hog", "dq", "dk", "dv", "gate_hg", "gate_da"),
               np.cumsum([0] + [HG_W] * 4 + [DA_W] * 3 + [D]).tolist()))


def block1_tensors(v):
    at = v.mem.at
    v.hqT = at("hqT", FREE, [P, HG_H, S])
    v.hfT = at("hfT", FREE + 16, [P, HG_H, S])
    v.hv = at("hv", FREE + 32, [P, NT, HG_W])
    v.dq = at("dq", FREE + 48, [P, NT, DA_W])
    v.dk = at("dk", FREE + 64, [P, NT, DA_W])
    v.dv = at("dv", FREE + 80, [P, NT, DA_W])


def project1_stage(v):
    nc, at, sem, d = v.nc, v.mem.at, v.sem, v.d
    act_ops = (v.act_hi, v.act_lo)
    w_in = d["w_in"]
    order = ["dq", "dv", "dk", "hf", "hog", "gate_hg", "gate_hg+", "gate_da", "gate_da+", "hq", "hi"]
    tiles = []
    for name in order:
        c0 = COL[name.rstrip("+")] + (N if name.endswith("+") else 0)
        tiles += group("tr" if name[:2] in ("hq", "hf", "ga") else "nat", w_in, ND, c0, c0 + N, act_ops)
    index = {name: g for g, name in enumerate(order)}

    temps = FREE + 96
    q_heads = Heads(v, "dq", lambda t: v.dq[:, t, :].rearrange("p (h d) -> p h d", d=DA_D), 8, temps)
    k_heads = Heads(v, "dk", lambda t: v.dk[:, t, :].rearrange("p (h d) -> p h d", d=DA_D), 8, temps + 3)
    rot = at("rot", temps + 6, [P, 4, 256])
    SLOTS = 2
    stage = at("stage", temps + 10, [P, SLOTS, N])
    cos, sin = at("cos", 29, [P, NT, DA_D // 2]), at("sin", 30, [P, NT, DA_D // 2])
    gains = at("gains", 28, [P, 2, DA_D])
    ready, free = sem("bank_ready"), sem("bank_free")
    tables, link = sem("tables"), sem("dve_link")
    staged, stored = sem("gate_staged"), [sem(f"gate_stored{i}") for i in range(SLOTS)]

    def load_tables(sp):
        sp.dma_start(cos[:, :, :], d["rope_cos"].rearrange("(t p) c -> p t c", p=P)).then_inc(tables, 16)
        sp.dma_start(sin[:, :, :], d["rope_sin"].rearrange("(t p) c -> p t c", p=P)).then_inc(tables, 16)
        sp.dma_start(gains[:, 0, :], d["da_q_norm"].broadcast_to([P, DA_D])).then_inc(tables, 16)
        sp.dma_start(gains[:, 1, :], d["da_k_norm"].broadcast_to([P, DA_D])).then_inc(tables, 16)

    n_staged = [0]

    def banks_to_dram(g, func, dst):
        def run(act):
            for b in range(8):
                i = n_staged[0]
                n_staged[0] += 1
                act.wait_ge(ready, 8 * g + b + 1)
                if i >= SLOTS:
                    act.wait_ge(stored[i % SLOTS], 16 * (i // SLOTS))
                act.activation(stage[:, i % SLOTS, :], v.bank[b][:, :], func).then_inc(free, 1)
                act.wait_ge(free, 8 * g + b + 1)
                act.dma_start(dst(b), stage[:, i % SLOTS, :]).then_inc(stored[i % SLOTS], 16)
        return run

    def gate_rows(gate, more):
        return lambda b: v.d["gateT"][gate, more * 4 + b % 4, :, (b // 4) * N:(b // 4) * N + N]

    steps = {}

    def after(g, offset, f):
        steps.setdefault(8 * (g + 1) + offset, []).append(f)

    def keep_decay(act):
        for b in range(8):
            act.wait_ge(ready, 8 * index["hf"] + b + 1)
            act.activation(v.hfT[:, b % 4, (b // 4) * N:(b // 4) * N + N], v.bank[b][:, :], ACT.Sigmoid).then_inc(free, 1)

    after(index["dq"], 6, q_heads.root)
    after(index["dk"], 6, k_heads.root)
    after(index["hf"], 2, keep_decay)
    last = []
    for name, func, dst in (("hog", ACT.Silu, lambda b: v.d["hog"][b * P:(b + 1) * P, :]),
                            ("gate_hg", ACT.Sigmoid, gate_rows(0, 0)), ("gate_hg+", ACT.Sigmoid, gate_rows(0, 1)),
                            ("gate_da", ACT.Sigmoid, gate_rows(1, 0)), ("gate_da+", ACT.Sigmoid, gate_rows(1, 1))):
        g = index[name]
        if 8 * (g + 1) < len(tiles):
            after(g, 2, banks_to_dram(g, func, dst))
        else:
            last.append(banks_to_dram(g, func, dst))

    def act_after(act):
        for f in last:
            f(act)
        for i in range(SLOTS):
            act.wait_ge(stored[i], 16 * ((n_staged[0] + SLOTS - 1 - i) // SLOTS))

    def dve_program(dve):
        done, then = chain(dve, link)

        def copy(name, dst):
            for b in range(8):
                n = 8 * index[name] + b + 1
                dve.wait_ge(ready, n)
                dve.tensor_copy(dst(b), v.bank[b][:, :]).then_inc(free, 1)

        MEANWHILE = 4

        def norm(name, heads, gain, meanwhile=None):
            n = 8 * index[name]
            for t in range(NT):
                dve.wait_ge(ready, n + t + 1)
                heads.take(dve, then, v.bank[t][:, :], t, free)
            dve.wait_ge(free, n + NT)
            for t in range(NT):
                heads.stat(dve, then, t)
            heads.mean(dve)
            heads.inverse(dve, then)
            for t in range(NT):
                heads.scale(dve, then, t, gains[:, gain, :])
                rotate(dve, done, then, heads.dst(t), cos[:, t, :], sin[:, t, :], rot)
                if meanwhile and t == MEANWHILE:
                    meanwhile()

        dve.wait_ge(tables, 64)
        then(dve.tensor_scalar(gains[:, 0, :], gains[:, 0, :], DA_D ** -0.5, None, ALU.mult))
        norm("dq", q_heads, 0, lambda: copy("dv", lambda b: v.dv[:, b, :]))
        norm("dk", k_heads, 1)
        copy("hq", lambda b: v.hqT[:, b % 4, (b // 4) * N:(b // 4) * N + N])
        copy("hi", lambda b: v.hv[:, b, :])

    dense_stage(v, tiles, dve_program, steps, act_after, sp_before=load_tables, sems=(ready, free),
                prelude=norm_rows(v, d["norm_mix"], load_from=d["x"]))


def hgrn_stage(v):
    nc, at, sem, d = v.nc, v.mem.at, v.sem, v.d
    o = at("o_raw", ACTS, [P, NT, HG_W])
    sets = [dict((name, at(f"{name}{i}", ACTS + 16 + 16 * i + 4 * j, [P, S]))
                 for j, name in enumerate(("q_rel", "k_rel", "q_dec", "k_end"))) for i in range(2)]
    b_ = at("b", ACTS + 48, [P, S])
    sq = at("sq", ACTS + 52, [P, NT, HG_D])
    keep = at("keep", ACTS + 56, [P, S])
    k_rows = at("k_rows", ACTS + 60, [P, NT, P])
    from_mid, to_end, e_mid, e_b = (at(n, RINGS + 4 * i, [P, S]) for i, n in enumerate(("from_mid", "to_end", "e_mid", "e_b")))
    hog = at("hog", RINGS + 16, [P, 2, NT, HG_D])
    scT = at("scT", FREE + 96, [P, 2, NT, CHUNK])
    st = at("state", FREE + 100, [P, NCH, P])
    causal = at("causal", FREE + 108, [P, CHUNK], I32)
    lb = at("lb", FREE + 108.5, [P, 2, HG_H])
    lbt = at("lbt", FREE + 108.75, [P, 4, HG_H])
    dec = at("dec", FREE + 109, [P, 2, NCH])
    gain = at("hg_gain", FREE + 109.5, [P, HG_D])
    ssum, root, inv, itmp = (at(f"o_{n}", FREE + 110 + 0.125 * i, [P, HG_H, NT]) for i, n in enumerate(("ssum", "root", "inv", "tmp")))
    v.o_hg = at("o_hg", FREE, [P, NT, HG_W])

    consts, link, lb_exp, sig = sem("consts"), sem("dve_link"), sem("lb_exp"), sem("sig")
    f_done, ln_done, to_exp, exps, ops = sem("f_done"), sem("ln_done"), sem("to_exp"), sem("exps"), sem("operands")
    scores, scT_done, tr_done, rows_done = sem("scores"), sem("scT_done"), sem("tr_done"), sem("rows_done")
    u_done, state_done, o_done, o_read = sem("u_done"), sem("state_done"), sem("o_done"), sem("o_read")
    sum_done, root_done, gated, normed, zero = sem("sum_done"), sem("root_done"), sem("gated"), sem("normed"), sem("zero")
    hog_in = [sem(f"hog_in{i}") for i in range(2)]

    def by_chunk(x):
        return x.rearrange("p (c t) -> p c t", t=CHUNK)

    def head(x, h):
        return x[:, :, h * HG_D:(h + 1) * HG_D]

    def own_sum(c):
        return v.bank[((2, 3), (1, 5))[c // 8][c % 2]][:, (c // 2 % 4) * P:(c // 2 % 4 + 1) * P]

    def in_place_of_f(h):
        return v.hfT[:, h, :].rearrange("p (t c) -> p t c", t=NT)

    with nc.Block() as block:
        @block.sync
        def _(sp):
            sp.dma_start(keep[:, :], d["chunk_keep"].broadcast_to([P, S])).then_inc(consts, 16)
            sp.dma_start(causal[:, :], d["causal_st"]).then_inc(consts, 16)
            with nc.allow_non_contiguous_dma("lower bounds by partition"):
                sp.dma_start(lbt[:, 0:2, :], d["hg_lb"].rearrange("r (h p) -> p r h", p=P)).then_inc(consts, 16)
            sp.dma_start(gain[:, :], d["hg_out_norm"].broadcast_to([P, HG_D])).then_inc(consts, 16)
            for h in range(HG_H):
                if h >= 2:
                    sp.wait_ge(gated, 2 * h - 2)
                sp.dma_start(hog[:, h % 2, :, :], d["hog"][:, h * HG_D:(h + 1) * HG_D].rearrange("(t p) c -> p t c", p=P)).then_inc(hog_in[h % 2], 16)

        @block.scalar
        def _(act):
            act.wait_ge(lb_exp, 1)
            act.activation(lbt[:, 2:4, :], lbt[:, 2:4, :], ACT.Exp).then_inc(sig, 1)

            def log(h):
                act.wait_ge(f_done, h + 1)
                act.activation(v.hfT[:, h, :], v.hfT[:, h, :], ACT.Ln).then_inc(ln_done, 1)

            def exponentials(h):
                act.wait_ge(to_exp, 2 * h + 1)
                act.activation(e_mid[:, :], from_mid[:, :], ACT.Exp).then_inc(exps, 1)
                act.activation(e_b[:, :], b_[:, :], ACT.Exp).then_inc(exps, 1)
                act.wait_ge(exps, 4 * h + 1)
                act.activation(from_mid[:, :], from_mid[:, :], ACT.Exp, scale=-1.0).then_inc(exps, 1)
                act.wait_ge(to_exp, 2 * h + 2)
                act.activation(to_end[:, :], to_end[:, :], ACT.Exp).then_inc(exps, 1)

            def rows(h):
                for half in range(2):
                    n = 2 * h + half
                    act.wait_ge(tr_done, n + 1)
                    if h:
                        act.wait_ge(u_done, 2 * h)
                    act.activation(k_rows[:, 4 * half:4 * half + 4, :],
                                   v.bank[0][:, :].rearrange("p (t c) -> p t c", t=4), ACT.Copy).then_inc(rows_done, 1)

            def out(h):
                for half in range(2):
                    n = 2 * h + half
                    act.wait_ge(o_done, n + 1)
                    act.activation(o[:, 4 * half:4 * half + 4, h * P:(h + 1) * P],
                                   v.bank[6 + half][:, :].rearrange("p (t c) -> p t c", t=4), ACT.Copy).then_inc(o_read, 1)

            log(0)
            exponentials(0)
            for h in range(HG_H):
                if h + 1 < HG_H:
                    log(h + 1)
                rows(h)
                if h + 1 < HG_H:
                    exponentials(h + 1)
                out(h)
            act.wait_ge(sum_done, 1)
            act.activation(root[:, :, :], ssum[:, :, :], ACT.Sqrt).then_inc(root_done, 1)

        @block.gpsimd
        def _(pool):
            pool.wait_ge(consts, 64)
            for h in range(HG_H):
                og = hog[:, h % 2, :, :]
                pool.wait_ge(hog_in[h % 2], 16 * (h // 2 + 1))
                pool.tensor_tensor(og, og, gain[:, :].unsqueeze(1).broadcast_to([P, NT, HG_D]), ALU.mult).then_inc(gated, 1)
                pool.wait_ge(gated, 2 * h + 1)
                pool.wait_ge(o_read, 2 * h + 2)
                pool.tensor_tensor(in_place_of_f(h), head(o, h), og, ALU.mult).then_inc(gated, 1)

        @block.vector
        def _(dve):
            done, then = chain(dve, link)
            dve.memset(scT[:, :, :, :], 0.0).then_inc(zero, 1)
            dve.wait_ge(consts, 64)
            then(dve.tensor_tensor(lb[:, 0, :], lbt[:, 0, :], lbt[:, 1, :], ALU.max))
            dve.tensor_tensor(lbt[:, 2:4, :], lbt[:, 0:2, :], lb[:, 0:1, :].broadcast_to([P, 2, HG_H]), ALU.subtract).then_inc(lb_exp, 1)
            dve.wait_ge(sig, 1)
            then(dve.tensor_tensor(lb[:, 1, :], lbt[:, 2, :], lbt[:, 3, :], ALU.add))
            then(dve.reciprocal(lb[:, 1, :], lb[:, 1, :]))
            then(dve.tensor_tensor(lb[:, 0, :], lbt[:, 2, :], lb[:, 1, :], ALU.mult))
            then(dve.tensor_scalar(lb[:, 1, :], lb[:, 0, :], -1.0, 1.0, ALU.mult, ALU.add))

            def gates(h):
                if h >= 2:
                    dve.wait_ge(o_done, 2 * (h - 1))
                f = v.hfT[:, h, :]
                then(dve.tensor_scalar(f, f, lb[:, 1, h:h + 1], lb[:, 0, h:h + 1], ALU.mult, ALU.add))
                dve.tensor_scalar(sets[h % 2]["k_end"][:, :], f, -1.0, 1.0, ALU.mult, ALU.add).then_inc(f_done, 1)

            def sums(h):
                dve.wait_ge(ln_done, h + 1)
                then(dve.tensor_tensor_scan(b_[:, :], keep[:, :], v.hfT[:, h, :], 0.0, ALU.mult, ALU.add))
                b = by_chunk(b_[:, :])
                mid, end = (b[:, :, c:c + 1].broadcast_to([P, NCH, CHUNK]) for c in (CHUNK // 2 - 1, CHUNK - 1))
                dve.tensor_tensor(by_chunk(from_mid[:, :]), b, mid, ALU.subtract).then_inc(to_exp, 1)
                dve.tensor_tensor(by_chunk(to_end[:, :]), end, b, ALU.subtract).then_inc(to_exp, 1)

            def operands(h):
                s, q = sets[h % 2], v.hqT[:, h, :]
                k = s["k_end"][:, :]
                for i, (name, src, e) in enumerate((("q_rel", q, e_mid), ("q_dec", q, e_b), ("k_rel", k, from_mid), ("k_end", k, to_end))):
                    dve.wait_ge(exps, 4 * h + i + 1)
                    if i == 3:
                        dve.wait_ge(ops, 4 * h + 3)
                    dve.tensor_tensor(s[name][:, :], src, e[:, :], ALU.mult).then_inc(ops, 1)
                    if i == 1:
                        then(dve.tensor_copy(dec[:, h % 2, :], by_chunk(e_b[:, :])[:, :, CHUNK - 1:CHUNK].rearrange("p c o -> p (c o)")))
                dve.wait_ge(ops, 4 * h + 4)

            def causal_scores(h):
                dve.wait_ge(scores, h + 1)
                if h >= 2:
                    dve.wait_ge(o_done, 2 * (h - 1))
                dve.copy_predicated(scT[:, h % 2, :, :], causal[:, :].unsqueeze(1).broadcast_to([P, NT, CHUNK]),
                                    v.bank[4][:, :].rearrange("p (t c) -> p t c", t=NT)).then_inc(scT_done, 1)

            def states(h, half):
                dve.wait_ge(u_done, 2 * h + half + 1)
                for c in range(8 * half, 8 * half + 8):
                    u = own_sum(c)
                    if c == 0:
                        if h:
                            dve.wait_ge(o_done, 2 * h)
                        ins = dve.tensor_copy(st[:, 0, :], u)
                    else:
                        dve.wait_ge(state_done, NCH * h + c)
                        ins = dve.scalar_tensor_tensor(out=st[:, c, :], in0=st[:, c - 1, :], scalar=dec[:, h % 2, c:c + 1], in1=u,
                                                       op0=ALU.mult, op1=ALU.add)
                    ins.then_inc(state_done, 1)

            def squares(h):
                dve.wait_ge(o_read, 2 * h + 2)
                then(dve.tensor_tensor(sq[:, :, :], head(o, h), head(o, h), ALU.mult))
                then(dve.tensor_reduce(ssum[:, h, :], sq[:, :, :], AX.X, ALU.add))

            gates(0)
            sums(0)
            for h in range(HG_H):
                operands(h)
                if h + 1 < HG_H:
                    gates(h + 1)
                causal_scores(h)
                if h:
                    squares(h - 1)
                states(h, 0)
                if h + 1 < HG_H:
                    sums(h + 1)
                states(h, 1)
            squares(HG_H - 1)
            dve.tensor_scalar(ssum[:, :, :], ssum[:, :, :], 1.0 / HG_D, EPS, ALU.mult, ALU.add).then_inc(sum_done, 1)
            dve.wait_ge(root_done, 1)
            inverse_root(dve, then, inv[:, :, :], ssum[:, :, :], root[:, :, :], itmp[:, :, :])
            for h in range(HG_H):
                dve.wait_ge(gated, 2 * h + 2)
                dve.tensor_tensor(head(v.o_hg, h), in_place_of_f(h), inv[:, h, :].unsqueeze(2).broadcast_to([P, NT, HG_D]),
                                  ALU.mult).then_inc(normed, 1)

        @block.tensor
        def _(pe):
            def chunk_rows(c):
                return slice(c % 2 * CHUNK, c % 2 * CHUNK + CHUNK)

            for h in range(HG_H):
                s = sets[h % 2]
                hc = slice(h * P, (h + 1) * P)
                pe.wait_ge(ops, 4 * h + 3)
                if h:
                    pe.wait_ge(scT_done, h)
                for c in range(NCH):
                    t = slice(c * CHUNK, (c + 1) * CHUNK)
                    mm = pe.matmul(v.bank[4][chunk_rows(c), c // 2 * CHUNK:(c // 2 + 1) * CHUNK],
                                   s["k_rel"][:, t], s["q_rel"][:, t], start=True, stop=True)
                mm.then_inc(scores, 1)
                pe.wait_ge(ops, 4 * h + 4)
                for half in range(2):
                    if h or half:
                        pe.wait_ge(rows_done, 2 * h + half)
                    for t in range(4):
                        tt = 4 * half + t
                        mm = pe.transpose(v.bank[0][:, t * P:(t + 1) * P], s["k_end"][:, tt * P:(tt + 1) * P], v.ident[:, :])
                    mm.then_inc(tr_done, 1)
                for c in range(NCH):
                    n = 2 * h + c // 8
                    if c % 8 == 0:
                        pe.wait_ge(rows_done, n + 1)
                        if h:
                            pe.wait_ge(state_done, 8 * n - 8)
                    r = chunk_rows(c)
                    mm = pe.matmul(own_sum(c), k_rows[r, c // 2, :], v.hv[r, c // 2, hc], start=True, stop=True)
                    if c % 8 == 7:
                        mm.then_inc(u_done, 1)
                pe.wait_ge(scT_done, h + 1)
                for half in range(2):
                    n = 2 * h + half
                    if h:
                        pe.wait_ge(o_read, n - 1)
                    for c in range(8 * half, 8 * half + 8):
                        r, tt = chunk_rows(c), c // 2
                        out = v.bank[6 + half][r, (tt % 4) * P:(tt % 4 + 1) * P]
                        mm = pe.matmul(out, scT[r, h % 2, tt, :], v.hv[r, tt, hc], start=True, stop=(c == 0))
                        if c:
                            pe.wait_ge(state_done, NCH * h + c)
                            mm = pe.matmul(out, s["q_dec"][:, c * CHUNK:(c + 1) * CHUNK], st[:, c - 1, :], start=False, stop=True)
                    mm.then_inc(o_done, 1)


def split_scores(pe, v, pair, q_hi, k_hi, q_both, k_both, nk):
    for c0 in range(0, nk, N):
        c = slice(c0, min(c0 + N, nk))
        pe.matmul(pair[:, c], q_hi, k_hi[:, c], start=True, stop=False)
        mm = pe.matmul(pair[:, c], q_both, k_both[:, c], start=False, stop=(c.stop < nk))
    return pe.matmul(pair[:, nk - P:nk], v.ident_bf[:, :], v.mask_bf[:, :], start=False, stop=True)


def diff_attention_stage(v):
    nc, at, sem, d = v.nc, v.mem.at, v.sem, v.d
    q_both = [at(f"q_both{a}", ACTS + 16 * a, [P, DA_H, S], F32R) for a in range(2)]
    k_both = [at(f"k_both{a}", ACTS + 32 + 16 * a, [P, DA_H, S], F32R) for a in range(2)]
    k_hi = at("k_hi", FREE + 16, [P, DA_H, S], F32R)
    probs = at("probs", RINGS, [P, 2, 2, S])
    a_ = at("a", RINGS + 16, [P, 2, S])
    aT = at("aT", FREE + 96, [P, 2, S])
    o = v.dq
    v.o_da = v.dq
    small = FREE + 104
    lam_in = at("lam_in", small, [P, 4, DA_D])
    lam_pr = at("lam_pr", small + 1, [P, 2, DA_D])
    lam = at("lam", small + 1.5, [P, 4])
    gain = at("da_gain", small + 2, [P, 2 * DA_D])
    nmax, sums, inv, coef = (at(n, small + 3 + 0.25 * i, [P, 4, 2]) for i, n in enumerate(("nmax", "sums", "inv", "coef")))
    ssum, root, rinv, itmp = (at(f"oda_{i}", small + 4 + 0.25 * i, [P, NT, DA_H]) for i in range(4))
    junk = at("junk", small + 5, [P, 2 * DA_D])

    link, lam_loaded, lam_dot, lam_exp = sem("dve_link"), sem("lam_loaded"), sem("lam_dot"), sem("lam_exp")
    tr_ready, q_split, k_high, k_low, k_moved = sem("tr_ready"), sem("q_hi"), sem("k_hi"), sem("k_lo"), sem("k_moved")
    q_low = sem("q_lo")
    scored, maxed, exped, mixed = sem("scored"), sem("maxed"), sem("exped"), sem("mixed")
    turned_low, turned_high, low_read, high_read = sem("turned_low"), sem("turned_high"), sem("low_read"), sem("high_read")
    weighed, weigh_read, squared, scaled = sem("weighed"), sem("weigh_read"), sem("squared"), sem("scaled")
    sum_done, root_done = sem("sum_done"), sem("root_done")
    units = [(i, h) for i in range(NT) for h in range(DA_H)]
    n_units = len(units)
    highs = np.cumsum([0] + [int(i >= 4) for i, _ in units]).tolist()
    LOW, HIGH = v.bank[4], v.bank[5]

    def half_rows(a):
        return slice(a * DA_D, (a + 1) * DA_D)

    def prepares(p):
        i, h = units[p]
        return i + 1 if h == 1 and i + 1 < NT else None

    with nc.Block() as block:
        @block.sync
        def _(sp):
            sp.dma_start(lam_in[:, :, :], d["da_lambda"].rearrange("(o a) c -> o a c", o=1).broadcast_to([P, 4, DA_D])).then_inc(lam_loaded, 16)
            sp.dma_start(gain[:, :], d["da_out_norm"].broadcast_to([P, 2 * DA_D])).then_inc(lam_loaded, 16)

        def tile_of(x, t):
            return x[:, :, t * P:(t + 1) * P]

        def heads(bank, r):
            return bank[r, :].rearrange("p (h t) -> p h t", h=DA_H)

        @block.scalar
        def _(act):
            def prepare(t):
                act.wait_ge(tr_ready, 2 * t + 1)
                for a in range(2):
                    r = half_rows(a)
                    act.activation(tile_of(q_both[a][r], t), heads(LOW, r), ACT.Copy).then_inc(q_split, 1)
                act.wait_ge(tr_ready, 2 * t + 2)
                act.activation(tile_of(k_hi, t), heads(HIGH, slice(0, P)), ACT.Copy).then_inc(k_high, 1)
                for a in range(2):
                    act.activation(tile_of(k_both[a][half_rows(1 - a)], t), heads(HIGH, half_rows(a)), ACT.Copy).then_inc(k_moved, 1)

            def turn_out(p):
                act.wait_ge(turned_low, p + 1)
                if p >= 2:
                    act.wait_ge(weighed, p - 1)
                c = min((units[p][0] + 1) * P, N)
                act.activation(aT[:, p % 2, :c], LOW[:, :c], ACT.Copy).then_inc(low_read, 1)

            def out(p):
                i, h = units[p]
                act.wait_ge(weighed, p + 1)
                act.wait_ge(mixed, p + 1)
                if p:
                    act.wait_ge(squared, p)
                x, scale = v.bank[6 + p % 2][:, 0:P], inv[:, p % 4, 0:1]
                act.activation(junk[:, :], x, ACT.Square, scale=scale, accum_out=ssum[:, i, h:h + 1]).then_inc(squared, 1)
                act.activation(o[:, i, h * P:(h + 1) * P], x, ACT.Copy, scale=scale).then_inc(weigh_read, 1)

            prepare(0)
            act.wait_ge(lam_dot, 1)
            act.activation(lam[:, 0:2], lam[:, 0:2], ACT.Exp).then_inc(lam_exp, 1)
            for p, (i, h) in enumerate(units):
                nk = (i + 1) * P
                for a in range(2):
                    act.wait_ge(maxed, 2 * p + a + 1)
                    if p >= 2:
                        act.wait_ge(mixed, p - 1)
                    act.activation(probs[:, p % 2, a, :nk], v.pair[a][:, :nk], ACT.Exp, bias=nmax[:, p % 4, a:a + 1],
                                   accum_out=sums[:, p % 4, a:a + 1]).then_inc(exped, 1)
                if p >= 2:
                    turn_out(p - 2)
                if prepares(p):
                    prepare(prepares(p))
                if p >= 3:
                    out(p - 3)
            turn_out(n_units - 2)
            out(n_units - 3)
            turn_out(n_units - 1)
            out(n_units - 2)
            out(n_units - 1)
            act.wait_ge(sum_done, 1)
            act.activation(root[:, :, :], ssum[:, :, :], ACT.Sqrt).then_inc(root_done, 1)

        def weight_rows(pool, t):
            pool.wait_ge(weigh_read, DA_H * (t + 1))
            x = o[:, t, :].rearrange("p (h c) -> p h c", h=DA_H)
            pool.tensor_tensor(x, x, gain[:, :].unsqueeze(1).broadcast_to([P, DA_H, 2 * DA_D]), ALU.mult).then_inc(scaled, 1)

        @block.gpsimd
        def _(pool):
            pool.wait_ge(lam_dot, 1)
            for t in range(NT):
                weight_rows(pool, t)

        @block.vector
        def _(dve):
            done, then = chain(dve, link)

            def prepare(t):
                for a in range(2):
                    r, other = half_rows(a), half_rows(1 - a)
                    dve.wait_ge(q_split, 2 * t + a + 1)
                    dve.tensor_tensor(tile_of(q_both[a][other], t), heads(LOW, r), tile_of(q_both[a][r], t).bitcast(F32), ALU.subtract).then_inc(q_low, 1)
                dve.wait_ge(k_high, t + 1)
                dve.wait_ge(k_moved, 2 * t + 2)
                for a in range(2):
                    r = half_rows(a)
                    dve.tensor_tensor(tile_of(k_both[a][r], t), heads(HIGH, r), tile_of(k_hi[r], t).bitcast(F32), ALU.subtract).then_inc(k_low, 1)

            def mix(p):
                s, nk = p % 4, (units[p][0] + 1) * P
                dve.wait_ge(exped, 2 * p + 2)
                then(dve.reciprocal(inv[:, s, :], sums[:, s, :]))
                then(dve.scalar_tensor_tensor(out=coef[:, s, 0:1], in0=sums[:, s, 0:1], scalar=inv[:, s, 1:2], in1=lam[:, 3:4],
                                              op0=ALU.mult, op1=ALU.mult))
                if p >= 2:
                    dve.wait_ge(turned_low, p - 1)
                    if highs[p - 1]:
                        dve.wait_ge(turned_high, highs[p - 1])
                dve.scalar_tensor_tensor(out=a_[:, p % 2, :nk], in0=probs[:, p % 2, 1, :nk], scalar=coef[:, s, 0:1],
                                         in1=probs[:, p % 2, 0, :nk], op0=ALU.mult, op1=ALU.add).then_inc(mixed, 1)

            def turn_out(p):
                nk = (units[p][0] + 1) * P
                if nk > N:
                    dve.wait_ge(turned_high, highs[p + 1])
                    if p >= 2:
                        dve.wait_ge(weighed, p - 1)
                    dve.tensor_copy(aT[:, p % 2, N:nk], HIGH[:, :nk - N]).then_inc(high_read, 1)

            dve.wait_ge(lam_loaded, 32)
            pairs = lam_in[:, :, :].rearrange("p (a b) c -> p a b c", b=2)
            then(dve.tensor_tensor(lam_pr[:, :, :], pairs[:, :, 0, :], pairs[:, :, 1, :], ALU.mult))
            then(dve.tensor_scalar(gain[:, :], gain[:, :], 1.0 - LAM_INIT, None, ALU.mult))
            dve.tensor_reduce(lam[:, 0:2], lam_pr[:, :, :], AX.X, ALU.add).then_inc(lam_dot, 1)
            prepare(0)
            dve.wait_ge(lam_exp, 1)
            then(dve.tensor_tensor(lam[:, 2:3], lam[:, 1:2], lam[:, 0:1], ALU.subtract))
            then(dve.tensor_scalar(lam[:, 3:4], lam[:, 2:3], -LAM_INIT, None, ALU.add))
            for p, (i, h) in enumerate(units):
                nk = (i + 1) * P
                for a in range(2):
                    dve.wait_ge(scored, 2 * p + a + 1)
                    dve.tensor_reduce(nmax[:, p % 4, a:a + 1], v.pair[a][:, :nk], AX.X, ALU.max, negate=True).then_inc(maxed, 1)
                if p >= 1:
                    mix(p - 1)
                if p >= 2:
                    turn_out(p - 2)
                if prepares(p):
                    prepare(prepares(p))
            mix(n_units - 1)
            turn_out(n_units - 2)
            turn_out(n_units - 1)
            dve.wait_ge(squared, n_units)
            dve.tensor_scalar(ssum[:, :, :], ssum[:, :, :], 1.0 / (2 * DA_D), EPS, ALU.mult, ALU.add).then_inc(sum_done, 1)
            dve.wait_ge(root_done, 1)
            inverse_root(dve, then, rinv[:, :, :], ssum[:, :, :], root[:, :, :], itmp[:, :, :])
            dve.wait_ge(scaled, NT)
            x = o[:, :, :].rearrange("p t (h c) -> p (t h) c", c=2 * DA_D)
            then(dve.tensor_tensor(x, x, rinv[:, :, :].rearrange("p t h -> p (t h)").unsqueeze(2).broadcast_to([P, NT * DA_H, 2 * DA_D]), ALU.mult))

        @block.tensor
        def _(pe):
            def prepare(t):
                for bank, src in ((LOW, v.dq), (HIGH, v.dk)):
                    for h in range(DA_H):
                        mm = pe.transpose(bank[:, h * P:(h + 1) * P], src[:, t, h * P:(h + 1) * P], v.ident[:, :])
                    mm.then_inc(tr_ready, 1)

            def scores(p):
                i, h = units[p]
                if h == 0:
                    pe.wait_ge(q_low, 2 * i + 2)
                    pe.wait_ge(k_low, 2 * i + 2)
                    pe.wait_ge(k_moved, 2 * i + 2)
                t = slice(i * P, (i + 1) * P)
                for a in range(2):
                    if p:
                        pe.wait_ge(exped, 2 * (p - 1) + a + 1)
                    r = half_rows(a)
                    split_scores(pe, v, v.pair[a], q_both[a][r, h, t], k_hi[r, h, :], q_both[a][:, h, t], k_both[a][:, h, :],
                                 (i + 1) * P).then_inc(scored, 1)

            def free_banks(p):
                if p >= 0:
                    pe.wait_ge(low_read, p + 1)
                    if highs[p + 1]:
                        pe.wait_ge(high_read, highs[p + 1])

            def turn(p):
                pe.wait_ge(mixed, p + 1)
                free_banks(p - 1)
                i = units[p][0]
                for j in range(i + 1):
                    bank, c = (LOW, HIGH)[j // 4], slice(j % 4 * P, (j % 4 + 1) * P)
                    mm = pe.transpose(bank[:, c], a_[:, p % 2, j * P:(j + 1) * P], v.ident[:, :])
                    if j == min(i, 3):
                        mm.then_inc(turned_low, 1)
                if i >= 4:
                    mm.then_inc(turned_high, 1)

            def weigh(p):
                i, h = units[p]
                free_banks(p)
                if p >= 2:
                    pe.wait_ge(weigh_read, p - 1)
                for j in range(i + 1):
                    mm = pe.matmul(v.bank[6 + p % 2][:, 0:P], aT[:, p % 2, j * P:(j + 1) * P], v.dv[:, j, h * P:(h + 1) * P],
                                   start=(j == 0), stop=(j == i))
                mm.then_inc(weighed, 1)

            prepare(0)
            for p in range(n_units):
                scores(p)
                t = prepares(p - 1) if p else None
                if t:
                    pe.wait_ge(q_low, 2 * t + 2)
                    pe.wait_ge(k_low, 2 * t + 2)
                    pe.wait_ge(k_moved, 2 * t + 2)
                if p >= 2:
                    turn(p - 2)
                if prepares(p):
                    free_banks(p - 2)
                    prepare(prepares(p))
                if p >= 3:
                    weigh(p - 3)
            turn(n_units - 2)
            weigh(n_units - 3)
            turn(n_units - 1)
            weigh(n_units - 2)
            weigh(n_units - 1)


def turn_rows(v, chunk):
    nc, sem = v.nc, v.sem
    turned, hi_done, lo_done = sem("turned"), sem("hi_done"), sem("lo_done")

    def part(x, h, t):
        return x[:, 4 * h:4 * h + 4, t * P:(t + 1) * P]

    def bank(n):
        return v.bank[n % 8].rearrange("p (c t) -> p c t", c=4)

    def sync(sp):
        pass

    def scalar(act):
        for n in range(2 * NT):
            act.wait_ge(turned, n + 1)
            act.activation(part(v.act_hi, n % 2, n // 2), bank(n), ACT.Copy).then_inc(hi_done, 1)

    def vector(dve):
        for n in range(2 * NT):
            dve.wait_ge(hi_done, n + 1)
            dve.tensor_tensor(part(v.act_lo, n % 2, n // 2), bank(n), part(v.act_hi, n % 2, n // 2).bitcast(F32),
                              ALU.subtract).then_inc(lo_done, 1)

    def tensor(pe):
        for n in range(2 * NT):
            t, h = n // 2, n % 2
            if n >= 8:
                pe.wait_ge(lo_done, n - 7)
            for c in range(4):
                mm = pe.transpose(v.bank[n % 8][:, c * P:(c + 1) * P], chunk(t, 4 * h + c), v.ident[:, :])
            mm.then_inc(turned, 1)

    return Prelude(sync, scalar, vector, tensor, [(hi_done, 2 * NT), (lo_done, 2 * NT)])


def branch_stage(v):
    nc, at, sem, d = v.nc, v.mem.at, v.sem, v.d
    v.mix_hi, v.mix_lo = at("mix_hi", FREE, [P, ND, S], F32R), at("mix_lo", FREE + 32, [P, ND, S], F32R)
    hg = at("hg_part", FREE + 64, [P, 8, N])
    gate = at("gate", FREE + 80, [P, 8, N])
    m = at("m", FREE + 96, [P, 2, N])
    W = 2 * P
    act = (v.act_hi, v.act_lo)
    tiles = []
    for g in range(D // W):
        c0, c1 = g * W, (g + 1) * W
        tiles += group("tr", d["w_branch_hg"], HG_W // P, c0, c1, act, 0, 0)
        tiles += group("tr", d["w_branch_da"], DA_W // P, c0, c1, act, HG_W // P, 4)
    ready, free, link = sem("bank_ready"), sem("bank_free"), sem("dve_link")
    gate_in = [sem(f"gate_in{i}") for i in range(8)]
    m_done, hi_done = sem("m_done"), sem("mix_hi_done")
    used = []
    for g in range(D // W):
        used += [(g, side, u) for side in range(2) for u in range(4)]

    def load_gate(n):
        g, side, u = used[n]

        def run(sp):
            if n >= 8:
                sp.wait_ge(free, n - 7)
            sp.dma_start(gate[:, n % 8, :], d["gateT"][side, 2 * g + u % 2, :, u // 2 * N:u // 2 * N + N]).then_inc(gate_in[n % 8], 16)
        return run

    sp_steps = {n: [load_gate(n)] for n in range(len(used))}
    act_steps = {}

    def hi_part(g):
        def run(act_):
            for u in range(4):
                i = 4 * g + u
                act_.wait_ge(m_done, i + 1)
                act_.activation(v.mix_hi[:, 2 * g + u % 2, u // 2 * N:u // 2 * N + N], m[:, i % 2, :], ACT.Copy).then_inc(hi_done, 1)
        return run

    for g in range(D // W - 1):
        act_steps[8 * (g + 1) + 2] = [hi_part(g)]

    def dve_program(dve):
        done, then = chain(dve, link)
        for g in range(D // W):
            for side in range(2):
                for u in range(4):
                    n = 8 * g + 4 * side + u
                    dve.wait_ge(gate_in[n % 8], 16 * (n // 8 + 1))
                    dve.wait_ge(ready, n + 1)
                    if side == 0:
                        dve.tensor_tensor(hg[:, 4 * (g % 2) + u, :], v.bank[u], gate[:, n % 8, :], ALU.mult).then_inc(free, 1)
                        continue
                    i = 4 * g + u
                    if i >= 2:
                        dve.wait_ge(lo_done, i - 1)
                    dve.tensor_tensor(m[:, i % 2, :], v.bank[4 + u], gate[:, n % 8, :], ALU.mult).then_inc(free, 1)
                    dve.wait_ge(free, n + 1)
                    dve.tensor_tensor(m[:, i % 2, :], m[:, i % 2, :], hg[:, 4 * (g % 2) + u, :], ALU.add).then_inc(m_done, 1)
                    if i:
                        low(dve, i - 1)
        low(dve, 4 * (D // W) - 1)

    lo_done = sem("mix_lo_done")

    def low(dve, i):
        g, u = i // 4, i % 4
        dve.wait_ge(hi_done, i + 1)
        c, t = 2 * g + u % 2, slice(u // 2 * N, u // 2 * N + N)
        dve.tensor_tensor(v.mix_lo[:, c, t], m[:, i % 2, :], v.mix_hi[:, c, t].bitcast(F32), ALU.subtract).then_inc(lo_done, 1)

    def mixers(t, k):
        return (v.o_hg if k < 4 else v.o_da)[:, t, k % 4 * P:(k % 4 + 1) * P]

    dense_stage(v, tiles, dve_program, act_steps, act_after=hi_part(D // W - 1), sp_steps=sp_steps, sems=(ready, free),
                prelude=turn_rows(v, mixers))


def add_rows_stage(v, tiles, groups_of, load_from=None, prelude=None):
    nc, sem = v.nc, v.sem
    ready, free = sem("bank_ready"), sem("bank_free")
    x_in = sem("x_in")

    def load(sp):
        if load_from is not None:
            sp.dma_start(v.xres[:, :, :], load_from.rearrange("(t p) c -> p t c", p=P)).then_inc(x_in, 16)

    def dve_program(dve):
        if load_from is not None:
            dve.wait_ge(x_in, 16)
        for g, c0 in enumerate(groups_of):
            for t in range(NT):
                dve.wait_ge(ready, 8 * g + t + 1)
                x = v.xres[:, t, c0:c0 + N]
                dve.tensor_tensor(x, v.bank[t], x, ALU.add).then_inc(free, 1)

    dense_stage(v, tiles, dve_program, sp_steps={RING: [load]}, sems=(ready, free), prelude=prelude)


def output1_stage(v):
    act = (v.mix_hi, v.mix_lo)
    tiles = sum((group("nat", v.d["w_out"], ND, c, c + N, act) for c in (0, N)), [])
    add_rows_stage(v, tiles, (0, N), load_from=v.d["x"])


def router_stage(v):
    nc, at, sem, d = v.nc, v.mem.at, v.sem, v.d
    f = FREE
    gain_b, junk = at("gain_b", f, [P, D]), at("junk", f + 4, [P, D])
    XS = 4
    xs = at("xs", f + 60, [P, XS, D])
    xT = at("xT", f + 16, [P, 2, ND, P])
    wr = at("w_router", f + 24, [P, ND, NG + NE])
    bias = at("b_router", f + 25.5, [P, NG + NE])
    lg = at("logits", f + 26, [P, NT, NG + NE])
    upper, ones = at("upper", f + 28, [P, P]), at("ones", f + 28.5, [P, P])
    n_first = NG + NE8 + NSLOT_BLK + NT + NBLK // 2
    firsts = at("firsts", f + 29, [P, n_first])
    ss, ms, rt, rstd, tmp = (at(f"r{i}", f + 30 + 0.125 * i, [P, NT]) for i in range(5))
    A = [at(f"route{i}", f + 31 + i, [P, NT * NE]) for i in range(12)]
    B = [at(f"small{i}", f + 43 + 0.25 * i, [P, NT * NE8]) for i in range(12)]
    cmp_ = at("cmp", f + 48, [P, NSLOT_BLK * NE])
    before = at("before", f + 57, [P, NT + 1, NE])
    v.e_w = at("e_w", CONST + 2, [P, TOPK, NT])
    v.dest = at("dest", CONST + 2.25, [P, TOPK, NT], I32)
    v.blk_e = at("blk_e", CONST + 2.5, [1, NSLOT_BLK], I32)
    v.turns = at("turns", CONST + 2.75, [1, 8], I32)
    v.token_rows = at("token_rows", CONST + 2.875, [P, TOPK, NT, 2], I32)
    v.slots = at("slots", CONST + 3, [P, NSLOT_BLK, 2], I32)

    gain_in, const_in, slots_init = sem("gain_in"), sem("const_in"), sem("slots_init")
    sq_done, ms_done, rt_done, link = sem("sq_done"), sem("ms_done"), sem("rt_done"), sem("dve_link")
    xs_done, stored, turned, xT_done, logit, logit_read = (sem(n) for n in ("xs_done", "stored", "turned", "xT_done", "logit", "logit_read"))
    x_exp, exped, chosen, ranked, ones_set = sem("x_exp"), sem("exped"), sem("chosen"), sem("ranked"), sem("ones_set")
    store_n = [sem(f"store{i}") for i in range(XS)]
    groups = [range(0, 1)] + [range(t, min(t + 2, NT)) for t in range(1, NT, 2)]

    def first(a, n):
        return firsts[:, a:a + n]

    f_group, f_expert, f_block, f_tile, f_turn = (first(a, n) for a, n in zip(
        np.cumsum([0, NG, NE8, NSLOT_BLK, NT]).tolist(), (NG, NE8, NSLOT_BLK, NT, NBLK // 2)))

    with nc.Block() as block:
        @block.sync
        def _(sp):
            sp.dma_start(gain_b[:, :], d["norm_moe"].broadcast_to([P, D])).then_inc(gain_in, 16)
            sp.dma_start(wr[:, :, 0:NG], d["w_router_group"].rearrange("(k p) n -> p k n", p=P)).then_inc(const_in, 16)
            sp.dma_start(wr[:, :, NG:], d["w_router_expert"].rearrange("(k p) n -> p k n", p=P)).then_inc(const_in, 16)
            sp.dma_start(bias[:, 0:NG], d["b_router_group"].broadcast_to([P, NG])).then_inc(const_in, 16)
            sp.dma_start(bias[:, NG:], d["b_router_expert"].broadcast_to([P, NE])).then_inc(const_in, 16)
            sp.dma_start(upper[:, :], d["upper"]).then_inc(const_in, 16)
            sp.dma_start(firsts[:, :], d["firsts"].broadcast_to([P, n_first])).then_inc(const_in, 16)
            sp.dma_start(v.token_rows[:, :, :, :], d["token_rows"]).then_inc(const_in, 16)
            sp.dma_start(d["slot_table"], d["slot_init"]).then_inc(slots_init, 16)
            for t in range(NT):
                sp.wait_ge(xs_done, t + 1)
                sp.dma_start(d["xn"][t * P:(t + 1) * P, :], xs[:, t % XS, :]).then_inc(store_n[t % XS], 16)
            for i in range(XS):
                sp.wait_ge(store_n[i], 16 * NT // XS)
            sp.wait_ge(slots_init, 16)

        @block.scalar
        def _(act):
            def evacuate(t):
                for h in range(2):
                    act.wait_ge(turned, 2 * t + h + 1)
                    if t >= 2:
                        act.wait_ge(logit, t - 1)
                    act.activation(xT[:, t % 2, 4 * h:4 * h + 4, :], v.bank[(2 * t + h) % 4].rearrange("p (c t) -> p c t", c=4),
                                   ACT.Copy).then_inc(xT_done, 1)

            for g, tiles in enumerate(groups):
                for t in tiles:
                    if t:
                        act.wait_ge(sq_done, t)
                    act.activation(junk[:, :], v.xres[:, t, :], ACT.Square, accum_out=ss[:, t:t + 1]).then_inc(sq_done, 1)
                col = slice(tiles[0], tiles[-1] + 1)
                act.wait_ge(ms_done, g + 1)
                act.activation(rt[:, col], ms[:, col], ACT.Sqrt).then_inc(rt_done, 1)
                if g:
                    for t in groups[g - 1]:
                        evacuate(t)
            for t in groups[-1]:
                evacuate(t)
            act.wait_ge(x_exp, 1)
            act.activation(B[1][:, 0:NT * NG], B[0][:, 0:NT * NG], ACT.Exp).then_inc(exped, 1)
            act.wait_ge(x_exp, 2)
            act.activation(B[11][:, 0:NT], B[10][:, 0:NT], ACT.Exp).then_inc(exped, 1)

        @block.vector
        def _(dve):
            done, then = chain(dve, link)
            dve.memset(ones[:, :], 1.0).then_inc(ones_set, 1)
            done(dve.memset(before[:, 0, :], 0.0))
            dve.wait_ge(gain_in, 16)
            def add_bias(t):
                dve.wait_ge(logit, t + 1)
                dve.tensor_tensor(lg[:, t, :], v.bank[4 + t % 4][:, 0:NG + NE], bias[:, :], ALU.add).then_inc(logit_read, 1)

            for g, tiles in enumerate(groups):
                if g == 2:
                    dve.wait_ge(const_in, 112)
                col = slice(tiles[0], tiles[-1] + 1)
                dve.wait_ge(sq_done, tiles[-1] + 1)
                dve.tensor_scalar(ms[:, col], ss[:, col], 1.0 / D, EPS, ALU.mult, ALU.add).then_inc(ms_done, 1)
                dve.wait_ge(rt_done, g + 1)
                inverse_root(dve, then, rstd[:, col], ms[:, col], rt[:, col], tmp[:, col])
                for t in tiles:
                    if t >= XS:
                        dve.wait_ge(turned, 2 * (t - XS + 1))
                        dve.wait_ge(store_n[t % XS], 16 * (t // XS))
                    dve.scalar_tensor_tensor(out=xs[:, t % XS, :], in0=v.xres[:, t, :], scalar=rstd[:, t:t + 1], in1=gain_b[:, :],
                                             op0=ALU.mult, op1=ALU.mult).then_inc(xs_done, 1)
                if g >= 2:
                    for t in groups[g - 2]:
                        add_bias(t)
            for tiles in groups[-2:]:
                for t in tiles:
                    add_bias(t)
            dve.wait_ge(logit_read, NT)

            def grid(x, n):
                return x[:, 0:NT * n].rearrange("p (t n) -> p t n", n=n)

            def over(x, n):
                return x[:, 0:NT].unsqueeze(2).broadcast_to([P, NT, n])

            def row(x, n):
                return x.unsqueeze(1).broadcast_to([P, NT, n])

            def first_max(values, n, order, hot, top, t1, t2):
                then(dve.tensor_reduce(top, values, AX.X, ALU.max))
                then(dve.tensor_tensor(t1, values, top.unsqueeze(2).broadcast_to([P, NT, n]), ALU.is_equal))
                then(dve.tensor_tensor(t1, t1, row(order, n), ALU.mult))
                then(dve.tensor_reduce(t2, t1, AX.X, ALU.max))
                then(dve.tensor_tensor(hot, t1, t2.unsqueeze(2).broadcast_to([P, NT, n]), ALU.is_equal))

            G, E = lg[:, :, 0:NG], lg[:, :, NG:].rearrange("p t (g e) -> p t g e", g=NG)
            g_hot, g_top, g_w = grid(B[2], NG), B[3][:, 0:NT], B[4][:, 0:NT]
            first_max(G, NG, f_group, g_hot, g_top, grid(B[5], NG), B[6][:, 0:NT])
            dve.tensor_tensor(grid(B[0], NG), G, g_top.unsqueeze(2).broadcast_to([P, NT, NG]), ALU.subtract).then_inc(x_exp, 1)
            dve.wait_ge(exped, 1)
            then(dve.tensor_reduce(g_w, grid(B[1], NG), AX.X, ALU.add))
            then(dve.reciprocal(g_w, g_w))
            four = "p (t g e) -> p t g e"
            masked = A[0][:, :].rearrange(four, t=NT, g=NG)
            eg = grid(B[7], NE8)
            for t in range(NT):
                done(dve.tensor_tensor(masked[:, t], E[:, t], g_hot[:, t].unsqueeze(2).broadcast_to([P, NG, NE8]), ALU.mult))
            dve.wait_ge(link, done(dve.memset(tmp[:, :], 0.0)))
            then(dve.tensor_reduce(eg, masked.rearrange("p t g e -> p t e g"), AX.X, ALU.add))
            hot = [grid(B[8], NE8), grid(B[9], NE8)]
            first_max(eg, NE8, f_expert, hot[0], ss[:, :], grid(B[5], NE8), B[6][:, 0:NT])
            then(dve.scalar_tensor_tensor(out=eg, in0=hot[0], scalar=-3e38, in1=eg, op0=ALU.mult, op1=ALU.add))
            first_max(eg, NE8, f_expert, hot[1], ms[:, :], grid(B[5], NE8), B[6][:, 0:NT])
            dve.tensor_tensor(B[10][:, 0:NT], ms[:, :], ss[:, :], ALU.subtract).then_inc(x_exp, 1)
            dve.wait_ge(exped, 2)
            then(dve.tensor_scalar(rt[:, :], B[11][:, 0:NT], 1.0, None, ALU.add))
            then(dve.reciprocal(rt[:, :], rt[:, :]))
            then(dve.tensor_tensor(v.e_w[:, 0, :], rt[:, :], g_w, ALU.mult))
            then(dve.tensor_tensor(v.e_w[:, 1, :], v.e_w[:, 0, :], B[11][:, 0:NT], ALU.mult))
            pick = [A[1], A[2]]
            for k in range(TOPK):
                for t in range(NT):
                    done(dve.tensor_tensor(pick[k][:, :].rearrange(four, t=NT, g=NG)[:, t], hot[k][:, t].unsqueeze(1).broadcast_to([P, NG, NE8]),
                                           g_hot[:, t].unsqueeze(2).broadcast_to([P, NG, NE8]), ALU.mult))
            dve.wait_ge(link, done(dve.memset(tmp[:, :], 0.0)))
            dve.tensor_tensor(A[3][:, :], A[1][:, :], A[2][:, :], ALU.add).then_inc(chosen, 1)
            dve.wait_ge(chosen, 1)
            for t in range(NT):
                ins = dve.tensor_tensor(before[:, t + 1, :], before[:, t, :], A[3][:, t * NE:(t + 1) * NE], ALU.add)
                if t < NT - 1:
                    then(ins)
                else:
                    ins.then_inc(chosen, 1)
            dve.wait_ge(ranked, 1)
            count, blocks, upto = A[4][:, 0:NE], A[5][:, 0:NE], A[6][:, 0:NE]
            then(dve.tensor_copy(count, v.bank[1][:, 0:NE]))
            c3 = cmp_[:, 0:NE * NT].rearrange("p (e n) -> p e n", n=NT)
            then(dve.tensor_tensor(c3, count.unsqueeze(2).broadcast_to([P, NE, NT]), f_tile.unsqueeze(1).broadcast_to([P, NE, NT]), ALU.is_gt))
            then(dve.tensor_reduce(blocks, c3, AX.X, ALU.add))
            then(dve.tensor_tensor_scan(upto, ones[:, 0:NE], blocks, 0.0, ALU.mult, ALU.add))
            then(dve.tensor_tensor(blocks, upto, blocks, ALU.subtract))
            then(dve.tensor_scalar(blocks, blocks, float(P), None, ALU.mult))
            r3 = v.bank[0][:, 0:NT * NE].rearrange("p (t e) -> p t e", e=NE)
            dve.wait_ge(ranked, 2)
            s3 = A[10][:, :].rearrange("p (t e) -> p t e", e=NE)
            then(dve.tensor_tensor(s3, r3, blocks.unsqueeze(1).broadcast_to([P, NT, NE]), ALU.add))
            for k in range(TOPK):
                p3 = pick[k][:, :].rearrange("p (t e) -> p t e", e=NE)
                then(dve.tensor_tensor(p3, p3, s3, ALU.mult))
                then(dve.tensor_reduce(B[k][:, 0:NT], p3, AX.X, ALU.add))
                then(dve.tensor_copy(v.dest[:, k, :], B[k][:, 0:NT]))
            c3 = cmp_[0:1, :].rearrange("p (b e) -> p b e", e=NE)
            then(dve.tensor_tensor(c3, upto[0:1].unsqueeze(1).broadcast_to([1, NSLOT_BLK, NE]),
                                   f_block[0:1].unsqueeze(2).broadcast_to([1, NSLOT_BLK, NE]), ALU.is_le))
            then(dve.tensor_reduce(A[7][0:1, 0:NSLOT_BLK], c3, AX.X, ALU.add))
            then(dve.tensor_scalar(v.blk_e[:, :], A[7][0:1, 0:NSLOT_BLK], float(NE - 1), None, ALU.min))
            then(dve.tensor_scalar(A[8][0:1, 0:NBLK // 2], f_turn[0:1], upto[0:1, NE - 1:NE], None, ALU.is_lt))
            then(dve.tensor_reduce(A[9][0:1, 0:1], A[8][0:1, 0:NBLK // 2], AX.X, ALU.add))
            then(dve.tensor_copy(v.turns[:, 0:1], A[9][0:1, 0:1]))

        @block.tensor
        def _(pe):
            def turn(t):
                pe.wait_ge(xs_done, t + 1)
                for h in range(2):
                    n = 2 * t + h
                    if n >= 4:
                        pe.wait_ge(xT_done, n - 3)
                    for c in range(4):
                        k = 4 * h + c
                        mm = pe.transpose(v.bank[n % 4][:, c * P:(c + 1) * P], xs[:, t % XS, k * P:(k + 1) * P], v.ident[:, :])
                    mm.then_inc(turned, 1)

            pe.wait_ge(const_in, 112)
            turn(0)
            for t in range(NT):
                if t < NT - 1:
                    turn(t + 1)
                pe.wait_ge(xT_done, 2 * t + 2)
                if t >= 4:
                    pe.wait_ge(logit_read, t - 3)
                for k in range(ND):
                    mm = pe.matmul(v.bank[4 + t % 4][:, 0:NG + NE], xT[:, t % 2, k, :], wr[:, k, :], start=(k == 0), stop=(k == ND - 1))
                mm.then_inc(logit, 1)
            pe.wait_ge(ones_set, 1)
            pe.wait_ge(chosen, 1)
            pe.matmul(v.bank[0][:, 0:NT * NE], upper[:, :], A[3][:, :], start=True, stop=False)
            pe.wait_ge(chosen, 2)
            pe.matmul(v.bank[1][:, 0:NE], ones[:, :], before[:, NT, :], start=True, stop=True).then_inc(ranked, 1)
            pe.matmul(v.bank[0][:, 0:NT * NE], ones[:, :], before[:, 0:NT, :].rearrange("p t e -> p (t e)"), start=False, stop=True).then_inc(ranked, 1)


def experts_stage(v):
    nc, at, sem, d = v.nc, v.mem.at, v.sem, v.d
    TILES, SLOTS, COLS = 6, 4, 4 * N
    SHARE = 1280
    HALF = FF // 2
    raw = [at(f"w_raw{r}", ACTS + 8 * r, [P, COLS]) for r in range(TILES)]
    o = ACTS + 8 * TILES
    hi = [at(f"w_hi{s}", o + 8 * s, [P, COLS], F32R) for s in range(SLOTS)]
    lo = [at(f"w_lo{s}", o + 8 * (SLOTS + s), [P, COLS], F32R) for s in range(SLOTS)]
    o += 16 * SLOTS
    hid = at("hid", o, [P, 2, HALF])
    silu = at("silu", o + 2, [P, 2, HALF])
    hidT = [at(f"hidT{i}", o + 4 + 2 * i, [P, FF // P, P], F32R) for i in range(2)]
    y = [at(f"y{i}", o + 8 + 4 * i, [P, D]) for i in range(2)]
    xg = [at(f"xg{i}", RINGS + 4 * i, [P, D]) for i in range(2)]
    xT = [[at(f"xT{i}{j}", RINGS + 8 + 8 * i + 4 * j, [P, ND, P], F32R) for j in range(2)] for i in range(2)]
    warm = at("warm", CONST + 5.75, [P, 8])
    idx = [at(f"idx{i}", CONST + 6 + 0.125 * i, [P, 2], I32) for i in range(4)]
    b_x, b_h, b_hT, pair_y = v.bank[0:2], v.bank[2:4], v.bank[4:6], v.pair[3]

    landed = [sem(f"w_landed{r}") for r in range(TILES)]
    hi_done, lo_dve, lo_pool, w_used = sem("w_hi_done"), sem("w_lo_dve"), sem("w_lo_pool"), sem("w_used")
    x_in, y_out = [sem(f"x_in{i}") for i in range(2)], [sem(f"y_out{i}") for i in range(2)]
    idx_set, idx_seen, x_turned, x_hi, x_lo = (sem(n) for n in ("idx_set", "idx_seen", "x_turned", "x_hi", "x_lo"))
    silu_done, hid_done, h_turned, hidT_hi, hidT_lo, y_read = (sem(n) for n in ("silu_done", "hid_done", "h_turned", "hidT_hi", "hidT_lo", "y_read"))
    y_zero, y_seen = sem("y_zero"), sem("y_seen")
    scattered, listed = sem("scattered"), sem("listed")

    def turns(eng):
        return eng.value_load(v.turns[0:1, 0:1], min_val=1, max_val=NBLK // 2)

    def slot(p, r):
        return (TILES * p + r) % SLOTS

    def low(eng, r, p, done):
        s, c = slot(p, r), (slice(0, SHARE) if done is lo_dve else slice(SHARE, COLS))
        eng.tensor_tensor(lo[s][:, c], raw[r][:, c], hi[s][:, c].bitcast(F32), ALU.subtract).then_inc(done, 1)

    def wait_split(eng, n):
        eng.wait_ge(lo_dve, n + 3)
        eng.wait_ge(lo_pool, n + 3)

    with nc.Block() as block:
        @block.sync
        def _(sp):
            n_turns = turns(sp)

            def load(e, r):
                if r < 4:
                    src = d["w3" if r % 2 else "w1"][bass.ds(e, 1), :, r // 2 * HALF:(r // 2 + 1) * HALF]
                else:
                    src = d["w2"][bass.ds(e, 1), (r - 4) * HALF:(r - 3) * HALF, :]
                n = HALF if r < 4 else D
                sp.dma_start(raw[r][:, :].rearrange("p (k n) -> p k n", n=n), src.rearrange("o (k p) n -> p (o k) n", p=P)).then_inc(landed[r], 16)

            def expert(b):
                return sp.value_load(v.blk_e[0:1, b], min_val=0, max_val=NE - 1)

            e = expert(slice(0, 1))
            for r in range(4):
                load(e, r)
            sp.wait_ge(scattered, 16 * TOPK * NT)
            with nc.allow_non_contiguous_dma("slots of a block by partition"):
                sp.dma_start(v.slots[:, :, :], d["slot_table"].rearrange("(b p) o -> p b o", p=P)).then_inc(listed, 16)
            with sp.Fori(0, n_turns) as i:
                for p in range(2):
                    b = 2 * i + p
                    e = expert(bass.ds(b, 1))
                    for r in (4, 5):
                        wait_split(sp, TILES * b + r - TILES)
                        load(e, r)
                    e = expert(bass.ds(b + 1, 1))
                    for r in range(4):
                        wait_split(sp, TILES * b + r)
                        load(e, r)

        @block.gpsimd
        def _(pool):
            n_turns = turns(pool)

            def index(j, slots, count):
                pool.tensor_copy(idx[j][:, :], slots).then_inc(idx_set, 1)
                pool.wait_ge(idx_set, count)
                pool.sem_inc(idx_seen, 1)

            def gather(p):
                pool.indirect_dma_start(xg[p][:, :], None, d["xn"], bass.IndirectOffsetOnAxis(ap=idx[p][:, 0:1], axis=0)).then_inc(x_in[p], 16)

            def scatter(p):
                pool.indirect_dma_start(d["y"], bass.IndirectOffsetOnAxis(ap=idx[2 + p][:, 1:2], axis=0), y[p][:, :], None).then_inc(y_out[p], 16)

            for k in range(TOPK):
                for t in range(NT):
                    pool.indirect_dma_start(d["slot_table"], bass.IndirectOffsetOnAxis(ap=v.dest[:, k, t:t + 1], axis=0),
                                            v.token_rows[:, k, t, :], None).then_inc(scattered, 16)
            pool.wait_ge(listed, 16)
            index(0, v.slots[:, 0, :], 1)
            gather(0)
            for p in range(2):
                pool.memset(y[p][:, :], 0.0).then_inc(y_zero, 1)
                pool.wait_ge(y_zero, p + 1)
                index(2 + p, v.slots[:, NBLK + p, :], 2 + p)
                scatter(p)
            pool.sem_inc(lo_pool, 2)
            for r in range(4):
                pool.wait_ge(hi_done, r + 1)
                low(pool, r, 0, lo_pool)
            with pool.Fori(0, n_turns) as i:
                for p in range(2):
                    b = 2 * i + p
                    pool.wait_ge(x_turned, 2 * b + 2)
                    index(1 - p, v.slots[:, bass.ds(b + 1, 1), :].rearrange("p o c -> p (o c)"), 2 * b + 4)
                    gather(1 - p)
                    for m in range(4, 10):
                        pool.wait_ge(hi_done, TILES * b + m + 1)
                        low(pool, m % TILES, (p + m // TILES) % 2, lo_pool)
                    pool.wait_ge(y_read, b + 2)
                    pool.wait_ge(y_out[p], 16 * i + 16)
                    pool.sem_inc(y_seen, 1)
                    index(2 + p, v.slots[:, bass.ds(b, 1), :].rearrange("p o c -> p (o c)"), 2 * b + 5)
                    scatter(p)
            for p in range(2):
                pool.wait_ge(y_out[p], 16 * n_turns + 16)

        @block.scalar
        def _(act):
            n_turns = turns(act)

            def high(r, p):
                s = slot(p, r)
                act.activation(hi[s][:, :], raw[r][:, :], ACT.Copy).then_inc(hi_done, 1)

            def x_high(p, count):
                for c in range(2):
                    act.wait_ge(x_turned, count + c + 1)
                    act.activation(xT[p][0][:, 4 * c:4 * c + 4, :], b_x[c].rearrange("p (k t) -> p k t", t=P), ACT.Copy).then_inc(x_hi, 1)

            def gate(half, b):
                act.wait_ge(w_used, TILES * b + 2 * half + 2)
                act.wait_ge(hid_done, 2 * b + half + 1)
                act.activation(silu[:, half, :], b_h[half][:, 0:HALF], ACT.Silu).then_inc(silu_done, 1)

            def h_high(half, b):
                act.wait_ge(h_turned, 2 * b + half + 1)
                act.activation(hidT[0][:, 2 * half:2 * half + 2, :], b_hT[half][:, 0:HALF].rearrange("p (k t) -> p k t", t=P),
                               ACT.Copy).then_inc(hidT_hi, 1)

            for r in range(4):
                act.wait_ge(landed[r], 16)
                high(r, 0)
            x_high(0, 0)
            with act.Fori(0, n_turns) as i:
                act.activation(warm[:, :], v.e_w[:, 0, :], ACT.Silu)
                for p in range(2):
                    b = 2 * i + p

                    def split(r, q):
                        act.wait_ge(landed[r], 16 * b + 16 + 16 * q)
                        act.wait_ge(w_used, TILES * b + TILES * q + r - 3)
                        high(r, (p + q) % 2)

                    split(4, 0)
                    gate(0, b)
                    split(5, 0)
                    h_high(0, b)
                    split(0, 1)
                    gate(1, b)
                    split(1, 1)
                    h_high(1, b)
                    x_high(1 - p, 2 * b + 2)
                    split(2, 1)
                    split(3, 1)

        @block.vector
        def _(dve):
            n_turns = turns(dve)

            def x_low(p, count):
                for c in range(2):
                    dve.wait_ge(x_hi, count + c + 1)
                    dve.tensor_tensor(xT[p][1][:, 4 * c:4 * c + 4, :], b_x[c].rearrange("p (k t) -> p k t", t=P),
                                      xT[p][0][:, 4 * c:4 * c + 4, :].bitcast(F32), ALU.subtract).then_inc(x_lo, 1)

            def times(half, b):
                dve.wait_ge(silu_done, 2 * b + half + 1)
                dve.tensor_tensor(hid[:, half, :], silu[:, half, :], b_h[half][:, HALF:], ALU.mult).then_inc(hid_done, 1)

            def h_low(half, b):
                dve.wait_ge(hidT_hi, 2 * b + half + 1)
                dve.tensor_tensor(hidT[1][:, 2 * half:2 * half + 2, :], b_hT[half][:, 0:HALF].rearrange("p (k t) -> p k t", t=P),
                                  hidT[0][:, 2 * half:2 * half + 2, :].bitcast(F32), ALU.subtract).then_inc(hidT_lo, 1)

            dve.sem_inc(hid_done, 2)
            dve.sem_inc(hidT_lo, 2)
            dve.sem_inc(lo_dve, 2)
            dve.sem_inc(y_read, 1)
            for r in range(4):
                dve.wait_ge(hi_done, r + 1)
                low(dve, r, 0, lo_dve)
            x_low(0, 0)
            with dve.Fori(0, n_turns) as i:
                for p in range(2):
                    b = 2 * i + p

                    def split(r, q):
                        dve.wait_ge(hi_done, TILES * b + TILES * q + r + 1)
                        low(dve, r, (p + q) % 2, lo_dve)

                    split(4, 0)
                    times(0, b)
                    split(5, 0)
                    h_low(0, b)
                    split(0, 1)
                    times(1, b)
                    h_low(1, b)
                    split(1, 1)
                    x_low(1 - p, 2 * b + 2)
                    split(2, 1)
                    dve.wait_ge(w_used, TILES * b + TILES)
                    dve.wait_ge(y_out[p], 16 * i + 16)
                    dve.tensor_copy(y[p][:, :], pair_y[:, :]).then_inc(y_read, 1)
                    split(3, 1)

        @block.tensor
        def _(pe):
            n_turns = turns(pe)

            def three(out, left, right, first, last):
                pe.matmul(out, left[0], right[0], start=first, stop=False)
                pe.matmul(out, left[0], right[1], start=False, stop=False)
                return pe.matmul(out, left[1], right[0], start=False, stop=last)

            def turn_x(p):
                for c in range(2):
                    for k in range(4 * c, 4 * c + 4):
                        mm = pe.transpose(b_x[c][:, k % 4 * P:(k % 4 + 1) * P], xg[p][:, k * P:(k + 1) * P], v.ident[:, :])
                    mm.then_inc(x_turned, 1)

            def up(r, p, b):
                s = slot(p, r)
                wait_split(pe, TILES * b + r)
                for k in range(ND):
                    c = slice(k * HALF, (k + 1) * HALF)
                    mm = three(b_h[r // 2][:, r % 2 * HALF:(r % 2 + 1) * HALF], [x[:, k, :] for x in xT[p]], [w[s][:, c] for w in (hi, lo)],
                               k == 0, k == ND - 1)
                mm.then_inc(w_used, 1)

            def turn_h(half, b):
                pe.wait_ge(hid_done, 2 * b + half + 3)
                pe.wait_ge(hidT_lo, 2 * b + half + 1)
                for k in range(2):
                    mm = pe.transpose(b_hT[half][:, k * P:(k + 1) * P], hid[:, half, k * P:(k + 1) * P], v.ident[:, :])
                mm.then_inc(h_turned, 1)

            def down(r, p, b):
                s, half = slot(p, r), r - 4
                wait_split(pe, TILES * b + r)
                pe.wait_ge(hidT_lo, 2 * b + half + 3)
                for k in range(2):
                    for c in range(D // N):
                        cols = slice(k * D + c * N, k * D + (c + 1) * N)
                        mm = three(pair_y[:, c * N:(c + 1) * N], [h[:, 2 * half + k, :] for h in hidT], [w[s][:, cols] for w in (hi, lo)],
                                   half + k == 0, half + k == 2)
                mm.then_inc(w_used, 1)

            pe.wait_ge(x_in[0], 16)
            turn_x(0)
            with pe.Fori(0, n_turns) as i:
                for p in range(2):
                    b = 2 * i + p
                    pe.wait_ge(x_lo, 2 * b + 2)
                    pe.wait_ge(hid_done, 2 * b + 1)
                    up(0, p, b)
                    up(1, p, b)
                    pe.wait_ge(hid_done, 2 * b + 2)
                    up(2, p, b)
                    turn_h(0, b)
                    up(3, p, b)
                    pe.wait_ge(y_read, b + 1)
                    down(4, p, b)
                    turn_h(1, b)
                    pe.wait_ge(x_in[1 - p], 16 * i + 16 + 16 * p)
                    turn_x(1 - p)
                    down(5, p, b)


QA_W, KVA_W, B_W = AH * HD, 2 * AKV * HD, BH * HD
COL2 = dict(zip(("qa", "kva", "qb", "kb", "vb", "f"), np.cumsum([0, QA_W, KVA_W, B_W, B_W, B_W]).tolist()))
KVF_W = KVA_W + BH


def block2_tensors(v):
    at = v.mem.at
    v.qa = at("qa", FREE, [P, NT, QA_W])
    v.kvf = at("kvf", FREE + 16, [P, NT, KVF_W])
    v.vb = at("vb", FREE + 24.5, [P, NT, B_W])
    v.qb = at("qb_aug", FREE + 40.5, [P, NT, BH, BAUG])
    v.kb = at("kb_aug", FREE + 61.5, [P, NT, BH, BAUG])
    v.log_f = at("log_f", CONST + 7.5, [P, NT, BH])


def gate_column(x, c):
    return x[:, :, :, HD + c:HD + c + 1].rearrange("p t h o -> p t (h o)")


def project2_stage(v):
    nc, at, sem, d = v.nc, v.mem.at, v.sem, v.d
    block2_tensors(v)
    act_ops, w = (v.act_hi, v.act_lo), d["w_in_2"]
    order = ["kva", "qa", "qb", "kb", "vb"]
    index = {name: g for g, name in enumerate(order)}
    tiles = [Tile("nat", [(rows(w, k, COL2["kva"], COL2["kva"] + KVA_W), 0, KVA_W), (rows(w, k, COL2["f"], COL2["f"] + BH), KVA_W, KVF_W)],
                  KVF_W, act_ops, k, k == 0, k == ND - 1) for k in range(ND)]
    for name in order[1:]:
        tiles += group("nat", w, ND, COL2[name], COL2[name] + N, act_ops)

    gains = at("gains2", CONST + 3, [P, 4, HD])
    bias = at("b_forget", CONST + 7.75, [P, BH])
    z, e, u, dif, corr = (at(f"forget{i}", CONST + kb, [P, NT, BH]) for i, kb in enumerate((2.25, 2.5, 2.75, 7, 7.25)))

    def heads_of(name, dst, heads):
        return Heads(v, name, dst, heads, CONST + 4)

    plain = "p (h d) -> p h d"
    heads = {"kva": heads_of("ka", lambda t: v.kvf[:, t, 0:AKV * HD].rearrange(plain, d=HD), AKV),
             "qa": heads_of("qa", lambda t: v.qa[:, t, :].rearrange(plain, d=HD), AH),
             "qb": heads_of("qb", lambda t: v.qb[:, t, :, 0:HD], BH),
             "kb": heads_of("kb", lambda t: v.kb[:, t, :, 0:HD], BH)}
    ready, free, link, tables = sem("bank_ready"), sem("bank_free"), sem("dve_link"), sem("tables")
    saved = sem("xres_saved")
    e_arg, e_done, u_set, ln_done = sem("e_arg"), sem("e_done"), sem("u_set"), sem("ln_done")

    def load_tables(sp):
        for i, name in enumerate(("k_norm_a_2", "q_norm_a_2", "q_norm_b_2", "k_norm_b_2")):
            sp.dma_start(gains[:, i, :], d[name].broadcast_to([P, HD])).then_inc(tables, 16)
        sp.dma_start(bias[:, :], d["b_forget_2"].broadcast_to([P, BH])).then_inc(tables, 16)

    def save_xres(sp):
        sp.dma_start(d["xres"].rearrange("(t p) c -> p t c", p=P), v.xres[:, :, :]).then_inc(saved, 16)

    def forget_exp(act):
        act.wait_ge(e_arg, 1)
        act.activation(e[:, :, :], e[:, :, :], ACT.Exp).then_inc(e_done, 1)

    def forget_ln(act):
        act.wait_ge(u_set, 1)
        act.activation(z[:, :, :], u[:, :, :], ACT.Ln).then_inc(ln_done, 1)

    steps = {8 + 2: [forget_exp], 8 + 3: [forget_ln]}
    for name, h in heads.items():
        steps.setdefault(8 * (index[name] + 1) + (4 if name == "kva" else 6), []).append(h.root)

    def dve_program(dve):
        done, then = chain(dve, link)
        dve.wait_ge(tables, 80)
        for i in (1, 2):
            then(dve.tensor_scalar(gains[:, i, :], gains[:, i, :], HD ** -0.5, None, ALU.mult))
        g = index["kva"]
        for t in range(NT):
            dve.wait_ge(ready, 8 * g + t + 1)
            dve.tensor_copy(v.kvf[:, t, :], v.bank[t][:, 0:KVF_W]).then_inc(free, 1)
        dve.wait_ge(free, 8 * g + NT)
        then(dve.tensor_tensor(z[:, :, :], v.kvf[:, :, KVA_W:], bias[:, :].unsqueeze(1).broadcast_to([P, NT, BH]), ALU.add))
        dve.scalar_tensor_tensor(out=e[:, :, :], in0=z[:, :, :], scalar=-1.0, in1=z[:, :, :], op0=ALU.mult, op1=ALU.min).then_inc(e_arg, 1)
        then(dve.tensor_scalar(v.log_f[:, :, :], z[:, :, :], 0.0, None, ALU.min))
        dve.wait_ge(e_done, 1)
        dve.tensor_scalar(u[:, :, :], e[:, :, :], 1.0, None, ALU.add).then_inc(u_set, 1)
        dve.wait_ge(u_set, 1)
        then(dve.scalar_tensor_tensor(out=dif[:, :, :], in0=u[:, :, :], scalar=-1.0, in1=e[:, :, :], op0=ALU.add, op1=ALU.subtract))
        then(dve.reciprocal(corr[:, :, :], u[:, :, :]))
        then(dve.tensor_tensor(corr[:, :, :], dif[:, :, :], corr[:, :, :], ALU.mult))
        dve.wait_ge(ln_done, 1)
        then(dve.tensor_tensor(corr[:, :, :], corr[:, :, :], z[:, :, :], ALU.subtract))
        then(dve.tensor_tensor(v.log_f[:, :, :], v.log_f[:, :, :], corr[:, :, :], ALU.add))
        for i, name in enumerate(("kva", "qa", "qb", "kb")):
            h, g = heads[name], index[name]
            if name == "kb":
                dve.wait_ge(saved, 16)
            if name != "kva":
                for t in range(NT):
                    dve.wait_ge(ready, 8 * g + t + 1)
                    if name == "qa":
                        dve.tensor_copy(v.qa[:, t, :].rearrange("p (a g d) -> p g a d", g=AKV, d=HD),
                                        v.bank[t].rearrange("p (g a d) -> p g a d", g=AKV, d=HD)).then_inc(free, 1)
                    else:
                        h.take(dve, then, v.bank[t][:, :], t, free)
                dve.wait_ge(free, 8 * g + NT)
            for t in range(NT):
                h.stat(dve, then, t)
            h.mean(dve)
            h.inverse(dve, then)
            for t in range(NT):
                h.scale(dve, then, t, gains[:, i, :])
        then(dve.memset(v.kb[:, :, :, HD + 4:], 0.0))
        for x, c in ((v.qb, 0), (v.qb, 3), (v.kb, 1), (v.kb, 2)):
            done(dve.memset(gate_column(x, c), 1.0))
        for t in range(NT):
            done(dve.memset(v.kb[:, t, :, HD + 4:].rearrange("p h (a j) -> p h a j", a=2)[:, :, :, t:t + 1], 1.0))
        g = index["vb"]
        for t in range(NT):
            dve.wait_ge(ready, 8 * g + t + 1)
            dve.tensor_copy(v.vb[:, t, :], v.bank[t][:, :]).then_inc(free, 1)

    dense_stage(v, tiles, dve_program, steps, sp_before=load_tables, sp_steps={RING: [save_xres]}, sems=(ready, free),
                prelude=norm_rows(v, d["attn_norm_g_2"], experts=True))


class ForgetUnit:

    def __init__(self, h, i):
        self.h, self.i, self.window = h, i, False
        self.width, self.exps = (i + 1) * P, 1
        self.blocks = [(j * P, j, 0, j == 0, j == i) for j in range(i + 1)]


class WindowUnit:

    def __init__(self, g, i):
        self.g, self.i, self.window = g, i, True
        self.keys = min(2, i + 1) * P
        self.width, self.exps = self.keys * (AH // AKV), AH // AKV + 1
        first = max(0, i - 1)
        self.blocks = [(a * self.keys + (j - first) * P, j, a, j == first, j == i) for a in range(AH // AKV) for j in range(first, i + 1)]


def attention2_stage(v):
    nc, at, sem, d = v.nc, v.mem.at, v.sem, v.d
    k_hi, k_both = at("kb_hi", ACTS, [P, BH, S], F32R), at("kb_both", ACTS + 32, [P, BH, S], F32R)
    o = FREE + 82.5
    q_hi = [at(f"qb_hi{i}", o + 8 * i, [P, BH, P], F32R) for i in range(2)]
    q_both = [at(f"qb_both{i}", o + 8 * i + 4, [P, BH, P], F32R) for i in range(2)]
    qaT = [at(f"qaT{g}", o + 16 + 2 * g, [P, AH // AKV, P]) for g in range(AKV)]
    kaT = at("kaT", o + 20, [P, S])
    probs, aT = at("probs", RINGS, [P, 3, S]), at("probsT", RINGS + 12, [P, 2, S])
    alibi = [at("alibi0", o + 24, [P, AH // AKV, 2 * P]), at("alibi1", RINGS + 20, [P, AH // AKV, 2 * P])]
    v.out_a, v.out_b = v.qa, v.qb[:, :, :, :].rearrange("p t h c -> p t (h c)")
    small = CONST + 2
    upto, ones = at("upto", small, [P, P]), at("ones", small + 0.5, [P, P])
    sinks = at("sinks", small + 1, [P, AH])
    mraw, nmax, snk, sums, inv = (at(n, small + 1.25 + 0.125 * i, [P, 4, 4]) for i, n in enumerate(("mraw", "nmax", "snk", "sums", "inv")))
    c_hi = at("c_hi", small + 2, [P, NT, BH], F32R)
    c_lo = at("c_lo", small + 2.25, [P, NT, BH])
    R, R_hi = at("R", RINGS, [P, NT, BH, NT]), at("R_hi", RINGS + 2, [P, NT, BH, NT], F32R)

    HALF = AH // AKV
    units = []
    for i in range(NT):
        for g in range(AKV):
            units += [ForgetUnit(h, i) for h in range(4 * g, 4 * g + 4)] + [WindowUnit(g, i)]
    n_units, per_tile = len(units), len(units) // NT
    exped_upto = np.cumsum([0] + [u.exps for u in units]).tolist()
    halves = [-(-u.width // N) for u in units]
    high_upto = np.cumsum([0] + [n - 1 for n in halves]).tolist()
    LOW, HIGH = v.bank[4], v.bank[5]
    AHEAD = (7, 3, -1)
    AT_ONCE = 2
    STEPS, OF_ACT, OF_DVE = 3, (4, 4, AKV + 1), (2, 2, 0)

    consts, link, cum_ready, columns = sem("consts"), sem("dve_link"), sem("cum_ready"), sem("columns")
    alibi_in, tr_ready, prep_act, prep_dve = sem("alibi_in"), sem("tr_ready"), sem("prep_act"), sem("prep_dve")
    upto_set = sem("upto_set")
    scored, maxed, exped = sem("scored"), sem("maxed"), sem("exped")
    turned_low, turned_high, low_read, high_read = sem("turned_low"), sem("turned_high"), sem("low_read"), sem("high_read")
    weighed, weigh_read = sem("weighed"), sem("weigh_read")

    def prepares(p):
        for step, n in enumerate(AHEAD):
            t, rest = divmod(p + n, per_tile)
            if p >= 0 and rest == 0 and t < NT and (t or step >= AT_ONCE):
                return t, step

    def prepared(t, step):
        return sum(OF_ACT) * t + sum(OF_ACT[:step + 1]), sum(OF_DVE) * t + sum(OF_DVE[:step + 1])

    def blocks(bank, r):
        return bank[r, :].rearrange("p (a t) -> p a t", t=P)

    def tile(t):
        return slice(t * P, (t + 1) * P)

    TOP, BOTTOM = slice(0, HD), slice(HD, 2 * HD)

    with nc.Block() as block:
        @block.sync
        def _(sp):
            sp.dma_start(upto[:, :], d["upper"]).then_inc(consts, 16)
            sp.dma_start(sinks[:, :], d["sink_logits_2"].broadcast_to([P, AH])).then_inc(consts, 16)
            for g in range(AKV):
                sp.dma_start(alibi[g][:, :, :], d["alibi"][:, g * HALF:(g + 1) * HALF, :]).then_inc(alibi_in, 16)

        @block.scalar
        def _(act):
            def prepare(t, step):
                for b, bank in enumerate((LOW, HIGH)):
                    act.wait_ge(tr_ready, 2 * STEPS * t + 2 * step + b + 1)
                    heads = slice(4 * b, 4 * b + 4)
                    if step == 0:
                        moves = ((q_hi[t % 2][0:BAUG, heads, :], bank, slice(0, BAUG)), (q_both[t % 2][TOP, heads, :], bank, TOP))
                    elif step == 1:
                        moves = ((k_hi[0:BAUG, heads, tile(t)], bank, slice(0, BAUG)), (k_both[BOTTOM, heads, tile(t)], bank, TOP))
                    elif b == 0:
                        moves = tuple((qaT[g][r, :, :], bank, r) for g, r in enumerate((TOP, BOTTOM)))
                    else:
                        moves = ((kaT[:, tile(t)].rearrange("p (a t) -> p a t", t=P), bank[:, 0:P], slice(0, P)),)
                    for dst, src, r in moves:
                        act.activation(dst, blocks(src, r), ACT.Copy).then_inc(prep_act, 1)

            def turn_out(p):
                act.wait_ge(turned_low, p + 1)
                if p >= 2:
                    act.wait_ge(weighed, p - 1)
                c = min(units[p].width, N)
                act.activation(aT[:, p % 2, :c], LOW[:, :c], ACT.Copy).then_inc(low_read, 1)

            for step in range(AT_ONCE):
                prepare(0, step)
            for p, u in enumerate(units):
                if p >= 2:
                    turn_out(p - 2)
                act.wait_ge(maxed, p + 1)
                s, q = p % 4, probs[:, p % 3, :]
                if u.window:
                    for a in range(HALF):
                        c = slice(a * u.keys, (a + 1) * u.keys)
                        act.activation(q[:, c], q[:, c], ACT.Exp, bias=nmax[:, s, a:a + 1], accum_out=sums[:, s, a:a + 1]).then_inc(exped, 1)
                    act.activation(snk[:, s, :], snk[:, s, :], ACT.Exp).then_inc(exped, 1)
                else:
                    if p >= 3:
                        act.wait_ge(turned_low, p - 2)
                        if high_upto[p - 2]:
                            act.wait_ge(turned_high, high_upto[p - 2])
                    act.activation(q[:, :u.width], v.pair[p % 2][:, :u.width], ACT.Exp, bias=nmax[:, s, 0:1],
                                   accum_out=sums[:, s, 0:1]).then_inc(exped, 1)
                if prepares(p):
                    prepare(*prepares(p))
            for p in (n_units - 2, n_units - 1):
                turn_out(p)

        @block.vector
        def _(dve):
            done, then = chain(dve, link)

            def prepare(t, step):
                for b, bank in enumerate((LOW, HIGH)):
                    heads = slice(4 * b, 4 * b + 4)
                    if step < 2:
                        dve.wait_ge(prep_act, prepared(t, step)[0] - 2 + 2 * b)
                    if step == 0:
                        lo, hi = q_both[t % 2][BOTTOM, heads, :], q_both[t % 2][TOP, heads, :]
                    elif step == 1:
                        lo, hi = k_both[TOP, heads, tile(t)], k_hi[TOP, heads, tile(t)]
                    if step < 2:
                        dve.tensor_tensor(lo, blocks(bank, TOP), hi.bitcast(F32), ALU.subtract).then_inc(prep_dve, 1)

            def turn_out(p):
                if halves[p] < 2:
                    return
                dve.wait_ge(turned_high, high_upto[p + 1])
                if p >= 2:
                    dve.wait_ge(weighed, p - 1)
                c = units[p].width
                dve.tensor_copy(aT[:, p % 2, N:c], HIGH[:, :c - N]).then_inc(high_read, 1)

            def out(p):
                u, s = units[p], p % 4
                dve.wait_ge(weighed, p + 1)
                if u.window:
                    then(dve.tensor_tensor(inv[:, s, :], sums[:, s, :], snk[:, s, :], ALU.add))
                    then(dve.reciprocal(inv[:, s, :], inv[:, s, :]))
                    c = u.g * HALF * HD
                    dve.tensor_tensor(v.out_a[:, u.i, c:c + HALF * HD].rearrange("p (a d) -> p a d", d=HD),
                                      v.bank[6 + p % 2].rearrange("p (a g d) -> p a g d", g=AKV, d=HD)[:, :, u.g, :],
                                      inv[:, s, :].unsqueeze(2).broadcast_to([P, HALF, HD]), ALU.mult).then_inc(weigh_read, 1)
                else:
                    then(dve.reciprocal(inv[:, s, 0:1], sums[:, s, 0:1]))
                    dve.tensor_scalar(v.out_b[:, u.i, u.h * HD:(u.h + 1) * HD], v.bank[6 + p % 2][:, u.h % 2 * HD:(u.h % 2 + 1) * HD], inv[:, s, 0:1], None,
                                      ALU.mult).then_inc(weigh_read, 1)

            dve.wait_ge(consts, 32)
            done(dve.memset(ones[:, :], 1.0))
            dve.tensor_tensor(upto[:, :], upto[:, :], v.ident[:, :], ALU.add).then_inc(upto_set, 1)
            for g, r in enumerate((BOTTOM, TOP)):
                done(dve.memset(qaT[g][r, :, :], 0.0))
            then(dve.memset(R[:, :, :, :], 0.0))
            dve.wait_ge(cum_ready, 1)
            own = v.bank[7][:, 0:NT * BH].rearrange("p (t h) -> p t h", h=BH)
            total = v.bank[7][:, NT * BH:2 * NT * BH].rearrange("p (t h) -> p t h", h=BH)
            then(dve.tensor_copy(c_hi[:, :, :], own))
            hi = c_hi[:, :, :].bitcast(F32)
            then(dve.tensor_tensor(c_lo[:, :, :], own, hi, ALU.subtract))
            done(dve.tensor_copy(gate_column(v.qb, 1), hi))
            done(dve.tensor_copy(gate_column(v.qb, 2), c_lo[:, :, :]))
            done(dve.tensor_scalar(gate_column(v.kb, 0), hi, -1.0, None, ALU.mult))
            done(dve.tensor_scalar(gate_column(v.kb, 3), c_lo[:, :, :], -1.0, None, ALU.mult))
            for i in range(1, NT):
                then(dve.tensor_tensor(R[:, i, :, 0:i], R[:, i - 1, :, 0:i], total[:, i - 1, :].unsqueeze(2).broadcast_to([P, BH, i]), ALU.add))
            then(dve.tensor_copy(R_hi[:, :, :, :], R[:, :, :, :]))
            done(dve.tensor_copy(v.qb[:, :, :, HD + 4:HD + 4 + NT], R_hi[:, :, :, :].bitcast(F32)))
            dve.tensor_tensor(v.qb[:, :, :, HD + 4 + NT:], R[:, :, :, :], R_hi[:, :, :, :].bitcast(F32), ALU.subtract).then_inc(columns, 1)
            for step in range(AT_ONCE):
                prepare(0, step)
            dve.wait_ge(alibi_in, 32)
            dve.wait_ge(columns, 1)
            for p, u in enumerate(units):
                dve.wait_ge(scored, p + 1)
                s, q = p % 4, probs[:, p % 3, :]
                if u.window:
                    if p >= 3:
                        dve.wait_ge(turned_low, p - 2)
                        if high_upto[p - 2]:
                            dve.wait_ge(turned_high, high_upto[p - 2])
                    sink = sinks[:, u.g * HALF:(u.g + 1) * HALF]
                    for a in range(HALF):
                        c = slice(a * u.keys, (a + 1) * u.keys)
                        ins = dve.tensor_tensor_reduce(q[:, c], v.pair[p % 2][:, c], alibi[u.g][:, a, 2 * P - u.keys:], 1.0, -3.0e38,
                                                       ALU.add, ALU.max, mraw[:, s, a:a + 1])
                        (done if a < HALF - 1 else then)(ins)
                    then(dve.tensor_tensor(mraw[:, s, :], mraw[:, s, :], sink, ALU.max))
                    then(dve.tensor_scalar(nmax[:, s, :], mraw[:, s, :], -1.0, None, ALU.mult))
                    dve.tensor_tensor(snk[:, s, :], sink, nmax[:, s, :], ALU.add).then_inc(maxed, 1)
                else:
                    dve.tensor_reduce(nmax[:, s, 0:1], v.pair[p % 2][:, :u.width], AX.X, ALU.max, negate=True).then_inc(maxed, 1)
                if p >= 2:
                    turn_out(p - 2)
                if prepares(p):
                    prepare(*prepares(p))
                if p >= 3:
                    out(p - 3)
            turn_out(n_units - 2)
            out(n_units - 3)
            turn_out(n_units - 1)
            out(n_units - 2)
            out(n_units - 1)

        @block.tensor
        def _(pe):
            pe.wait_ge(upto_set, 1)
            logs = v.log_f[:, :, :].rearrange("p t h -> p (t h)")
            pe.matmul(v.bank[7][:, 0:NT * BH], upto[:, :], logs, start=True, stop=True)
            pe.matmul(v.bank[7][:, NT * BH:2 * NT * BH], ones[:, :], logs, start=True, stop=True).then_inc(cum_ready, 1)

            def prepare(t, step):
                for b, bank in enumerate((LOW, HIGH)):
                    if step < 2:
                        src, n = (v.qb, v.kb)[step], BAUG
                        parts = [src[:, t, 4 * b + a, :] for a in range(4)]
                    elif b == 0:
                        n, parts = P, [v.qa[:, t, a * P:(a + 1) * P] for a in range(HALF)]
                    else:
                        n, parts = P, [v.kvf[:, t, 0:P]]
                    for a, x in enumerate(parts):
                        mm = pe.transpose(bank[0:n, a * P:(a + 1) * P], x, v.ident[:, :])
                    mm.then_inc(tr_ready, 1)

            def wait_prepared(t, step):
                n_act, n_dve = prepared(t, step)
                pe.wait_ge(prep_act, n_act)
                pe.wait_ge(prep_dve, n_dve)

            def scores(p):
                u = units[p]
                if p % per_tile == 0:
                    wait_prepared(u.i, 1)
                if p % per_tile == 4:
                    wait_prepared(u.i, 2)
                if p >= 2 and units[p - 2].window:
                    pe.wait_ge(maxed, p - 1)
                elif p >= 2:
                    pe.wait_ge(exped, exped_upto[p - 1])
                pair, s = v.pair[p % 2], u.i % 2
                if u.window:
                    for a in range(HALF):
                        mm = pe.matmul(pair[:, a * u.keys:(a + 1) * u.keys], qaT[u.g][:, a, :], kaT[:, (u.i + 1) * P - u.keys:(u.i + 1) * P],
                                       start=True, stop=True)
                else:
                    mm = split_scores(pe, v, pair, q_hi[s][0:BAUG, u.h, :], k_hi[0:BAUG, u.h, :], q_both[s][:, u.h, :], k_both[:, u.h, :], u.width)
                mm.then_inc(scored, 1)

            def free_banks(p):
                if p >= 0:
                    pe.wait_ge(low_read, p + 1)
                    if high_upto[p + 1]:
                        pe.wait_ge(high_read, high_upto[p + 1])

            def turn(p):
                u = units[p]
                pe.wait_ge(exped, exped_upto[p + 1])
                free_banks(p - 1)
                for c in range(0, u.width, P):
                    bank = (LOW, HIGH)[c // N]
                    mm = pe.transpose(bank[:, c % N:c % N + P], probs[:, p % 3, c:c + P], v.ident[:, :])
                    if c + P == min(u.width, N):
                        mm.then_inc(turned_low, 1)
                if halves[p] > 1:
                    mm.then_inc(turned_high, 1)

            def weigh(p):
                u = units[p]
                free_banks(p)
                if p >= 2:
                    pe.wait_ge(weigh_read, p - 1)
                for c, j, a, first, last in u.blocks:
                    if u.window:
                        vals = v.kvf[:, j, AKV * HD:2 * AKV * HD]
                    else:
                        vals = v.vb[:, j, u.h // 2 * P:(u.h // 2 + 1) * P]
                    mm = pe.matmul(v.bank[6 + p % 2][:, a * P:(a + 1) * P], aT[:, p % 2, c:c + P], vals, start=first, stop=last)
                mm.then_inc(weighed, 1)

            pe.wait_ge(columns, 1)
            for step in range(AT_ONCE):
                prepare(0, step)
                wait_prepared(0, step)
            for p in range(n_units):
                scores(p)
                if prepares(p - 1):
                    wait_prepared(*prepares(p - 1))
                if p >= 2:
                    turn(p - 2)
                if prepares(p):
                    free_banks(p - 2)
                    prepare(*prepares(p))
                if p >= 3:
                    weigh(p - 3)
            turn(n_units - 2)
            weigh(n_units - 3)
            turn(n_units - 1)
            weigh(n_units - 2)
            weigh(n_units - 1)


def output2_stage(v):
    def mixers(t, k):
        return (v.out_a if k < 4 else v.out_b)[:, t, k % 4 * P:(k % 4 + 1) * P]

    act = (v.act_hi, v.act_lo)
    tiles = sum((group("nat", v.d["w_out_2"], ND, c, c + N, act) for c in (0, N)), [])
    add_rows_stage(v, tiles, (0, N), load_from=v.d["xres"], prelude=turn_rows(v, mixers))


def mlp_stage(v):
    nc, at, sem, d = v.nc, v.mem.at, v.sem, v.d
    hid = (at("hid_hi", FREE, [P, ND, S], F32R), at("hid_lo", FREE + 32, [P, ND, S], F32R))
    SLOTS = 7
    sq = at("hid", FREE + 64, [P, SLOTS, N])
    act_ops = (v.act_hi, v.act_lo)
    PARTS = DFF // D
    tiles = []
    for c in range(PARTS):
        for g in range(2):
            tiles += group("tr", d["w_up_2"], ND, c * D + g * N, c * D + (g + 1) * N, act_ops)
        for g in range(2):
            tiles += group("nat", d["w_down_2"][c * D:(c + 1) * D, :], ND, g * N, (g + 1) * N, hid)
    ready, free = sem("bank_ready"), sem("bank_free")
    squared, hi_done, lo_done, stored = sem("squared"), sem("hid_hi_done"), sem("hid_lo_done"), sem("stored")
    act_steps = {}

    def place(i):
        return i % 16 // 8 * 4 + i % 4, slice(i % 8 // 4 * N, i % 8 // 4 * N + N)

    def up_part(c, g):
        def run(act):
            def relu(u):
                i = 16 * c + 8 * g + u
                act.wait_ge(ready, 32 * c + 8 * g + u + 1)
                if i >= SLOTS:
                    act.wait_ge(lo_done, i - SLOTS + 1)
                act.activation(sq[:, i % SLOTS, :], v.bank[u][:, :], ACT.Relu).then_inc(free, 1)

            def high(u):
                i = 16 * c + 8 * g + u
                k, t = place(i)
                act.wait_ge(squared, i + 1)
                act.activation(hid[0][:, k, t], sq[:, i % SLOTS, :], ACT.Copy).then_inc(hi_done, 1)

            for u in range(8):
                relu(u)
                if u >= 4:
                    high(u - 4)
            for u in range(4, 8):
                high(u)
        return run

    for c in range(PARTS):
        for g in range(2):
            act_steps[32 * c + 8 * (g + 1) + 1] = [up_part(c, g)]
    for c in range(PARTS):
        for k in range(ND):
            tiles[32 * c + 16 + k].after = (lo_done, 16 * c + k // 4 * 8 + 4 + k % 4 + 1)

    def dve_program(dve):
        def low(i):
            k, t = place(i)
            dve.wait_ge(hi_done, i + 1)
            dve.tensor_tensor(hid[1][:, k, t], sq[:, i % SLOTS, :], hid[0][:, k, t].bitcast(F32), ALU.subtract).then_inc(lo_done, 1)

        for c in range(PARTS):
            for g in range(2):
                for u in range(8):
                    i = 16 * c + 8 * g + u
                    dve.wait_ge(free, 32 * c + 8 * g + u + 1)
                    x = sq[:, i % SLOTS, :]
                    dve.tensor_tensor(x, x, x, ALU.mult).then_inc(squared, 1)
                    if u >= 4:
                        low(i - 4)
                for u in range(4, 8):
                    low(16 * c + 8 * g + u)
            for g in range(2):
                for t in range(NT):
                    dve.wait_ge(ready, 32 * c + 16 + 8 * g + t + 1)
                    x = v.xres[:, t, g * N:(g + 1) * N]
                    dve.tensor_tensor(x, v.bank[t], x, ALU.add).then_inc(free, 1)

    def store(act):
        for g in range(2):
            for t in range(NT):
                act.wait_ge(free, 32 * (PARTS - 1) + 16 + 8 * g + t + 1)
                act.dma_start(d["out"][t * P:(t + 1) * P, g * N:(g + 1) * N], v.xres[:, t, g * N:(g + 1) * N]).then_inc(stored, 16)
        act.wait_ge(stored, 16 * 2 * NT)

    dense_stage(v, tiles, dve_program, act_steps, act_after=store, sems=(ready, free),
                prelude=norm_rows(v, d["mlp_norm_g_2"]))


def constants_stage(v):
    nc, d = v.nc, v.d
    loaded, made = v.sem("constants"), v.sem("constants_bf")
    with nc.Block() as block:
        @block.sync
        def _(sp):
            sp.dma_start(v.ident[:, :], d["ident"]).then_inc(loaded, 16)
            sp.dma_start(v.mask_f[:, :], d["mask"]).then_inc(loaded, 16)

        @block.vector
        def _(dve):
            dve.wait_ge(loaded, 32)
            dve.tensor_copy(v.ident_bf[:, :], v.ident[:, :]).then_inc(made, 1)
            dve.tensor_copy(v.mask_bf[:, :], v.mask_f[:, :]).then_inc(made, 1)


def program(nc, dram, out, until=99, dump=None):
    with ExitStack() as ctx:
        d = dict(dram)
        for name, shape, dt in (("gateT", (2, ND, P, S), F32), ("hog", (S, HG_W), F32), ("xn", (S, D), F32),
                                ("slot_table", (NSLOT_BLK * P, 2), I32), ("y", ((TOPK + 1) * S, D), F32), ("xres", (S, D), F32)):
            d[name] = nc.dram_tensor(f"scratch_{name}", shape, dt).ap()
        d["out"] = out
        v = Env(nc, ctx, d)
        constants_stage(v)
        block1_tensors(v)
        stages = [project1_stage, hgrn_stage] + MORE
        for n, stage in enumerate(stages):
            if n < until:
                stage(v)
                if len(v.sems) > 80:
                    v.recycle_sems()
        if dump:
            dump(v)


MORE = [diff_attention_stage, branch_stage, output1_stage, router_stage, experts_stage,
        project2_stage, attention2_stage, output2_stage, mlp_stage]


def constants():
    i = np.arange(P)
    half = DA_D // 2
    inv = (10000.0 ** (-np.arange(half) / half)).astype(np.float32)
    ang = (np.arange(S, dtype=np.float32)[:, None] * inv[None, :]).astype(np.float64)
    keep = np.ones((1, S), np.float32)
    keep[0, ::CHUNK] = 0.0
    slopes = np.exp2(-(8.0 / AH) * (np.arange(AH, dtype=np.float32) + 1.0)).astype(np.float32)
    dist = (P + i)[:, None] - np.arange(2 * P)[None, :]
    band = (dist >= 0) & (dist < P)
    alibi = np.where(band[None], -slopes[:, None, None] * dist[None].astype(np.float32), np.float32(NEG))
    token = np.arange(NT)[None, :] * P + i[:, None]
    slot = np.arange(NSLOT_BLK * P)
    return {
        "ident": np.eye(P, dtype=np.float32),
        "upper": (i[:, None] < i[None, :]).astype(np.float32),
        "rope_cos": np.cos(ang).astype(np.float32), "rope_sin": np.sin(ang).astype(np.float32),
        "chunk_keep": keep,
        "causal_st": ((i % CHUNK)[:, None] <= np.arange(CHUNK)[None, :]).astype(np.int32),
        "mask": np.where(i[None, :] <= i[:, None], 0.0, NEG).astype(np.float32),
        "alibi": np.ascontiguousarray(alibi.transpose(1, 0, 2)).astype(np.float32),
        "token_rows": np.ascontiguousarray(np.stack(np.broadcast_arrays(token[:, None, :], token[:, None, :] + S * np.arange(TOPK)[None, :, None]),
                                                    axis=-1)).astype(np.int32),
        "slot_init": np.stack([0 * slot, TOPK * S + slot % (2 * P)], axis=-1).astype(np.int32),
        "firsts": np.concatenate([np.arange(NG, 0, -1), np.arange(NE8, 0, -1), np.arange(0, NSLOT_BLK),
                                  np.arange(NT) * P, 2 * np.arange(NBLK // 2)]).astype(np.float32)[None, :],
    }


_ROWS = ("norm_mix", "hg_out_norm", "da_q_norm", "da_k_norm", "da_out_norm", "norm_moe", "b_router_group", "b_router_expert",
         "attn_norm_g_2", "b_forget_2", "q_norm_a_2", "k_norm_a_2", "sink_logits_2", "q_norm_b_2", "k_norm_b_2", "mlp_norm_g_2")


def layout(inputs):
    out = {}
    for name, a in inputs.items():
        a = np.asarray(a)
        if name in _ROWS:
            a = a.reshape(1, -1)
        elif name not in ("hg_lb",) and a.shape[0] == 1:
            a = a.reshape(a.shape[1:])
        out[name] = np.ascontiguousarray(a)
    out.update(constants())
    return out


def kernel(**inputs):
    from concourse import bacc
    from concourse.bass_utils import run_bass_kernel_spmd

    arrays = layout(inputs)
    nc = bacc.Bacc("TRN2", target_bir_lowering=False, num_devices=1)
    dram = {name: nc.dram_tensor(f"in_{name}", a.shape, mybir.dt.from_np(a.dtype), kind="ExternalInput").ap()
            for name, a in arrays.items()}
    out = nc.dram_tensor("out", (S, D), F32, kind="ExternalOutput").ap()
    program(nc, dram, out)
    got = run_bass_kernel_spmd(nc, [{f"in_{name}": a for name, a in arrays.items()}], core_ids=[0])
    return got.results[0]["out"].reshape(1, S, D)
```
